# Optimizing a Trainium2 kernel written in Bass

```python
import jax, jax.numpy as jnp
from jax import lax
import numpy as np

D_MODEL = 1024
BATCH = 1
SEQ = 256
DEPTH = 2

N_A_LAYERS = DEPTH // 2
N_B_LAYERS = DEPTH - N_A_LAYERS
RMS_EPS = 1e-6
RWKV_HEAD = 64
RWKV_HEADS = D_MODEL // RWKV_HEAD
LORA_DECAY = 64
LORA_AAA = 64
LORA_MV = 32
LORA_GATE = 160
LNX_EPS = 64e-5
ATT_HEAD = 64
HEADS_PER_GROUP = D_MODEL // ATT_HEAD
DILATED_GROUPS = ((128, 1), (512, 4), (2048, 16))
N_GROUPS = len(DILATED_GROUPS)
BLOCK = 128
ROPE_THETA = 10000.0
Q_WIDTH = N_GROUPS * HEADS_PER_GROUP * ATT_HEAD
O_WIDTH = HEADS_PER_GROUP * ATT_HEAD
D_FF = -(-8 * D_MODEL // (3 * 256)) * 256

kernel_name = "yoco_rwkv7_dilated_window_hybrid"

def rms_norm(x, g):
    x32 = x.astype(jnp.float32)
    y = x32 * lax.rsqrt(jnp.mean(x32 * x32, axis=-1, keepdims=True) + RMS_EPS)
    return (y * g.astype(jnp.float32)).astype(x.dtype)

def rope_tables(seq):
    inv = ROPE_THETA ** (-jnp.arange(0, ATT_HEAD, 2, dtype=jnp.float32) / ATT_HEAD)
    ang = jnp.arange(seq, dtype=jnp.float32)[:, None] * inv[None, :]
    return jnp.cos(ang), jnp.sin(ang)

def apply_rope(t, cos, sin):
    c = cos[None, :, None, None, :]
    s = sin[None, :, None, None, :]
    t32 = t.astype(jnp.float32)
    t1, t2 = jnp.split(t32, 2, axis=-1)
    return jnp.concatenate([t1 * c - t2 * s, t2 * c + t1 * s], axis=-1).astype(t.dtype)

def swiglu_ffn(x, norm_g, w_gu, w_down):
    h = rms_norm(x, norm_g)
    gate, up = jnp.split(h @ w_gu, 2, axis=-1)
    return (jax.nn.silu(gate) * up) @ w_down

def wkv7_scan(r, w, k, v, a, b):
    Bn, Sn, Hn, Nn = r.shape

    def step(state, inp):
        r_t, w_t, k_t, v_t, a_t, b_t = inp
        sa = jnp.einsum('bhij,bhj->bhi', state, a_t)
        state = (state * w_t[:, :, None, :] + sa[..., None] * b_t[:, :, None, :]
                 + v_t[..., None] * k_t[:, :, None, :])
        return state, jnp.einsum('bhij,bhj->bhi', state, r_t)

    xs = tuple(jnp.moveaxis(t, 1, 0) for t in (r, w, k, v, a, b))
    state0 = jnp.zeros((Bn, Hn, Nn, Nn), jnp.float32)
    _, out = lax.scan(step, state0, xs)
    return jnp.moveaxis(out, 0, 1)

def rwkv7_time_mix(x, v_first, norm_g, mu, w_r, w_k, w_v, w0, w1, w2, a0, a1, a2,
                   g1, g2, k_k, k_a, r_k, lnx_g, lnx_b, w_o, v_mix):
    Bn, Sn, Dn = x.shape
    f32 = jnp.float32
    h = rms_norm(x, norm_g)
    dx = jnp.pad(h, ((0, 0), (1, 0), (0, 0)))[:, :-1] - h
    xr, xw, xk, xv, xa, xg = (h + dx * mu[i] for i in range(6))
    r = xr @ w_r
    w = -jax.nn.softplus(-(w0 + jnp.tanh(xw @ w1) @ w2)) - 0.5
    k = xk @ w_k
    v = xv @ w_v
    if v_mix is None:
        v_first = v
    else:
        v0, v1, v2 = v_mix
        v = v + (v_first - v) * jax.nn.sigmoid(v0 + (xv @ v1) @ v2)
    a = jax.nn.sigmoid(a0 + (xa @ a1) @ a2)
    g = jax.nn.sigmoid(xg @ g1) @ g2
    heads = lambda t: t.astype(f32).reshape(Bn, Sn, RWKV_HEADS, RWKV_HEAD)
    kk = heads(k * k_k)
    kk = kk / jnp.maximum(jnp.sqrt(jnp.sum(kk * kk, axis=-1, keepdims=True)), 1e-12)
    k = k * (1.0 + (a - 1.0) * k_a)
    rh, kh, vh, ah = heads(r), heads(k), heads(v), heads(a)
    decay = jnp.exp(-jnp.exp(heads(w)))
    o = wkv7_scan(rh, decay, kh, vh, -kk, kk * ah)
    mean = jnp.mean(o, axis=-1, keepdims=True)
    var = jnp.mean(jnp.square(o - mean), axis=-1, keepdims=True)
    o = (o - mean) * lax.rsqrt(var + LNX_EPS)
    o = o.reshape(Bn, Sn, Dn) * lnx_g.astype(f32) + lnx_b.astype(f32)
    bonus = jnp.sum(rh * kh * r_k.astype(f32), axis=-1, keepdims=True) * vh
    y = (o + bonus.reshape(Bn, Sn, Dn)) * g.astype(f32)
    return y.astype(x.dtype) @ w_o, v_first

def dilated_window_attention(q, k, v, window, dilation):
    Bn, Sn, Hn, Dh = q.shape
    span = window // dilation
    L = Sn // dilation
    nblk = -(-L // BLOCK)
    Lp = nblk * BLOCK

    def to_blocks(t):
        t = t.reshape(Bn, L, dilation, Hn, Dh).transpose(0, 2, 1, 3, 4)
        t = jnp.pad(t, ((0, 0), (0, 0), (0, Lp - L), (0, 0), (0, 0)))
        return t.reshape(Bn, dilation, nblk, BLOCK, Hn, Dh)

    def with_prev(t):
        prev = jnp.pad(t, ((0, 0), (0, 0), (1, 0), (0, 0), (0, 0), (0, 0)))[:, :, :-1]
        return jnp.concatenate([prev, t], axis=3)

    qb = to_blocks(q)
    kc = with_prev(to_blocks(k))
    vc = with_prev(to_blocks(v))
    s = jnp.einsum('brnqhd,brnkhd->brnhqk', qb, kc,
                   preferred_element_type=jnp.float32) * (Dh ** -0.5)
    qi = jnp.arange(BLOCK)[:, None]
    kj = jnp.arange(2 * BLOCK)[None, :]
    dist = qi + BLOCK - kj
    nb = jnp.arange(nblk)[:, None, None]
    valid = (dist >= 0) & (dist <= span) & ((nb > 0) | (kj >= BLOCK))
    s = jnp.where(valid[None, None, :, None, :, :], s, -jnp.inf)
    m = jnp.max(s, axis=-1, keepdims=True)
    p = jnp.exp(s - m)
    den = jnp.sum(p, axis=-1, keepdims=True)
    o = jnp.einsum('brnhqk,brnkhd->brnqhd', p, vc.astype(jnp.float32))
    o = o / jnp.swapaxes(den, 3, 4)
    lse = jnp.swapaxes((m + jnp.log(den))[..., 0], 3, 4)
    o = o.reshape(Bn, dilation, Lp, Hn, Dh)[:, :, :L].transpose(0, 2, 1, 3, 4).reshape(Bn, Sn, Hn, Dh)
    lse = lse.reshape(Bn, dilation, Lp, Hn)[:, :, :L].transpose(0, 2, 1, 3).reshape(Bn, Sn, Hn)
    return o, lse

def shared_kv(x, kv_norm_g, w_kv, k_norm_g, cos, sin):
    Bn, Sn, _ = x.shape
    h = rms_norm(x, kv_norm_g)
    kv = (h @ w_kv).reshape(Bn, Sn, 2, N_GROUPS, HEADS_PER_GROUP, ATT_HEAD)
    k = apply_rope(rms_norm(kv[:, :, 0], k_norm_g[:, None, :]), cos, sin)
    return k, kv[:, :, 1]

def dilated_mixer(x, k_sh, v_sh, cos, sin, norm_g, w_q, q_norm_g, w_o):
    Bn, Sn, _ = x.shape
    h = rms_norm(x, norm_g)
    q = (h @ w_q).reshape(Bn, Sn, N_GROUPS, HEADS_PER_GROUP, ATT_HEAD)
    q = apply_rope(rms_norm(q, q_norm_g[:, None, :]), cos, sin)
    outs, lses = [], []
    for gi, (window, dilation) in enumerate(DILATED_GROUPS):
        o, l = dilated_window_attention(q[:, :, gi], k_sh[:, :, gi], v_sh[:, :, gi], window, dilation)
        outs.append(o)
        lses.append(l)
    alpha = jax.nn.softmax(jnp.stack(lses), axis=0)
    o = jnp.einsum('gbsh,gbshd->bshd', alpha, jnp.stack(outs))
    return o.reshape(Bn, Sn, O_WIDTH).astype(x.dtype) @ w_o

def setup_inputs(seed: int = 0) -> dict:
    key = jax.random.key(seed)
    ks = iter(jax.random.split(key, 64))
    D, NA, NB = D_MODEL, N_A_LAYERS, N_B_LAYERS
    nrm = lambda shape, scale: jax.random.normal(next(ks), shape, jnp.float32) * scale
    gain = lambda shape: 1.0 + nrm(shape, 0.02)
    return {
        "x": nrm((BATCH, SEQ, D), 1.0),
        "a_norm_g": gain((NA, D)),
        "a_mu": jax.random.uniform(next(ks), (NA, 6, D), jnp.float32),
        "a_w_r": nrm((NA, D, D), D ** -0.5),
        "a_w_k": nrm((NA, D, D), D ** -0.5),
        "a_w_v": nrm((NA, D, D), D ** -0.5),
        "a_w0": jax.random.uniform(next(ks), (NA, D), jnp.float32, -6.5, -1.5),
        "a_w1": nrm((NA, D, LORA_DECAY), D ** -0.5),
        "a_w2": nrm((NA, LORA_DECAY, D), 0.1 * LORA_DECAY ** -0.5),
        "a_a0": nrm((NA, D), 0.1),
        "a_a1": nrm((NA, D, LORA_AAA), D ** -0.5),
        "a_a2": nrm((NA, LORA_AAA, D), 0.5 * LORA_AAA ** -0.5),
        "a_v0": nrm((NA - 1, D), 0.1),
        "a_v1": nrm((NA - 1, D, LORA_MV), D ** -0.5),
        "a_v2": nrm((NA - 1, LORA_MV, D), 0.5 * LORA_MV ** -0.5),
        "a_g1": nrm((NA, D, LORA_GATE), D ** -0.5),
        "a_g2": nrm((NA, LORA_GATE, D), LORA_GATE ** -0.5),
        "a_k_k": 0.85 + nrm((NA, D), 0.05),
        "a_k_a": 1.0 + nrm((NA, D), 0.05),
        "a_r_k": -0.04 + nrm((NA, RWKV_HEADS, RWKV_HEAD), 0.02),
        "a_lnx_g": gain((NA, D)),
        "a_lnx_b": nrm((NA, D), 0.01),
        "a_w_o": nrm((NA, D, D), D ** -0.5),
        "kv_norm_g": gain((D,)),
        "w_kv": nrm((D, 2 * Q_WIDTH), D ** -0.5),
        "k_norm_g": gain((N_GROUPS, ATT_HEAD)),
        "b_norm_g": gain((NB, D)),
        "b_w_q": nrm((NB, D, Q_WIDTH), D ** -0.5),
        "b_q_norm_g": gain((NB, N_GROUPS, ATT_HEAD)),
        "b_w_o": nrm((NB, O_WIDTH, D), O_WIDTH ** -0.5),
        "f_norm_g": gain((DEPTH, D)),
        "f_w_gu": nrm((DEPTH, D, 2 * D_FF), D ** -0.5),
        "f_w_down": nrm((DEPTH, D_FF, D), D_FF ** -0.5),
    }

def reference(x, a_norm_g, a_mu, a_w_r, a_w_k, a_w_v, a_w0, a_w1, a_w2, a_a0, a_a1, a_a2,
              a_v0, a_v1, a_v2, a_g1, a_g2, a_k_k, a_k_a, a_r_k, a_lnx_g, a_lnx_b, a_w_o,
              kv_norm_g, w_kv, k_norm_g, b_norm_g, b_w_q, b_q_norm_g, b_w_o,
              f_norm_g, f_w_gu, f_w_down):
    cos, sin = rope_tables(x.shape[1])
    v_first = None
    k_sh = v_sh = None
    for layer in range(DEPTH):
        if layer < N_A_LAYERS:
            i = layer
            v_mix = None if i == 0 else (a_v0[i - 1], a_v1[i - 1], a_v2[i - 1])
            y, v_first = rwkv7_time_mix(
                x, v_first, a_norm_g[i], a_mu[i], a_w_r[i], a_w_k[i], a_w_v[i],
                a_w0[i], a_w1[i], a_w2[i], a_a0[i], a_a1[i], a_a2[i], a_g1[i], a_g2[i],
                a_k_k[i], a_k_a[i], a_r_k[i], a_lnx_g[i], a_lnx_b[i], a_w_o[i], v_mix)
            x = x + y
        else:
            j = layer - N_A_LAYERS
            x = x + dilated_mixer(x, k_sh, v_sh, cos, sin, b_norm_g[j], b_w_q[j],
                                  b_q_norm_g[j], b_w_o[j])
        x = x + swiglu_ffn(x, f_norm_g[layer], f_w_gu[layer], f_w_down[layer])
        if layer == N_A_LAYERS - 1:
            k_sh, v_sh = shared_kv(x, kv_norm_g, w_kv, k_norm_g, cos, sin)
    return x


_drawn_inputs = setup_inputs


def setup_inputs(seed=0):
    import zlib

    import numpy as np

    out = dict(_drawn_inputs(seed))
    spreads = {}
    factors = {'a_w1': 8.0,
     'a_w2': 8.0,
     'a_lnx_g': 5.291,
     'a_lnx_b': 8.0,
     'kv_norm_g': 8.0,
     'k_norm_g': 8.0,
     'b_norm_g': 8.0,
     'b_q_norm_g': 8.0,
     'f_norm_g': 2.877}
    for name, (base, spread) in spreads.items():
        noise = np.random.default_rng([zlib.crc32(name.encode()), seed]).standard_normal(out[name].shape)
        drawn = base * np.exp(spread * noise) if base else spread * noise
        out[name] = __import__('jax').numpy.asarray(drawn.astype(out[name].dtype))
    for name, factor in factors.items():
        out[name] = (out[name] * factor).astype(out[name].dtype)
    return out
```

```python
import math

import numpy as np
import concourse.bass as bass
from concourse import mybir
from contextlib import ExitStack

F32 = mybir.dt.float32
I32 = mybir.dt.int32
ALU = mybir.AluOpType
ACT = mybir.ActivationFunctionType
AX = mybir.AxisListType

P = 128
D, T = 1024, 256
KT, RT = D // P, T // P
HD, NH = 64, D // 64
LW, LG = 64, 160
FF = -(-8 * D // (3 * 256)) * 256
NF = FF // P
GROUPS = ((128, 1), (512, 4), (2048, 16))
NG = len(GROUPS)
QW = NG * D
KAPPA = math.exp(-0.5)
RMS_EPS, LNX_EPS = 1e-6, 64e-5
LEVELS = 7
NEG = -1e30
SCALE = HD ** -0.5

ROWS = ["mu0", "mu1", "mu2", "mu3", "mu4", "mu5", "w0", "a0", "k_k", "k_a", "r_k", "lnx_g", "lnx_b"]
NR = len(ROWS)


def constants():
    p = np.arange(P)[:, None]
    f = np.arange(P)[None, :]
    out = {"ident": (p == f).astype(np.float32)}
    out["halves"] = (p // HD == f // HD).astype(np.float32)
    strict, incl = (p < f), (p <= f)
    out["tri"] = np.concatenate([strict, incl, strict, incl], 1).astype(np.float32)
    lev = []
    for l in range(LEVELS):
        m = 1 << l
        lev.append(((p // (2 * m) == f // (2 * m)) & (p // m % 2 == 1) & (f // m % 2 == 0)).astype(np.float32))
    out["levels"] = np.concatenate(lev, 1)
    for r in range(RT):
        t = p + r * P
        s = np.arange((r + 1) * P)[None, :]
        parts = []
        for window, dil in GROUPS:
            ok = (t >= s) & ((t - s) % dil == 0) & (t - s <= window)
            parts.append(np.where(ok, 0.0, NEG).astype(np.float32))
        out[f"mask{r}"] = np.concatenate(parts, 1)
    inv = (10000.0 ** (-np.arange(0, HD, 2, dtype=np.float32) / HD)).astype(np.float32)
    ang = np.arange(T, dtype=np.float32)[:, None] * inv[None, :]
    cos, sin = np.cos(ang).astype(np.float32), np.sin(ang).astype(np.float32)
    c = np.concatenate([cos, cos], 1).reshape(RT, P, HD)
    s = np.concatenate([-sin, sin], 1).reshape(RT, P, HD)
    out["cos"] = np.concatenate([c[r] for r in range(RT)], 1)
    out["sin"] = np.concatenate([s[r] for r in range(RT)], 1)
    return out


CONSTS = constants()
CAT = {}
_at = 0
for _n, _v in CONSTS.items():
    CAT[_n] = (_at, _v.shape[1])
    _at += _v.shape[1]
NCONST = _at


def program(nc, ins, out):
    ctx = ExitStack()
    with ctx:
        def sb(name, shape, dt=F32):
            return ctx.enter_context(nc.sbuf_tensor(name, shape, dt))

        def sem(name):
            return ctx.enter_context(nc.semaphore(name))

        x = sb("x", [P, RT, D])
        cst = sb("cst", [P, NCONST])
        trib = sb("trib", [P, 4, P], I32)
        gain = sb("gain", [P, 2, D])
        rows = sb("rows", [16, D])
        par = sb("par", [P, KT, NR])
        omk = sb("omk", [P, KT])
        onec = sb("onec", [P, P])
        mhalf = sb("mhalf", [P, 16])
        small = sb("small", [P, 64])
        ring = sb("ring", [P, 9216])
        wmix = sb("wmix", [P, 4, KT * 256])
        work = sb("work", [P, 25600])

        def C(name):
            a, n = CAT[name]
            return cst[:, a:a + n]

        ident, halves = C("ident"), C("halves")

        class Carve:
            def __init__(self, at=0):
                self.at = at

            def take(self, size, pattern=None, **k):
                v = work[:, self.at:self.at + size]
                self.at += size
                assert self.at <= 25600, self.at
                return v.rearrange(pattern, **k) if pattern else v

        bank = [ctx.enter_context(nc.psum_tensor(f"bank{i}", [P, 512], F32)) for i in range(3)]
        wide = ctx.enter_context(nc.psum_tensor("wide", [P, 1024], F32))
        bank += [wide[:, 0:512], wide[:, 512:1024]]
        bank += [ctx.enter_context(nc.psum_tensor(f"bank{i}", [P, 512], F32)) for i in range(5, 8)]
        bank = [b[:, :] for b in bank]

        names = {}

        def S(name):
            if name not in names:
                names[name] = sem(name)
            return names[name]

        cv = Carve()
        hT = cv.take(KT * T, "p (k t) -> p k t", k=KT)
        dT = cv.take(KT * T, "p (k t) -> p k t", k=KT)
        M = work[:, 0:8 * 512].rearrange("p (u m t) -> p u m t", u=8, m=4)
        xr, xk, xv = (cv.take(KT * T, "p (k t) -> p k t", k=KT) for _ in range(3))
        tw = cv.take(T)
        ta = cv.take(T)
        tg = cv.take(2 * T, "p (k t) -> p k t", k=2)
        gat = cv.at
        xs = [cv.take(KT * T, "p (k t) -> p k t", k=KT) for _ in range(3)]
        hn = cv.take(RT * D, "p (r d) -> p r d", r=RT)
        w1s = cv.take(KT * LW, "p (k n) -> p k n", k=KT)
        a1s = cv.take(KT * LW, "p (k n) -> p k n", k=KT)
        g1s = cv.take(KT * LG, "p (k n) -> p k n", k=KT)
        cg = Carve(gat)
        n4 = dict(n=2, c=2)
        Us = cg.take(8 * P, "p (u t) -> p u t", u=8)
        Ts = cg.take(8 * P, "p (u t) -> p u t", u=8)
        Xs = cg.take(8 * P, "p (u t) -> p u t", u=8)
        ar = cg.take(8 * P, "p (n c m t) -> p n c m t", n=2, c=2, m=2)
        sz = cg.take(512, "p (n t) -> p n t", n=2)
        sa = cg.take(512, "p (n t) -> p n t", n=2)
        Gs = cg.take(4 * 129, "p (q t) -> p q t", q=4)
        Gc = cg.take(4 * 129, "p (q t) -> p q t", q=4)
        E1 = cg.take(4 * 129, "p (q t) -> p q t", q=4)
        En = sz.rearrange("p n t -> p (n t)")
        over_X = Xs.rearrange("p u t -> p (u t)")
        kkr = over_X[:, 0:512].rearrange("p (n t) -> p n t", n=2)
        sq = cg.take(512, "p (n t) -> p n t", n=2)
        nrm = cg.take(512)
        rn = over_X[:, 512:1024]
        kn = cg.take(512)
        t1 = cg.take(512, "p (n t) -> p n t", n=2)
        kT_ = cg.take(512, "p (n t) -> p n t", n=2)
        rkr = cg.take(512, "p (n t) -> p n t", n=2)
        bb = sq.rearrange("p n t -> p (n t)")
        kP = cg.take(512, "p (n t) -> p n t", n=2)
        bP = cg.take(512, "p (n t) -> p n t", n=2)
        vT = cg.take(512)
        gT = cg.take(512)
        bv = nrm
        Vn = cg.take(512, "p (c n i) -> p c n i", c=2, n=2)
        kPn = cg.take(256, "p (n i) -> p n i", n=2)
        bPn = cg.take(256, "p (n i) -> p n i", n=2)
        Zs = cg.take(256)
        UUs = cg.take(512, "p (c n i) -> p c n i", c=2, n=2)
        St = cg.take(256, "p (n i) -> p n i", n=2)
        oc = kkr.rearrange("p n t -> p (n t)")
        osq = kn
        on = t1.rearrange("p n t -> p (n t)").rearrange("p (c n i) -> p c n i", c=2, n=2)
        yT = kT_
        pg = sb("pg", [P, 2, NR + 1])
        w2s = sb("w2s", [LW, 256])
        a2s = sb("a2s", [LW, 256])
        g2s = sb("g2s", [P, 2, 256])
        gsm = sb("gsm", [P, 64])
        levels = C("levels").rearrange("p (l t) -> p l t", l=LEVELS)
        NGRP = D // 256

        cf = Carve()
        fhT = cf.take(KT * T, "p (k t) -> p k t", k=KT)
        fhn = cf.take(RT * D, "p (r d) -> p r d", r=RT)
        sg = cf.take(512, "p (b t) -> p b t", b=2)
        aT = cf.take(512, "p (b t) -> p b t", b=2)
        gus = [ring[:, b * 3072:b * 3072 + 2048].rearrange("p (k m n) -> p k m n", k=KT, m=2) for b in range(2)]
        dns = [ring[:, b * 3072 + 2048:b * 3072 + 3072] for b in range(2)]

        ca = Carve(2 * KT * T)
        khT, qhT = (work[:, i * KT * T:(i + 1) * KT * T].rearrange("p (k t) -> p k t", k=KT) for i in range(2))
        ahn = ca.take(RT * D, "p (r d) -> p r d", r=RT)
        ahn2 = ca.take(RT * D, "p (r d) -> p r d", r=RT)
        rot = ca.take(8 * 192, "p (w m r g d) -> p w m r g d", w=2, m=2, r=2, g=3)
        qkg = ca.take(2 * 192, "p (w g d) -> p w g d", w=2, g=3)
        asq = ca.take(384)
        akn = ca.take(384, "p (g h d) -> p g h d", g=3, h=2)
        am1 = ca.take(384, "p (g h d) -> p g h d", g=3, h=2)
        am2 = ca.take(384, "p (g h d) -> p g h d", g=3, h=2)
        akr = ca.take(2 * 384, "p (b n) -> p b n", b=2)
        kTt = ca.take(3 * T, "p (g t) -> p g t", g=3)
        qTt = ca.take(3 * T, "p (g t) -> p g t", g=3)
        Vs = ca.take(RT * 384, "p (r n) -> p r n", r=RT)
        pr = ca.take(2 * 768, "p (b n) -> p b n", b=2)
        pT = ca.take(2 * 768, "p (b n) -> p b n", b=2)
        ao = ca.take(RT * P, "p (r n) -> p r n", r=RT)
        oT = ca.take(KT * T, "p (k t) -> p k t", k=KT)
        asm = gsm
        wqkv = [ring[:, i * 3072:(i + 1) * 3072].rearrange("p (k g n) -> p k g n", k=KT, g=3) for i in range(3)]
        wo_v = wmix[:, :, :].rearrange("p a (b n) -> p (a b) n", n=D)

        s_const, s_x, s_rows, s_lora = S("const_loaded"), S("x_loaded"), S("rows_loaded"), S("lora_loaded")
        s_gain = [S("gain0_loaded"), S("gain1_loaded")]
        s_wm = [S(f"wmix{i}_loaded") for i in range(4)]
        s_l2 = S("lora2_loaded")
        s_gu = [S(f"gate_up{i}_loaded") for i in range(2)]
        s_dn = [S(f"down{i}_loaded") for i in range(2)]
        s_qkv = [S(f"qkv{i}_loaded") for i in range(3)]
        s_wo, s_qkg, s_out = S("wo_loaded"), S("qk_gains_loaded"), S("stored")

        block = ctx.enter_context(nc.Block())

        @block.sync
        def _(sp):
            sp.dma_start(x[:, :, :], ins["x"][0].rearrange("(r p) d -> p r d", p=P)).then_inc(s_x, 16)

            def load_gain(i, src):
                sp.dma_start(gain[:, i, :], src.partition_broadcast(P)).then_inc(s_gain[i], 16)

            load_gain(0, ins["a_norm_g"][0])
            sp.dma_start(cst[:, :], ins["const"]).then_inc(s_const, 16)
            for i in range(6):
                sp.dma_start(rows[i:i + 1, :], ins["a_mu"][0][i:i + 1, :]).then_inc(s_rows, 16)
            for i, n in enumerate(["a_w0", "a_a0", "a_k_k", "a_k_a", "a_r_k", "a_lnx_g", "a_lnx_b"]):
                src = ins[n].rearrange("a h j -> a (h j)") if n == "a_r_k" else ins[n]
                sp.dma_start(rows[6 + i:7 + i, :], src).then_inc(s_rows, 16)
            for dst, n in ((w1s, "a_w1"), (a1s, "a_a1"), (g1s, "a_g1")):
                sp.dma_start(dst, ins[n][0].rearrange("(k p) n -> p k n", p=P)).then_inc(s_lora, 16)
            load_gain(1, ins["f_norm_g"][0])

            cols = [ins[n][0].rearrange("(k p) n -> p k n", p=P) for n in ("a_w_r", "a_w_k", "a_w_v")]
            wo_rows = ins["a_w_o"][0].rearrange("(g n p) d -> g p n d", p=P, n=2)

            def load_mix(it):
                for i, free in ((1, "pe_k"), (0, "pe_r"), (2, "pe_v")):
                    if it is not None:
                        sp.wait_ge(S(free), it)
                    c0 = 0 if it is None else it * 256
                    sp.dma_start(wmix[:, i, :].rearrange("p (k n) -> p k n", k=KT),
                                 cols[i][:, :, bass.ds(c0, 256)]).then_inc(s_wm[i], 16)
                if it is not None:
                    sp.wait_ge(S("pe_z"), it * 2)
                    sp.wait_ge(S("pe_g"), it)
                c0 = 0 if it is None else it * 256
                sp.dma_start(w2s[:, :], ins["a_w2"][0][:, bass.ds(c0, 256)]).then_inc(s_l2, 16)
                sp.dma_start(a2s[:, :], ins["a_a2"][0][:, bass.ds(c0, 256)]).then_inc(s_l2, 16)
                sp.dma_start(g2s[:, 0, :], ins["a_g2"][0][0:P, bass.ds(c0, 256)]).then_inc(s_l2, 16)
                sp.dma_start(g2s[0:LG - P, 1, :], ins["a_g2"][0][P:LG, bass.ds(c0, 256)]).then_inc(s_l2, 16)
                if it is not None:
                    sp.wait_ge(S("pe_wo"), it * 4)
                sp.dma_start(wmix[:, 3, :].rearrange("p (n d) -> p n d", n=2),
                             wo_rows[0 if it is None else bass.ds(it, 1)] if it is None
                             else wo_rows[bass.ds(it, 1)].rearrange("a p n d -> p (a n) d")).then_inc(s_wm[3], 16)

            load_mix(None)
            with sp.Fori(1, NGRP) as it:
                load_mix(it)

            def load_ffn(layer, f, b, n, first):
                gu = ins["f_w_gu"][layer].rearrange("(k p) (m n) -> p m k n", p=P, m=2)
                if not first:
                    sp.wait_ge(S("pe_gu"), n[0])
                for m in range(2):
                    sp.dma_start(gus[b][:, :, m, :], gu[:, m, :, bass.ds(f * P, P)]).then_inc(s_gu[b], 16)
                if not first:
                    sp.wait_ge(S("pe_dn"), n[1])
                sp.dma_start(dns[b], ins["f_w_down"][layer][bass.ds(f * P, P), :]).then_inc(s_dn[b], 16)

            def ffn(layer):
                base = layer * NF
                for b in range(2):
                    load_ffn(layer, b, b, None, True)
                with sp.Fori(1, NF // 2) as i:
                    for b in range(2):
                        done = i * 2 + (base + b - 1)
                        load_ffn(layer, i * 2 + b, b, (done, done), False)

            ffn(0)
            sp.wait_ge(S("dve_hn"), 2 * RT)
            load_gain(0, ins["kv_norm_g"])
            load_gain(1, ins["b_norm_g"][0])
            kvw = ins["w_kv"].rearrange("(k p) (m g n) -> p m k g n", p=P, m=2, g=NG)
            qw = ins["b_w_q"][0].rearrange("(k p) (g n) -> p k g n", p=P, g=NG)
            srcs = [kvw[:, 0], qw, kvw[:, 1]]

            def load_qkv(p, first):
                for i, free in enumerate(("pe_pk", "pe_pq", "pe_pv")):
                    if not first:
                        sp.wait_ge(S(free), p * 2)
                    c0 = 0 if first else p * P
                    for g in range(NG):
                        sp.dma_start(wqkv[i][:, :, g, :], srcs[i][:, :, g, bass.ds(c0, P)]).then_inc(s_qkv[i], 16)

            sp.wait_ge(S("dve_ffn"), 1)
            for w, n in ((0, "k_norm_g"), (1, "b_q_norm_g")):
                src = ins[n] if w == 0 else ins[n][0]
                sp.dma_start(qkg[:, w], src.partition_broadcast(P)).then_inc(s_qkg, 16)
            load_qkv(0, True)
            sp.dma_start(wo_v, ins["b_w_o"][0].rearrange("(k p) d -> p k d", p=P)).then_inc(s_wo, 16)
            with sp.Fori(1, KT) as p:
                load_qkv(p, False)
            sp.wait_ge(S("dve_ahn"), 2 * RT)
            load_gain(0, ins["f_norm_g"][1])
            sp.wait_ge(S("pe_pv"), KT * 2)
            sp.wait_ge(S("pe_pk"), KT * 2)
            sp.wait_ge(S("pe_pq"), KT * 2)
            ffn(1)
            sp.wait_ge(S("dve_ffn"), 2)
            sp.dma_start(out[0].rearrange("(r p) d -> p r d", p=P), x[:, :, :]).then_inc(s_out, 16)
            sp.wait_ge(s_out, 16)

        @block.tensor
        def _(pe):
            def mm(o, a, b, start=True, stop=True):
                return pe.matmul(o, a, b, start=start, stop=stop)

            def turn_rows(src, n0):
                for r in range(RT):
                    pe.wait_ge(S(src[1]), n0 + r + 1)
                    for j in range(2):
                        for q in range(4):
                            k = 4 * j + q
                            m = pe.transpose(bank[2 * r + j][:, q * P:(q + 1) * P], src[0][:, r, k * P:(k + 1) * P], ident)
                        m.then_inc(S("pe_turned"), 1)

            pe.wait_ge(s_const, 16)
            pe.wait_ge(s_rows, 16 * NR)
            for k in range(KT):
                m = pe.transpose(bank[7][:, k * NR:(k + 1) * NR], rows[0:NR, k * P:(k + 1) * P], ident[0:NR, 0:NR])
            m.then_inc(S("pe_par"), 1)
            turn_rows((hn, "dve_hn"), 0)
            pe.wait_ge(s_lora, 48)
            pe.wait_ge(S("act_turned"), 2)
            pe.wait_ge(S("dve_turned"), 2)
            pe.wait_ge(S("dve_xs"), 1)
            for k in range(KT):
                m = mm(bank[0][0:LW, 0:T], w1s[:, k, :], xs[0][:, k, :], k == 0, k == KT - 1)
            m.then_inc(S("pe_lora"), 1)
            pe.wait_ge(S("dve_xs"), 2)
            for k in range(KT):
                m = mm(bank[1][0:LW, 0:T], a1s[:, k, :], xs[1][:, k, :], k == 0, k == KT - 1)
            m.then_inc(S("pe_lora"), 1)
            pe.wait_ge(S("dve_xs"), 3)
            for k in range(KT):
                mm(bank[2][:, 0:T], g1s[:, k, 0:P], xs[2][:, k, :], k == 0, k == KT - 1)
            for k in range(KT):
                m = mm(bank[3][0:LG - P, 0:T], g1s[:, k, P:LG], xs[2][:, k, :], k == 0, k == KT - 1)
            m.then_inc(S("pe_lora"), 1)

            def project(b, i, src, name):
                for n in range(2):
                    for k in range(KT):
                        w = wmix[:, i, :].rearrange("p (k n) -> p k n", k=KT)[:, k, n * P:(n + 1) * P]
                        m = mm(bank[b][:, n * T:(n + 1) * T], w, src[:, k, :], k == 0, k == KT - 1)
                m.then_inc(S(name), 1)

            def unit(nn, h):
                return 2 * nn + h

            def group(it):
                pe.wait_ge(s_l2, it * 64 + 64)
                pe.wait_ge(S("act_lora"), 4)
                for n in range(2):
                    m = mm(bank[0][:, n * T:(n + 1) * T], w2s[:, n * P:(n + 1) * P], tw[0:LW, :])
                m.then_inc(S("pe_z"), 1)
                for n in range(2):
                    m = mm(bank[1][:, n * T:(n + 1) * T], a2s[:, n * P:(n + 1) * P], ta[0:LW, :])
                m.then_inc(S("pe_z"), 1)
                pe.wait_ge(s_wm[1], it * 16 + 16)
                pe.wait_ge(S("dve_mix"), 1)
                project(2, 1, xk, "pe_k")
                pe.wait_ge(s_wm[0], it * 16 + 16)
                pe.wait_ge(S("dve_mix"), 2)
                project(4, 0, xr, "pe_r")
                pe.wait_ge(S("act_sq"), it + 1)
                mm(bank[3], halves, sq.rearrange("p n t -> p (n t)")).then_inc(S("pe_ss"), 1)
                pe.wait_ge(s_wm[2], it * 16 + 16)
                pe.wait_ge(S("dve_mix"), 3)
                project(5, 2, xv, "pe_v")
                for n in range(2):
                    mm(bank[6][:, n * T:(n + 1) * T], g2s[:, 0, n * P:(n + 1) * P], tg[:, 0, :], True, False)
                    m = mm(bank[6][:, n * T:(n + 1) * T], g2s[0:LG - P, 1, n * P:(n + 1) * P], tg[0:LG - P, 1, :], False, True)
                m.then_inc(S("pe_g"), 1)
                pe.wait_ge(S("dve_rkr"), it + 1)
                mm(bank[7], halves, rkr.rearrange("p n t -> p (n t)")).then_inc(S("pe_bonus"), 1)
                pe.wait_ge(S("act_v"), it + 1)
                for c in range(2):
                    for n in range(2):
                        m = pe.transpose(bank[0][:, (2 * c + n) * P:(2 * c + n + 1) * P],
                                         vT[:, n * T + c * P:n * T + (c + 1) * P], ident)
                m.then_inc(S("pe_tv"), 1)
                pe.wait_ge(S("dve_scaled"), it + 1)
                for j, src in enumerate((kP, bP)):
                    for n in range(2):
                        m = pe.transpose(bank[1][:, (2 * j + n) * P:(2 * j + n + 1) * P], src[:, n, 0:P], ident)
                m.then_inc(S("pe_tk"), 1)

                for c in range(2):
                    for nn in range(2):
                        for h in range(2):
                            u = 4 * c + 2 * nn + h
                            if u >= 4:
                                pe.wait_ge(S("dve_mats"), it * 8 + u - 3)
                            b = bank[2 + u % 4]
                            hp = slice(h * HD, (h + 1) * HD)
                            rhs = ar[hp, nn, c, :, :].rearrange("p m t -> p (m t)")
                            mm(b[:, 0:256], bP[hp, nn, c * P:(c + 1) * P], rhs)
                            m = mm(b[:, 256:512], kP[hp, nn, c * P:(c + 1) * P], rhs)
                            m.then_inc(S("pe_mats"), 1)
                pe.wait_ge(S("act_vn"), it + 1)
                pe.wait_ge(S("dve_mats"), it * 8 + 4)
                pe.wait_ge(S("act_g"), it + 1)
                for u in range(4):
                    m = mm(bank[6][:, u * HD:(u + 1) * HD], M[:, u, 2, :], Vn[:, 0, u // 2, (u % 2) * HD:(u % 2 + 1) * HD])
                m.then_inc(S("pe_z0"), 1)

                for l in range(LEVELS):
                    for q in range(2):
                        if l == 0:
                            pe.wait_ge(S("dve_mats"), it * 8 + 4 * q + 4)
                            pe.wait_ge(S("act_vn"), it + 1)
                            pe.wait_ge(S("act_kn"), it + 1)
                        else:
                            pe.wait_ge(S("act_T"), it * 12 + 2 * l + q - 1)
                        for j in range(4):
                            u = 4 * q + j
                            m = mm(bank[q][:, j * P:(j + 1) * P], M[:, u, 0, :], ident if l == 0 else Ts[:, u, :])
                        m.then_inc(S("pe_X"), 1)
                    for q in range(2):
                        pe.wait_ge(S("dve_X"), it * 14 + 2 * l + q + 1)
                        for j in range(4):
                            u = 4 * q + j
                            m = mm(bank[2 + q][:, j * P:(j + 1) * P], Xs[:, u, :], ident if l == 0 else Us[:, u, :])
                        m.then_inc(S("pe_U"), 1)
                    for q in range(2):
                        pe.wait_ge(S("dve_U"), it * 14 + 2 * l + q + 1)
                        if l < LEVELS - 1:
                            for j in range(4):
                                u = 4 * q + j
                                m = pe.transpose(bank[4 + q][:, j * P:(j + 1) * P], Us[:, u, :], ident)
                            m.then_inc(S("pe_T"), 1)

                def hcols(v, u):
                    return v[:, u * HD:(u + 1) * HD]

                pe.wait_ge(S("act_z"), it * 2 + 1)
                for u in range(4):
                    m = mm(hcols(bank[1], u), Us[:, u, :], hcols(Zs, u))
                m.then_inc(S("pe_uu"), 1)
                pe.wait_ge(S("act_uu"), it * 2 + 1)
                for n in range(2):
                    mm(bank[2][:, n * P:(n + 1) * P], kPn[:, n, :], Vn[:, 0, n, :], True, False)
                    m = mm(bank[2][:, n * P:(n + 1) * P], bPn[:, n, :], UUs[:, 0, n, :], False, True)
                m.then_inc(S("pe_S"), 1)
                for u in range(4):
                    hh = slice((u % 2) * HD, (u % 2 + 1) * HD)
                    mm(hcols(bank[3], u), M[:, u, 3, :], Vn[:, 0, u // 2, hh], True, False)
                    mm(hcols(bank[3], u), M[:, u, 1, :], UUs[:, 0, u // 2, hh], False, True)
                pe.wait_ge(S("dve_S"), it + 1)
                for n in range(2):
                    mm(bank[4][:, n * P:(n + 1) * P], ar[:, n, 1, 0, :], St[:, n, :], True, False)
                    for h in range(2):
                        u = 2 * n + h
                        m = mm(hcols(bank[4], u), M[:, 4 + u, 2, :], Vn[:, 1, n, h * HD:(h + 1) * HD], False, h == 1)
                m.then_inc(S("pe_z1"), 1)
                pe.wait_ge(S("act_z"), it * 2 + 2)
                for u in range(4):
                    m = mm(hcols(bank[5], u), Us[:, 4 + u, :], hcols(Zs, u))
                m.then_inc(S("pe_uu"), 1)
                pe.wait_ge(S("act_uu"), it * 2 + 2)
                for n in range(2):
                    mm(bank[3][:, 256 + n * P:256 + (n + 1) * P], ar[:, n, 1, 1, :], St[:, n, :], True, False)
                    for h in range(2):
                        u = 2 * n + h
                        hh = slice(h * HD, (h + 1) * HD)
                        o = bank[3][:, 256 + u * HD:256 + (u + 1) * HD]
                        mm(o, M[:, 4 + u, 3, :], Vn[:, 1, n, hh], False, False)
                        m = mm(o, M[:, 4 + u, 1, :], UUs[:, 1, n, hh], False, h == 1)
                m.then_inc(S("pe_o"), 1)
                pe.wait_ge(S("dve_on"), it + 1)
                for n in range(2):
                    for c in range(2):
                        m = pe.transpose(bank[6][:, (2 * n + c) * P:(2 * n + c + 1) * P], on[:, c, n, :], ident)
                m.then_inc(S("pe_on"), 1)
                pe.wait_ge(S("dve_y"), it + 1)
                pe.wait_ge(s_wm[3], it * 16 + 16)
                for r in range(RT):
                    for j in range(2):
                        for n in range(2):
                            w = wmix[:, 3, :].rearrange("p (n d) -> p n d", n=2)[:, n, j * 512:(j + 1) * 512]
                            m = mm(bank[(0, 1, 2, 5)[2 * r + j]], yT[:, n, r * P:(r + 1) * P], w, n == 0, n == 1)
                        m.then_inc(S("pe_wo"), 1)
                pe.wait_ge(S("dve_xadd"), it * 4 + 4)

            with pe.Fori(0, NGRP) as it:
                group(it)

            def ffn(layer):
                base = layer * NF
                turn_rows((fhn, "dve_hn"), RT * (1 + layer))
                t0 = 2 + 2 * layer
                pe.wait_ge(S("act_turned"), (4, 6)[layer])
                pe.wait_ge(S("dve_turned"), (4, 6)[layer])

                def gate_up(f, b, n, done):
                    pe.wait_ge(s_gu[b], n * 32)
                    if done is not None:
                        pe.wait_ge(S("dve_act"), done)
                    for m_ in range(2):
                        for k in range(KT):
                            m = mm(bank[4 + b][:, m_ * T:(m_ + 1) * T], gus[b][:, k, m_, :], fhT[:, k, :], k == 0, k == KT - 1)
                    m.then_inc(S("pe_gu"), 1)

                def down(f, b, n, first=False, last=False):
                    pe.wait_ge(S("dve_act"), f + base + 1)
                    pe.wait_ge(s_dn[b], n * 16)
                    for r in range(RT):
                        for j in range(2):
                            m = mm(bank[2 * r + j], aT[:, b, r * P:(r + 1) * P], dns[b][:, j * 512:(j + 1) * 512], first, last)
                    m.then_inc(S("pe_dn"), 1)

                n0 = layer * (NF // 2)
                gate_up(0, 0, n0 + 1, None)
                gate_up(1, 1, n0 + 1, None)
                down(0, 0, n0 + 1, first=True)
                gate_up(2, 0, n0 + 2, base + 1)
                down(1, 1, n0 + 1)
                with pe.Fori(1, NF // 2 - 1) as i:
                    gate_up(2 * i + 1, 1, i + (n0 + 1), i * 2 + base)
                    down(2 * i, 0, i + (n0 + 1))
                    gate_up(2 * i + 2, 0, i + (n0 + 2), i * 2 + (base + 1))
                    down(2 * i + 1, 1, i + (n0 + 1))
                i = NF // 2 - 1
                gate_up(2 * i + 1, 1, n0 + i + 1, 2 * i + base)
                down(2 * i, 0, n0 + i + 1)
                down(2 * i + 1, 1, n0 + i + 1, last=True)

            ffn(0)

            pe.wait_ge(S("dve_ffn"), 1)
            turn_rows((ahn, "dve_ahn"), 0)
            for r in range(RT):
                pe.wait_ge(S("dve_ahn"), RT + r + 1)
                for j in range(2):
                    for q in range(4):
                        k = 4 * j + q
                        m = pe.transpose(bank[4 + 2 * r + j][:, q * P:(q + 1) * P], ahn2[:, r, k * P:(k + 1) * P], ident)
                    m.then_inc(S("pe_turned"), 1)
            pe.wait_ge(S("act_aturned"), 4)
            pe.wait_ge(S("dve_aturned"), 4)

            def heads(p):
                def proj(i, src, name):
                    for r in range(RT):
                        if i == 0:
                            pe.wait_ge(s_qkv[0], p * 48 + 48)
                        elif i == 1:
                            pe.wait_ge(S("dve_kn"), p * 4 + r + 1)
                            pe.wait_ge(s_qkv[1], p * 48 + 48)
                        else:
                            pe.wait_ge(S("dve_kn"), p * 4 + r + 3)
                            pe.wait_ge(s_qkv[2], p * 48 + 48)
                        for k in range(KT):
                            m = mm(bank[r][:, 0:384], src[:, k, r * P:(r + 1) * P],
                                   wqkv[i][:, k, :, :].rearrange("p g n -> p (g n)"), k == 0, k == KT - 1)
                        m.then_inc(S(name), 1)

                def turn_qk(w):
                    for r in range(RT):
                        pe.wait_ge(S("dve_kr"), p * 4 + 2 * w + r + 1)
                        if w == 1:
                            pe.wait_ge(S("act_qkT"), p * 4 + r + 1)
                        for g in range(NG):
                            m = pe.transpose(bank[5 + r][:, g * P:(g + 1) * P], akr[:, r, g * P:(g + 1) * P], ident)
                        m.then_inc(S("pe_qkT"), 1)

                proj(0, khT, "pe_pk")
                proj(1, qhT, "pe_pq")
                turn_qk(0)
                proj(2, khT, "pe_pv")
                turn_qk(1)

                def score(i):
                    h, r = i // 2, i % 2
                    if i >= 2:
                        pe.wait_ge(S("dve_sm"), p * 4 + i - 1)
                    hp = slice(h * HD, (h + 1) * HD)
                    w = (r + 1) * P
                    for g in range(NG):
                        o = bank[2][:, g * P:(g + 1) * P] if r == 0 else wide[:, g * T:(g + 1) * T]
                        m = mm(o, qTt[hp, g, r * P:(r + 1) * P], kTt[hp, g, 0:w])
                    m.then_inc(S("pe_s"), 1)

                def turn_p(i):
                    h, r = i // 2, i % 2
                    pe.wait_ge(S("act_p"), p * 4 + i + 1)
                    if i > 0:
                        pe.wait_ge(S("act_pT"), p * 4 + i)
                    n = NG * (r + 1)
                    for j in range(n):
                        b = bank[5 + j // 4]
                        m = pe.transpose(b[:, j % 4 * P:(j % 4 + 1) * P], pr[:, i % 2, j * P:(j + 1) * P], ident)
                    m.then_inc(S("pe_pT"), 1)

                def values(i):
                    h, r = i // 2, i % 2
                    pe.wait_ge(S("act_pT"), p * 4 + i + 1)
                    n = NG * (r + 1)
                    for j in range(n):
                        g, s = j // (r + 1), j % (r + 1)
                        m = mm(bank[7][:, i * HD:(i + 1) * HD], pT[:, i % 2, j * P:(j + 1) * P],
                               Vs[:, s, g * P + h * HD:g * P + (h + 1) * HD], j == 0, j == n - 1)
                    if i == 3:
                        m.then_inc(S("pe_o2"), 1)

                pe.wait_ge(S("act_qkT"), p * 4 + 4)
                pe.wait_ge(S("act_Vs"), p * 2 + 2)
                score(0)
                score(1)
                score(2)
                turn_p(0)
                score(3)
                values(0)
                turn_p(1)
                values(1)
                turn_p(2)
                values(2)
                turn_p(3)
                values(3)
                pe.wait_ge(S("act_ao"), p * 4 + 4)
                for r in range(RT):
                    m = pe.transpose(bank[7][:, 256 + r * P:256 + (r + 1) * P], ao[:, r, :], ident)
                m.then_inc(S("pe_oT"), 1)

            with pe.Fori(0, KT) as p:
                heads(p)
            pe.wait_ge(s_wo, 16)
            pe.wait_ge(S("act_oT"), KT)
            for r in range(RT):
                for j in range(2):
                    for k in range(KT):
                        m = mm(bank[2 * r + j], oT[:, k, r * P:(r + 1) * P], wo_v[:, k, j * 512:(j + 1) * 512], k == 0, k == KT - 1)
                    m.then_inc(S("pe_awo"), 1)
            ffn(1)

        @block.scalar
        def _(act):
            def A(o, i, f, **k):
                return act.activation(o, i, f, **k)

            def squares(n):
                for r in range(RT):
                    if n or r:
                        act.wait_ge(S("act_ss"), n * RT + r)
                    A(work[:, 25600 - 1024:25600], x[:, r, :], ACT.Square, accum_out=small[:, r:r + 1]).then_inc(S("act_ss"), 1)

            act.wait_ge(s_x, 16)
            squares(0)

            def turned(dst, b0, n0, done):
                for r in range(RT):
                    act.wait_ge(S("pe_turned"), n0 + 2 * r + 2)
                    A(dst[:, 4:8, r * P:(r + 1) * P], bank[b0 + 2 * r + 1].rearrange("p (q t) -> p q t", q=4), ACT.Copy).then_inc(S(done), 1)

            turned(hT, 0, 0, "act_turned")
            act.wait_ge(S("pe_lora"), 1)
            A(tw[0:LW, :], bank[0][0:LW, 0:T], ACT.Tanh).then_inc(S("act_lora"), 1)
            act.wait_ge(S("pe_lora"), 2)
            A(ta[0:LW, :], bank[1][0:LW, 0:T], ACT.Copy).then_inc(S("act_lora"), 1)
            act.wait_ge(S("pe_lora"), 3)
            A(tg[:, 0, :], bank[2][:, 0:T], ACT.Sigmoid).then_inc(S("act_lora"), 1)
            A(tg[0:LG - P, 1, :], bank[3][0:LG - P, 0:T], ACT.Sigmoid).then_inc(S("act_lora"), 1)

            def pgc(n, name):
                i = ROWS.index(name)
                return pg[:, n, i:i + 1]

            def group(it):
                act.wait_ge(S("dve_pg"), it + 1)
                act.wait_ge(S("pe_z"), it * 2 + 1)
                for n in range(2):
                    m = A(sz[:, n, :], bank[0][:, n * T:(n + 1) * T], ACT.Sigmoid, bias=pgc(n, "w0"))
                m.then_inc(S("act_sz"), 1)
                act.wait_ge(S("pe_z"), it * 2 + 2)
                for n in range(2):
                    m = A(sa[:, n, :], bank[1][:, n * T:(n + 1) * T], ACT.Sigmoid, bias=pgc(n, "a0"))
                m.then_inc(S("act_sa"), 1)
                act.wait_ge(S("pe_k"), it + 1)
                for n in range(2):
                    A(kkr[:, n, :], bank[2][:, n * T:(n + 1) * T], ACT.Copy, scale=pgc(n, "k_k"))
                    m = A(sq[:, n, :], bank[2][:, n * T:(n + 1) * T], ACT.Square, scale=pgc(n, "k_k"))
                m.then_inc(S("act_sq"), 1)
                act.wait_ge(S("dve_G"), it + 1)
                A(E1[:, :, :], Gc[:, :, :], ACT.Exp, scale=-KAPPA).then_inc(S("act_E"), 1)
                A(En.rearrange("p (q t) -> p q t", q=4), Gc[:, :, 1:129], ACT.Exp, scale=KAPPA).then_inc(S("act_E"), 1)
                A(gsm[:, 2:4], gsm[:, 0:2], ACT.Exp, scale=-KAPPA).then_inc(S("act_E"), 1)
                act.wait_ge(S("dve_ssm"), it + 1)
                A(nrm, rn, ACT.Sqrt).then_inc(S("act_nrm"), 1)
                act.wait_ge(S("pe_v"), it + 1)
                A(vT, bank[5], ACT.Copy).then_inc(S("act_v"), 1)
                act.wait_ge(S("pe_g"), it + 1)
                A(gT, bank[6], ACT.Copy).then_inc(S("act_g"), 1)
                act.wait_ge(S("pe_tv"), it + 1)
                A(Vn.rearrange("p c n i -> p (c n i)"), bank[0], ACT.Copy).then_inc(S("act_vn"), 1)
                act.wait_ge(S("pe_tk"), it + 1)
                A(kPn.rearrange("p n i -> p (n i)"), bank[1][:, 0:256], ACT.Copy)
                A(bPn.rearrange("p n i -> p (n i)"), bank[1][:, 256:512], ACT.Copy).then_inc(S("act_kn"), 1)
                act.wait_ge(S("pe_z0"), it + 1)
                A(Zs, bank[6][:, 0:256], ACT.Copy).then_inc(S("act_z"), 1)
                for l in range(LEVELS - 1):
                    for q in range(2):
                        act.wait_ge(S("pe_T"), it * 12 + 2 * l + q + 1)
                        A(Ts[:, 4 * q:4 * q + 4, :], bank[4 + q].rearrange("p (u t) -> p u t", u=4), ACT.Copy).then_inc(S("act_T"), 1)
                for c in range(2):
                    if c == 1:
                        act.wait_ge(S("pe_z1"), it + 1)
                        A(Zs, bank[4][:, 0:256], ACT.Copy).then_inc(S("act_z"), 1)
                    act.wait_ge(S("pe_uu"), it * 2 + c + 1)
                    A(UUs[:, c, :, :].rearrange("p n i -> p (n i)"), bank[(1, 5)[c]][:, 0:256], ACT.Copy).then_inc(S("act_uu"), 1)
                act.wait_ge(S("dve_oc"), it + 1)
                A(osq, oc, ACT.Square).then_inc(S("act_osq"), 1)

            with act.Fori(0, NGRP) as it:
                group(it)

            def ffn(layer):
                base = layer * NF
                act.wait_ge(S("dve_xadd") if layer == 0 else S("dve_awo"), 4 * NGRP if layer == 0 else 4)
                squares((1, 3)[layer])
                turned(fhT, 0, (4, 16)[layer], "act_turned")
                with act.Fori(0, NF // 2) as i:
                    for b in range(2):
                        act.wait_ge(S("pe_gu"), i * 2 + (base + b + 1))
                        A(sg[:, b, :], bank[4 + b][:, 0:T], ACT.Silu).then_inc(S("act_sg"), 1)

            ffn(0)
            act.wait_ge(S("dve_ffn"), 1)
            squares(2)
            turned(khT, 0, 8, "act_aturned")
            turned(qhT, 4, 12, "act_aturned")

            def heads(p):
                for w in range(2):
                    for r in range(RT):
                        act.wait_ge(S("pe_pk" if w == 0 else "pe_pq"), p * 2 + r + 1)
                        A(asq, bank[r][:, 0:384], ACT.Square).then_inc(S("act_asq"), 1)
                        act.wait_ge(S("dve_ass"), p * 4 + 2 * w + r + 1)
                for r in range(RT):
                    act.wait_ge(S("pe_qkT"), p * 4 + r + 1)
                    A(kTt[:, :, r * P:(r + 1) * P], bank[5 + r][:, 0:384].rearrange("p (g t) -> p g t", g=3), ACT.Copy).then_inc(S("act_qkT"), 1)
                for r in range(RT):
                    act.wait_ge(S("pe_pv"), p * 2 + r + 1)
                    A(Vs[:, r, :], bank[r][:, 0:384], ACT.Copy).then_inc(S("act_Vs"), 1)
                for r in range(RT):
                    act.wait_ge(S("pe_qkT"), p * 4 + r + 3)
                    A(qTt[:, :, r * P:(r + 1) * P], bank[5 + r][:, 0:384].rearrange("p (g t) -> p g t", g=3), ACT.Copy).then_inc(S("act_qkT"), 1)

                def probs(i):
                    r = i % 2
                    n = NG * (r + 1) * P
                    act.wait_ge(S("dve_nm"), p * 4 + i + 1)
                    A(pr[:, i % 2, 0:n], pr[:, i % 2, 0:n], ACT.Exp, bias=asm[:, 4 + i:5 + i], scale=SCALE,
                      accum_out=asm[:, 8 + i:9 + i]).then_inc(S("act_p"), 1)

                def copy_pT(i):
                    r = i % 2
                    act.wait_ge(S("pe_pT"), p * 4 + i + 1)
                    n = NG * (r + 1) * P
                    m = A(pT[:, i % 2, 0:min(n, 512)], bank[5][:, 0:min(n, 512)], ACT.Copy)
                    if n > 512:
                        m = A(pT[:, i % 2, 512:n], bank[6][:, 0:n - 512], ACT.Copy)
                    m.then_inc(S("act_pT"), 1)

                probs(0)
                probs(1)
                copy_pT(0)
                probs(2)
                copy_pT(1)
                probs(3)
                copy_pT(2)
                copy_pT(3)
                act.wait_ge(S("pe_o2"), p + 1)
                act.wait_ge(S("dve_rden"), p + 1)
                for i in range(4):
                    h, r = i // 2, i % 2
                    A(ao[:, r, h * HD:(h + 1) * HD], bank[7][:, i * HD:(i + 1) * HD], ACT.Copy,
                      scale=asm[:, 12 + i:13 + i]).then_inc(S("act_ao"), 1)
                act.wait_ge(S("pe_oT"), p + 1)
                A(oT[:, bass.ds(p, 1), :].rearrange("p k t -> p (k t)"), bank[7][:, 256:512], ACT.Copy).then_inc(S("act_oT"), 1)

            with act.Fori(0, KT) as p:
                heads(p)
            ffn(1)

        @block.vector
        def _(dve):
            def tt(o, a, b, op):
                return dve.tensor_tensor(o, a, b, op)

            def stt(o, a, s, b, op0, op1):
                return dve.scalar_tensor_tensor(o, a, s, b, op0, op1)

            chain = S("dve_step")
            steps = [0]

            def then(m, it=None, n=0):
                m.then_inc(chain, 1)

            class Seq:
                def __init__(self, base=0):
                    self.n = base
                    self.per = 0
                    self.it = None

                def start(self, it, per):
                    self.it, self.per, self.k = it, per, 0

                def mark(self, m):
                    m.then_inc(chain, 1)
                    if self.it is None:
                        self.n += 1
                    else:
                        self.k += 1

                def sync(self):
                    if self.it is None:
                        dve.wait_ge(chain, self.n)
                    else:
                        dve.wait_ge(chain, self.it * self.per + (self.n + self.k))

                def end(self, count):
                    assert self.k == self.per, (self.k, self.per)
                    self.n += count * self.per
                    self.it = None

            q = Seq()

            def step(m):
                q.mark(m)
                q.sync()

            step(dve.memset(onec[:, :], 1.0))
            dve.memset(mhalf[:, :], -0.5).then_inc(S("dve_mhalf"), 1)
            dve.wait_ge(s_const, 16)
            tri_f = C("tri").rearrange("p (m t) -> p m t", m=4)
            step(dve.tensor_copy(trib[:, :, :], tri_f))

            def rstd(n, outs, name, first_gain):
                for r in range(RT):
                    dve.wait_ge(S("act_ss"), n * RT + r + 1)
                dve.tensor_scalar(small[:, 2:4], small[:, 0:2], 1.0 / D, RMS_EPS, ALU.mult, ALU.add).then_inc(S("dve_ms"), 1)
                dve.wait_ge(S("pool_rs"), n + 1)
                for o, gi in outs:
                    dve.wait_ge(s_gain[gi], first_gain[gi])
                    for r in range(RT):
                        stt(o[:, r, :], x[:, r, :], small[:, 4 + r:5 + r], gain[:, gi, :], ALU.mult, ALU.mult).then_inc(S(name), 1)

            def turned(dst, b0, n0, done):
                for r in range(RT):
                    dve.wait_ge(S("pe_turned"), n0 + 2 * r + 1)
                    dve.tensor_copy(dst[:, 0:4, r * P:(r + 1) * P], bank[b0 + 2 * r].rearrange("p (q t) -> p q t", q=4)).then_inc(S(done), 1)

            rstd(0, [(hn, 0)], "dve_hn", (16, 16))
            dve.wait_ge(S("pe_par"), 1)
            step(dve.tensor_copy(par[:, :, :], bank[7][:, 0:KT * NR].rearrange("p (k n) -> p k n", k=KT)))
            ka = ROWS.index("k_a")
            step(dve.tensor_scalar(omk[:, :], par[:, :, ka], -1.0, 1.0, ALU.mult, ALU.add))
            turned(hT, 0, 0, "dve_turned")
            dve.wait_ge(S("dve_turned"), 2)
            dve.wait_ge(S("act_turned"), 2)
            dve.tensor_scalar(dT[:, :, 0:1], hT[:, :, 0:1], -1.0, None, ALU.mult)
            step(tt(dT[:, :, 1:T], hT[:, :, 0:T - 1], hT[:, :, 1:T], ALU.subtract))
            for i, dst, name in ((1, xs[0], "dve_xs"), (4, xs[1], "dve_xs"), (5, xs[2], "dve_xs"),
                                 (2, xk, "dve_mix"), (0, xr, "dve_mix"), (3, xv, "dve_mix")):
                for k in range(KT):
                    m = stt(dst[:, k, :], dT[:, k, :], par[:, k, i:i + 1], hT[:, k, :], ALU.mult, ALU.add)
                m.then_inc(S(name), 1)
            dve.wait_ge(S("dve_mix"), 3)
            dve.wait_ge(S("pe_lora"), 3)
            q.mark(dve.memset(work[:, 0:8 * 512], 0.0))
            step(dve.memset(Gs[:, :, 0:1], 0.0))

            def pgc(n, name):
                i = ROWS.index(name)
                return pg[:, n, i:i + 1]

            def v4(a):
                return a.rearrange("p (q t) -> p q t", q=4)

            def v8(a):
                return a.rearrange("p (u i) -> p u i", u=8)

            def flat(a):
                return a.rearrange("p n t -> p (n t)")

            def group(it):
                if True:
                    q.mark(dve.tensor_copy(pg[:, :, 0:NR], par[:, bass.ds(it * 2, 2), :]))
                    dve.tensor_copy(pg[:, :, NR:NR + 1].rearrange("p n o -> p (n o)"), omk[:, bass.ds(it * 2, 2)]).then_inc(S("dve_pg"), 1)
                    q.sync()
                    dve.wait_ge(S("dve_pg"), it + 1)
                dve.wait_ge(S("act_sz"), it + 1)
                for n in range(2):
                    for c in range(2):
                        m = dve.tensor_tensor_scan(Gs[:, 2 * n + c, 1:129], onec[:, :], sz[:, n, c * P:(c + 1) * P], 0.0, ALU.mult, ALU.add)
                step(m)
                step(tt(Gc[:, :, :], Gs[:, :, :], Gs[:, :, 64:65].broadcast_to([P, 4, 129]), ALU.subtract))
                g0 = Gc.rearrange("p (n c) t -> p n c t", n=2)
                g1 = Gs.rearrange("p (n c) t -> p n c t", n=2)
                tt(gsm[:, 0:2], g0[:, :, 0, 128], g1[:, :, 1, 64], ALU.add).then_inc(S("dve_G"), 1)
                dve.wait_ge(S("act_sa"), it + 1)
                for n in range(2):
                    m = dve.tensor_scalar(t1[:, n, :], sa[:, n, :], pgc(n, "k_a"), pg[:, n, NR:NR + 1], ALU.mult, ALU.add)
                step(m)
                dve.wait_ge(S("pe_k"), it + 1)
                dve.wait_ge(S("act_sq"), it + 1)
                step(tt(flat(kT_), bank[2], flat(t1), ALU.mult))
                dve.wait_ge(S("act_E"), it * 3 + 3)
                tt(v4(flat(kP)), v4(flat(kT_)), v4(En), ALU.mult)
                dve.wait_ge(S("pe_r"), it + 1)
                for n in range(2):
                    m = stt(rkr[:, n, :], bank[4][:, n * T:(n + 1) * T], pgc(n, "r_k"), kT_[:, n, :], ALU.mult, ALU.mult)
                m.then_inc(S("dve_rkr"), 1)
                arf = ar.rearrange("p n c m t -> p (n c) m t")
                tt(arf[:, :, 1, :], v4(bank[4]), E1[:, :, 1:129], ALU.mult)
                dve.wait_ge(S("pe_ss"), it + 1)
                dve.tensor_scalar(rn, bank[3], 1e-24, None, ALU.max).then_inc(S("dve_ssm"), 1)
                dve.wait_ge(S("act_nrm"), it + 1)
                step(dve.reciprocal(rn, nrm))
                step(tt(kn, flat(kkr), rn, ALU.mult))
                q.mark(tt(bb, kn, flat(sa), ALU.mult))
                stt(arf[:, :, 0, :], v4(kn), -1.0, E1[:, :, 0:128], ALU.mult, ALU.mult)
                q.sync()
                tt(flat(bP), bb, En, ALU.mult).then_inc(S("dve_scaled"), 1)
                dve.wait_ge(S("pe_bonus"), it + 1)
                dve.wait_ge(S("act_v"), it + 1)
                tt(bv, bank[7], vT, ALU.mult)
                for u in range(8):
                    dve.wait_ge(S("pe_mats"), it * 8 + (u + 1))
                    dve.memset(gsm[:, 48 + u:49 + u], 0.0)
                    dve.copy_predicated(M[:, u, :, :], trib[:, :, :], bank[2 + u % 4].rearrange("p (m t) -> p m t", m=4)).then_inc(S("dve_mats"), 1)
                idb = ident.rearrange("p (o t) -> p o t", o=1).broadcast_to([P, 4, P])
                for l in range(LEVELS):
                    for h in range(2):
                        dve.wait_ge(S("pe_X"), it * 14 + 2 * l + h + 1)
                        tt(Xs[:, 4 * h:4 * h + 4, :], bank[h].rearrange("p (u t) -> p u t", u=4),
                           levels[:, l:l + 1, :].broadcast_to([P, 4, P]), ALU.mult).then_inc(S("dve_X"), 1)
                    for h in range(2):
                        dve.wait_ge(S("pe_U"), it * 14 + 2 * l + h + 1)
                        tt(Us[:, 4 * h:4 * h + 4, :], bank[2 + h].rearrange("p (u t) -> p u t", u=4),
                           idb if l == 0 else Us[:, 4 * h:4 * h + 4, :], ALU.add).then_inc(S("dve_U"), 1)
                dve.wait_ge(S("pe_S"), it + 1)
                for n in range(2):
                    m = stt(St[:, n, :], bank[2][:, n * P:(n + 1) * P], gsm[:, 2 + n:3 + n], halves, ALU.mult, ALU.mult)
                m.then_inc(S("dve_S"), 1)
                dve.wait_ge(S("pe_o"), it + 1)
                step(dve.tensor_reduce(gsm[:, 8:16], v8(bank[3]), AX.X, ALU.add))
                step(dve.tensor_scalar(gsm[:, 16:24], gsm[:, 8:16], 1.0 / HD, None, ALU.mult))
                mu = gsm[:, 16:24].rearrange("p (u o) -> p u o", o=1).broadcast_to([P, 8, HD])
                tt(v8(oc), v8(bank[3]), mu, ALU.subtract).then_inc(S("dve_oc"), 1)
                dve.wait_ge(S("act_osq"), it + 1)
                step(dve.tensor_reduce(gsm[:, 24:32], v8(osq), AX.X, ALU.add))
                dve.tensor_scalar(gsm[:, 32:40], gsm[:, 24:32], 1.0 / HD, LNX_EPS, ALU.mult, ALU.add).then_inc(S("dve_var"), 1)
                dve.wait_ge(S("pool_ors"), it + 1)
                rs = gsm[:, 40:48].rearrange("p (u o) -> p u o", o=1).broadcast_to([P, 8, HD])
                tt(v8(on.rearrange("p c n i -> p (c n i)")), v8(oc), rs, ALU.mult).then_inc(S("dve_on"), 1)
                dve.wait_ge(S("pe_on"), it + 1)
                dve.wait_ge(S("act_g"), it + 1)
                for n in range(2):
                    m = dve.tensor_scalar(yT[:, n, :], bank[6][:, n * T:(n + 1) * T], pgc(n, "lnx_g"), pgc(n, "lnx_b"), ALU.mult, ALU.add)
                step(m)
                step(tt(flat(yT), flat(yT), bv, ALU.add))
                tt(flat(yT), flat(yT), gT, ALU.mult).then_inc(S("dve_y"), 1)
                for i in range(4):
                    dve.wait_ge(S("pe_wo"), it * 4 + i + 1)
                    xv_ = x[:, i // 2, (i % 2) * 512:(i % 2 + 1) * 512]
                    tt(xv_, bank[(0, 1, 2, 5)[i]], xv_, ALU.add).then_inc(S("dve_xadd"), 1)

            PER = 13
            with dve.Fori(0, NGRP) as it:
                q.start(it, PER)
                group(it)
            q.end(NGRP)

            def ffn(layer):
                base = layer * NF
                rstd((1, 3)[layer], [(fhn, (1, 0)[layer])], "dve_hn", ((16, 16), (48, 32))[layer])
                turned(fhT, 0, (4, 16)[layer], "dve_turned")
                with dve.Fori(0, NF // 2) as i:
                    for b in range(2):
                        dve.wait_ge(S("act_sg"), i * 2 + (base + b + 1))
                        tt(aT[:, b, :], sg[:, b, :], bank[4 + b][:, T:2 * T], ALU.mult).then_inc(S("dve_act"), 1)
                dve.wait_ge(S("pe_dn"), base + NF)
                for i in range(4):
                    xv_ = x[:, i // 2, (i % 2) * 512:(i % 2 + 1) * 512]
                    m = tt(xv_, bank[i], xv_, ALU.add)
                m.then_inc(S("dve_ffn"), 1)

            ffn(0)
            rstd(2, [(ahn, 0), (ahn2, 1)], "dve_ahn", (32, 32))
            turned(khT, 0, 8, "dve_aturned")
            turned(qhT, 4, 12, "dve_aturned")
            dve.wait_ge(s_qkg, 32)
            for w in range(2):
                for r in range(RT):
                    cosr = C("cos")[:, r * HD:(r + 1) * HD].rearrange("p (o d) -> p o d", o=1)
                    sinr = C("sin")[:, r * HD:(r + 1) * HD].rearrange("p (o d) -> p o d", o=1)
                    tt(rot[:, w, 0, r, :, :], qkg[:, w, :, :], cosr.broadcast_to([P, NG, HD]), ALU.mult)
                    for a, b in ((0, 32), (32, 0)):
                        m = tt(rot[:, w, 1, r, :, a:a + 32], qkg[:, w, :, b:b + 32],
                               sinr[:, :, a:a + 32].broadcast_to([P, NG, 32]), ALU.mult)
            m.then_inc(S("dve_rot"), 1)
            dve.wait_ge(S("dve_rot"), 1)

            def heads(p):
                for w in range(2):
                    for r in range(RT):
                        j = 2 * w + r
                        bk = bank[r][:, 0:384]
                        dve.wait_ge(S("act_asq"), p * 4 + j + 1)
                        dve.tensor_reduce(asm[:, 16:22], asq.rearrange("p (g d) -> p g d", g=6), AX.X, ALU.add).then_inc(S("dve_ass"), 1)
                        dve.wait_ge(S("dve_ass"), p * 4 + j + 1)
                        dve.tensor_scalar(asm[:, 24:30], asm[:, 16:22], 1.0 / HD, RMS_EPS, ALU.mult, ALU.add).then_inc(S("dve_av"), 1)
                        dve.wait_ge(S("pool_ars"), p * 4 + j + 1)
                        rs = asm[:, 32:38].rearrange("p (g o) -> p g o", o=1).broadcast_to([P, 6, HD])
                        tt(akn.rearrange("p g h d -> p (g h) d"), bk.rearrange("p (g d) -> p g d", g=6), rs, ALU.mult).then_inc(S("dve_kn"), 1)
                        dve.wait_ge(S("dve_kn"), p * 4 + j + 1)
                        cosb = rot[:, w, 0, r, :, :].rearrange("p g (o d) -> p g o d", o=1).broadcast_to([P, NG, 2, HD])
                        q.mark(tt(am1[:, :, :, :], akn[:, :, :, :], cosb, ALU.mult))
                        for a, b in ((0, 32), (32, 0)):
                            sinb = rot[:, w, 1, r, :, a:a + 32].rearrange("p g (o d) -> p g o d", o=1).broadcast_to([P, NG, 2, 32])
                            m = tt(am2[:, :, :, a:a + 32], akn[:, :, :, b:b + 32], sinb, ALU.mult)
                        step(m)
                        if w == 1:
                            dve.wait_ge(S("pe_qkT"), p * 4 + r + 1)
                        tt(akr[:, r, :], am1.rearrange("p g h d -> p (g h d)"), am2.rearrange("p g h d -> p (g h d)"), ALU.add).then_inc(S("dve_kr"), 1)
                for i in range(4):
                    r = i % 2
                    n = NG * (r + 1) * P
                    dve.wait_ge(S("pe_s"), p * 4 + i + 1)
                    if i >= 2:
                        dve.wait_ge(S("pe_pT"), p * 4 + i - 1)
                    dve.memset(asm[:, 48 + i:49 + i], 0.0)
                    src = bank[2][:, 0:n] if r == 0 else wide[:, 0:n]
                    dve.tensor_tensor_reduce(pr[:, i % 2, 0:n], src, C(f"mask{r}"), 1.0, 3.0 * NEG, ALU.add, ALU.max,
                                             asm[:, i:i + 1]).then_inc(S("dve_sm"), 1)
                    dve.wait_ge(S("dve_sm"), p * 4 + i + 1)
                    dve.tensor_scalar(asm[:, 4 + i:5 + i], asm[:, i:i + 1], -SCALE, None, ALU.mult).then_inc(S("dve_nm"), 1)
                dve.wait_ge(S("act_p"), p * 4 + 4)
                dve.reciprocal(asm[:, 12:16], asm[:, 8:12]).then_inc(S("dve_rden"), 1)

            with dve.Fori(0, KT) as p:
                q.start(p, 8)
                heads(p)
            q.end(KT)
            for i in range(4):
                dve.wait_ge(S("pe_awo"), i + 1)
                xv_ = x[:, i // 2, (i % 2) * 512:(i % 2 + 1) * 512]
                tt(xv_, bank[i], xv_, ALU.add).then_inc(S("dve_awo"), 1)
            ffn(1)

        @block.gpsimd
        def _(pool):
            pool.wait_ge(S("dve_mhalf"), 1)

            def root(dst, src, n):
                return pool.tensor_tensor(dst, src, mhalf[:, 0:n], ALU.pow)

            def norm_root(n):
                pool.wait_ge(S("dve_ms"), n + 1)
                root(small[:, 4:6], small[:, 2:4], 2).then_inc(S("pool_rs"), 1)

            norm_root(0)
            with pool.Fori(0, NGRP) as it:
                pool.wait_ge(S("dve_var"), it + 1)
                root(gsm[:, 40:48], gsm[:, 32:40], 8).then_inc(S("pool_ors"), 1)
            norm_root(1)
            norm_root(2)
            with pool.Fori(0, KT) as p:
                for j in range(4):
                    pool.wait_ge(S("dve_av"), p * 4 + j + 1)
                    root(asm[:, 32:38], asm[:, 24:30], 6).then_inc(S("pool_ars"), 1)
            norm_root(3)


INS = ["x", "a_norm_g", "a_mu", "a_w_r", "a_w_k", "a_w_v", "a_w0", "a_w1", "a_w2", "a_a0", "a_a1", "a_a2",
       "a_g1", "a_g2", "a_k_k", "a_k_a", "a_r_k", "a_lnx_g", "a_lnx_b", "a_w_o", "kv_norm_g", "w_kv", "k_norm_g",
       "b_norm_g", "b_w_q", "b_q_norm_g", "b_w_o", "f_norm_g", "f_w_gu", "f_w_down"]


def kernel(**inputs):
    import concourse.bacc as bacc
    from concourse.bass_utils import run_bass_kernel_spmd

    nc = bacc.Bacc("TRN2", target_bir_lowering=False, num_devices=1)
    arrays, args = {}, {}
    table = np.concatenate([CONSTS[n] for n in CAT], 1)
    for name in INS + ["const"]:
        a = table if name == "const" else np.ascontiguousarray(inputs[name])
        arrays[f"in_{name}"] = a
        args[name] = nc.dram_tensor(f"in_{name}", a.shape, mybir.dt.from_np(a.dtype), kind="ExternalInput").ap()
    out = nc.dram_tensor("out", (1, T, D), F32, kind="ExternalOutput").ap()
    program(nc, args, out)
    r = run_bass_kernel_spmd(nc, [arrays], core_ids=[0])
    return r.results[0]["out"]
```

```python
import math

import numpy as np
import concourse.bass as bass
from concourse import mybir
from contextlib import ExitStack

F32 = mybir.dt.float32
I32 = mybir.dt.int32
F32R = mybir.dt.float32r
ALU = mybir.AluOpType
ACT = mybir.ActivationFunctionType
AX = mybir.AxisListType

P = 128
D, T = 1024, 256
KT, RT = D // P, T // P
HD, NH = 64, D // 64
LW, LG = 64, 160
FF = -(-8 * D // (3 * 256)) * 256
NF = FF // P
GROUPS = ((128, 1), (512, 4), (2048, 16))
NG = len(GROUPS)
QW = NG * D
KAPPA = math.exp(-0.5)
RMS_EPS, LNX_EPS = 1e-6, 64e-5
LEVELS = 7
NEG = -1e30
SCALE = HD ** -0.5

ROWS = ["mu0", "mu1", "mu2", "mu3", "mu4", "mu5", "w0", "a0", "k_k", "k_a", "r_k", "lnx_g", "lnx_b"]
NR = len(ROWS)


def constants():
    p = np.arange(P)[:, None]
    f = np.arange(P)[None, :]
    out = {"ident": (p == f).astype(np.float32)}
    out["halves"] = (p // HD == f // HD).astype(np.float32)
    strict, incl = (p < f), (p <= f)
    out["tri"] = np.concatenate([strict, incl, strict, incl], 1).astype(np.float32)
    lev = []
    for l in range(LEVELS):
        m = 1 << l
        lev.append(((p // (2 * m) == f // (2 * m)) & (p // m % 2 == 1) & (f // m % 2 == 0)).astype(np.float32))
    lev[0] = lev[0].T
    out["levels"] = np.concatenate(lev, 1)
    for r in range(RT):
        t = p + r * P
        s = np.arange((r + 1) * P)[None, :]
        parts = []
        for window, dil in GROUPS:
            ok = (t >= s) & ((t - s) % dil == 0) & (t - s <= window)
            parts.append(np.where(ok, 0.0, NEG).astype(np.float32))
        out[f"mask{r}"] = np.concatenate(parts, 1)
    inv = (10000.0 ** (-np.arange(0, HD, 2, dtype=np.float32) / HD)).astype(np.float32)
    ang = np.arange(T, dtype=np.float32)[:, None] * inv[None, :]
    cos, sin = np.cos(ang).astype(np.float32), np.sin(ang).astype(np.float32)
    c = np.concatenate([cos, cos], 1).reshape(RT, P, HD)
    s = np.concatenate([-sin, sin], 1).reshape(RT, P, HD)
    out["cos"] = np.concatenate([c[r] for r in range(RT)], 1)
    out["sin"] = np.concatenate([s[r] for r in range(RT)], 1)
    return out


CONSTS = constants()
CAT = {}
_at = 0
for _n, _v in CONSTS.items():
    CAT[_n] = (_at, _v.shape[1])
    _at += _v.shape[1]
NCONST = _at


def program(nc, ins, out):
    ctx = ExitStack()
    with ctx:
        def sb(name, shape, dt=F32):
            return ctx.enter_context(nc.sbuf_tensor(name, shape, dt))

        def sem(name):
            return ctx.enter_context(nc.semaphore(name))

        x = sb("x", [P, RT, D])
        cst = sb("cst", [P, NCONST])
        trib = sb("trib", [P, 4, P], I32)
        gain = sb("gain", [P, 2, D])
        rows = sb("rows", [NR, D])
        par = sb("par", [P, KT, NR])
        omk = sb("omk", [P, KT])
        onec = sb("onec", [P, P])
        mhalf = sb("mhalf", [P, 16])
        small = sb("small", [P, 64])
        ring = sb("ring", [P, 6144])
        wmix = sb("wmix", [P, 4, KT * 256])
        WORK = 28000
        pg = sb("pg", [P, 2, NR + 1])
        pl = sb("pl", [P, 2, 2])
        w2s = sb("w2s", [LW, 256])
        a2s = sb("a2s", [LW, 256])
        g2s = sb("g2s", [P, 2, 256])
        gsm = sb("gsm", [P, 64])
        first = ExitStack()
        work = first.enter_context(nc.sbuf_tensor("work", [P, WORK], F32))

        def C(name):
            a, n = CAT[name]
            return cst[:, a:a + n]

        ident, halves = C("ident"), C("halves")

        class Carve:
            def __init__(self, at=0):
                self.at = at

            def take(self, size, pattern=None, **k):
                v = work[:, self.at:self.at + size]
                self.at += size
                assert self.at <= WORK, self.at
                return v.rearrange(pattern, **k) if pattern else v

        bank = [ctx.enter_context(nc.psum_tensor(f"bank{i}", [P, 512], F32)) for i in range(3)]
        wide = ctx.enter_context(nc.psum_tensor("wide", [P, 1024], F32))
        bank += [wide[:, 0:512], wide[:, 512:1024]]
        bank += [ctx.enter_context(nc.psum_tensor(f"bank{i}", [P, 512], F32)) for i in range(5, 8)]
        bank = [b[:, :] for b in bank]

        names = {}

        def S(name):
            if name not in names:
                names[name] = sem(name)
            return names[name]

        cv = Carve()
        hT = cv.take(KT * T, "p (k t) -> p k t", k=KT)
        dT = cv.take(KT * T, "p (k t) -> p k t", k=KT)
        M = work[:, 0:8 * 512].rearrange("p (u m t) -> p u m t", u=8, m=4)
        xr, xk, xv = (cv.take(KT * T, "p (k t) -> p k t", k=KT) for _ in range(3))
        tw = cv.take(T)
        ta = cv.take(T)
        tg = cv.take(2 * T, "p (k t) -> p k t", k=2)
        gat = cv.at
        xs = [cv.take(KT * T, "p (k t) -> p k t", k=KT) for _ in range(3)]
        hn = cv.take(RT * D, "p (r d) -> p r d", r=RT)
        w1s = cv.take(KT * LW, "p (k n) -> p k n", k=KT)
        a1s = cv.take(KT * LW, "p (k n) -> p k n", k=KT)
        g1s = cv.take(KT * LG, "p (k n) -> p k n", k=KT)
        cg = Carve(gat)
        n4 = dict(n=2, c=2)
        Us = cg.take(8 * P, "p (u t) -> p u t", u=8)
        Ts = cg.take(8 * P, "p (u t) -> p u t", u=8)
        Xs = cg.take(8 * P, "p (u t) -> p u t", u=8)
        ar = cg.take(8 * P, "p (n c m t) -> p n c m t", n=2, c=2, m=2)
        sz = cg.take(512, "p (n t) -> p n t", n=2)
        sa = cg.take(512, "p (n t) -> p n t", n=2)
        Gs = cg.take(4 * 129, "p (q t) -> p q t", q=4)
        Gc = cg.take(4 * 129, "p (q t) -> p q t", q=4)
        E1 = cg.take(4 * 129, "p (q t) -> p q t", q=4)
        En = sz.rearrange("p n t -> p (n t)")
        over_X = Xs.rearrange("p u t -> p (u t)")
        kkr = over_X[:, 0:512].rearrange("p (n t) -> p n t", n=2)
        sq = cg.take(512, "p (n t) -> p n t", n=2)
        nrm = cg.take(512)
        rn = over_X[:, 512:1024]
        kn = cg.take(512)
        t1 = cg.take(512, "p (n t) -> p n t", n=2)
        kT_ = cg.take(512, "p (n t) -> p n t", n=2)
        rkr = cg.take(512, "p (n t) -> p n t", n=2)
        bb = sq.rearrange("p n t -> p (n t)")
        kP = cg.take(512, "p (n t) -> p n t", n=2)
        bP = cg.take(512, "p (n t) -> p n t", n=2)
        vT = cg.take(512)
        gT = cg.take(512)
        bv = nrm
        Vn = cg.take(512, "p (c n i) -> p c n i", c=2, n=2)
        kPn = cg.take(256, "p (n i) -> p n i", n=2)
        bPn = cg.take(256, "p (n i) -> p n i", n=2)
        Zs = cg.take(256)
        UUs = cg.take(512, "p (c n i) -> p c n i", c=2, n=2)
        St = cg.take(256, "p (n i) -> p n i", n=2)
        oc = kkr.rearrange("p n t -> p (n t)")
        osq = kn
        on = cg.take(512, "p (c n i) -> p c n i", c=2, n=2)
        yT = cg.take(512, "p (n t) -> p n t", n=2)
        scratch0 = work[:, WORK - D:WORK]
        levels = C("levels").rearrange("p (l t) -> p l t", l=LEVELS)
        NGRP = D // 256
        WO_BANKS = (5, 0, 1, 7)

        first.close()
        second = ExitStack()

        def sb2(name, shape, dt=F32):
            return second.enter_context(nc.sbuf_tensor(name, shape, dt))

        wsp = sb2("wsp", [P, 2, 2, 3072], F32R)
        hsp = sb2("hsp", [P, 2, KT * T], F32R)
        asp = sb2("asp", [P, 2, 2, T], F32R)
        fhn = sb2("fhn", [P, RT, D])
        sg = sb2("sg", [P, 2, T])
        am = sb2("am", [P, T])
        squared = sb2("squared", [P, D])
        PASSES = ((0, 0), (0, 1), (1, 0))
        gus = [wsp[:, b, :, 0:2048].rearrange("p s (k m n) -> p s k m n", k=KT, m=2) for b in range(2)]
        dns = [wsp[:, b, :, 2048:3072] for b in range(2)]
        raw = [ring[:, b * 3072:(b + 1) * 3072] for b in range(2)]
        hparts = hsp[:, :, :].rearrange("p s (k t) -> p s k t", k=KT)

        second.close()

        def sbv(name, shape):
            h = sb(name, shape)
            return h[tuple(slice(0, n) for n in shape)]

        hkq = ctx.enter_context(nc.sbuf_tensor("hkq", [P, 2, 2, KT * T], F32R))
        kparts, qparts = (hkq[:, w, :, :].rearrange("p s (k t) -> p s k t", k=KT) for w in range(2))
        HALF = KT // 2 * NG * P
        UNITS, RAWS = 6, 3
        wpj = ctx.enter_context(nc.sbuf_tensor("wpj", [P, 2, 2, HALF], F32R))
        rawh = [ring[:, i * HALF:(i + 1) * HALF] for i in range(RAWS)]
        rot = sbv("rot", [P, 2, 2, RT, NG, HD])
        qkg = sbv("qkg", [P, 2, NG, HD])
        asq = sbv("asq", [P, 384])
        akn, am1, am2 = (sbv(n, [P, NG, 2, HD]) for n in ("akn", "am1", "am2"))
        once = sbv("once", [P, 4608])
        ahn, ahn2 = (once[:, w * RT * D:(w + 1) * RT * D].rearrange("p (r d) -> p r d", r=RT) for w in range(2))
        akr = once[:, 0:1536].rearrange("p (j n) -> p j n", j=4)
        pr, pT = (once[:, 1536 * (i + 1):1536 * (i + 2)].rearrange("p (b n) -> p b n", b=2) for i in range(2))
        kTt, qTt = (sbv(n, [P, NG, T]) for n in ("kTt", "qTt"))
        Vs = sbv("Vs", [P, RT, 384])
        ao = sbv("ao", [P, RT, P])
        oT = sbv("oT", [P, KT, T])
        asm = gsm
        wo_v = wmix[:, :, :].rearrange("p a (b n) -> p (a b) n", n=D)

        s_ident, s_const, s_x, s_rows, s_lora = S("ident_loaded"), S("const_loaded"), S("x_loaded"), S("rows_loaded"), S("lora_loaded")
        s_gain = [S("gain0_loaded"), S("gain1_loaded")]
        s_wm = [S(f"wmix{i}_loaded") for i in range(4)]
        s_l2 = S("lora2_loaded")
        s_gu = [S(f"gate_up{i}_loaded") for i in range(2)]
        s_dn = [S(f"down{i}_loaded") for i in range(2)]
        s_raw = [S(f"projection_weights{i}_loaded") for i in range(RAWS)]
        s_wo, s_qkg, s_out = S("wo_loaded"), S("qk_gains_loaded"), S("stored")

        block = ctx.enter_context(nc.Block())

        @block.sync
        def _(sp):
            sp.dma_start(x[:, :, :], ins["x"][0].rearrange("(r p) d -> p r d", p=P)).then_inc(s_x, 16)

            def load_gain(i, src):
                sp.dma_start(gain[:, i, :], src.partition_broadcast(P)).then_inc(s_gain[i], 16)

            sp.dma_start(ident, ins["const"][:, 0:P]).then_inc(s_ident, 16)
            load_gain(0, ins["a_norm_g"][0])
            sp.dma_start(rows[:, :], ins["rows"]).then_inc(s_rows, 16)
            for dst, n in ((w1s, "a_w1"), (a1s, "a_a1"), (g1s, "a_g1")):
                sp.dma_start(dst, ins[n][0].rearrange("(k p) n -> p k n", p=P)).then_inc(s_lora, 16)

            cols = [ins[n][0].rearrange("(k p) n -> p k n", p=P) for n in ("a_w_r", "a_w_k", "a_w_v")]
            wo_rows = ins["a_w_o"][0].rearrange("(g n p) d -> g p n d", p=P, n=2)

            def load_mix(it):
                for i, free in ((1, "pe_k"), (0, "pe_r"), (2, "pe_v")):
                    if it is not None:
                        sp.wait_ge(S(free), it)
                    c0 = 0 if it is None else it * 256
                    sp.dma_start(wmix[:, i, :].rearrange("p (k n) -> p k n", k=KT),
                                 cols[i][:, :, bass.ds(c0, 256)]).then_inc(s_wm[i], 16)
                    if it is None and i == 1:
                        sp.dma_start(cst[:, P:NCONST], ins["const"][:, P:NCONST]).then_inc(s_const, 16)
                if it is not None:
                    sp.wait_ge(S("pe_z"), it * 2)
                    sp.wait_ge(S("pe_g"), it)
                c0 = 0 if it is None else it * 256
                sp.dma_start(w2s[:, :], ins["a_w2"][0][:, bass.ds(c0, 256)]).then_inc(s_l2, 16)
                sp.dma_start(a2s[:, :], ins["a_a2"][0][:, bass.ds(c0, 256)]).then_inc(s_l2, 16)
                sp.dma_start(g2s[:, 0, :], ins["a_g2"][0][0:P, bass.ds(c0, 256)]).then_inc(s_l2, 16)
                sp.dma_start(g2s[0:LG - P, 1, :], ins["a_g2"][0][P:LG, bass.ds(c0, 256)]).then_inc(s_l2, 16)
                if it is not None:
                    sp.wait_ge(S("pe_wo"), it * 4)
                sp.dma_start(wmix[:, 3, :].rearrange("p (n d) -> p n d", n=2),
                             wo_rows[0 if it is None else bass.ds(it, 1)] if it is None
                             else wo_rows[bass.ds(it, 1)].rearrange("a p n d -> p (a n) d")).then_inc(s_wm[3], 16)

            load_mix(None)
            load_gain(1, ins["f_norm_g"][0])
            with sp.Fori(1, NGRP) as it:
                load_mix(it)

            def load_ffn(layer, f, b, n, first):
                gu = ins["f_w_gu"][layer].rearrange("(k p) (m n) -> p m k n", p=P, m=2)
                if not first:
                    sp.wait_ge(S("dve_gu_lo"), n)
                for m in range(2):
                    sp.dma_start(raw[b][:, 0:2048].rearrange("p (k m n) -> p k m n", k=KT, m=2)[:, :, m, :],
                                 gu[:, m, :, bass.ds(f * P, P)]).then_inc(s_gu[b], 16)
                if not first:
                    sp.wait_ge(S("dve_dn_lo"), n)
                sp.dma_start(raw[b][:, 2048:3072], ins["f_w_down"][layer][bass.ds(f * P, P), :]).then_inc(s_dn[b], 16)

            def ffn(layer):
                base = layer * NF
                for b in range(2):
                    load_ffn(layer, b, b, None, True)
                with sp.Fori(1, NF // 2) as i:
                    for b in range(2):
                        done = i * 2 + (base + b - 1)
                        load_ffn(layer, i * 2 + b, b, done, False)

            ffn(0)
            sp.wait_ge(S("dve_hn"), 2 * RT)
            load_gain(0, ins["kv_norm_g"])
            load_gain(1, ins["b_norm_g"][0])
            kvw = ins["w_kv"].rearrange("(k p) (m g n) -> p m k g n", p=P, m=2, g=NG)
            qw = ins["b_w_q"][0].rearrange("(k p) (g n) -> p k g n", p=P, g=NG)
            srcs = [kvw[:, 0], qw, kvw[:, 1]]

            def load_half(p, u, fresh):
                if not fresh:
                    sp.wait_ge(S("dve_w_lo"), p * UNITS + (u + 1 - RAWS))
                c0 = p * P
                k0 = u % 2 * (KT // 2)
                for g in range(NG):
                    sp.dma_start(rawh[u % RAWS].rearrange("p (k g n) -> p k g n", g=NG, n=P)[:, :, g, :],
                                 srcs[u // 2][:, k0:k0 + KT // 2, g, bass.ds(c0, P)]).then_inc(s_raw[u % RAWS], 16)

            sp.wait_ge(S("dve_gu_lo"), NF)
            sp.wait_ge(S("dve_dn_lo"), NF)
            for u in range(RAWS):
                load_half(0, u, True)
            sp.wait_ge(S("dve_ffn"), 4)
            for w, n in ((0, "k_norm_g"), (1, "b_q_norm_g")):
                src = ins[n] if w == 0 else ins[n][0]
                sp.dma_start(qkg[:, w], src.partition_broadcast(P)).then_inc(s_qkg, 16)
            for u in range(RAWS, UNITS):
                load_half(0, u, False)
            sp.dma_start(wo_v, ins["b_w_o"][0].rearrange("(k p) d -> p k d", p=P)).then_inc(s_wo, 16)
            with sp.Fori(1, KT) as p:
                for u in range(UNITS):
                    load_half(p, u, False)
            sp.wait_ge(S("dve_ahn"), 2 * RT)
            load_gain(0, ins["f_norm_g"][1])
            sp.wait_ge(S("dve_w_lo"), KT * UNITS)
            ffn(1)
            for r in range(RT):
                sp.wait_ge(S("dve_ffn"), 4 + 2 * (r + 1))
                sp.dma_start(out[0][r * P:(r + 1) * P, :], x[:, r, :]).then_inc(s_out, 16)
            sp.wait_ge(s_out, 16 * RT)

        @block.tensor
        def _(pe):
            def mm(o, a, b, start=True, stop=True):
                return pe.matmul(o, a, b, start=start, stop=stop)

            def turn_rows(src, n0):
                for r in range(RT):
                    pe.wait_ge(S(src[1]), n0 + r + 1)
                    for j in range(2):
                        for q in range(4):
                            k = 4 * j + q
                            m = pe.transpose(bank[2 * r + j][:, q * P:(q + 1) * P], src[0][:, r, k * P:(k + 1) * P], ident)
                        m.then_inc(S("pe_turned"), 1)

            pe.wait_ge(s_ident, 16)
            pe.wait_ge(s_rows, 16)
            for k in range(KT):
                m = pe.transpose(bank[7][:, k * NR:(k + 1) * NR], rows[0:NR, k * P:(k + 1) * P], ident[0:NR, 0:NR])
            m.then_inc(S("pe_par"), 1)
            turn_rows((hn, "dve_hn"), 0)
            pe.wait_ge(s_lora, 48)
            pe.wait_ge(S("act_turned"), 2)
            pe.wait_ge(S("dve_turned"), 2)
            pe.wait_ge(S("dve_xs"), 1)
            for k in range(KT):
                m = mm(bank[0][0:LW, 0:T], w1s[:, k, :], xs[0][:, k, :], k == 0, k == KT - 1)
            m.then_inc(S("pe_lora"), 1)
            pe.wait_ge(S("dve_xs"), 2)
            for k in range(KT):
                m = mm(bank[1][0:LW, 0:T], a1s[:, k, :], xs[1][:, k, :], k == 0, k == KT - 1)
            m.then_inc(S("pe_lora"), 1)
            pe.wait_ge(S("dve_xs"), 3)
            for k in range(KT):
                mm(bank[2][:, 0:T], g1s[:, k, 0:P], xs[2][:, k, :], k == 0, k == KT - 1)
            for k in range(KT):
                m = mm(bank[3][0:LG - P, 0:T], g1s[:, k, P:LG], xs[2][:, k, :], k == 0, k == KT - 1)
            m.then_inc(S("pe_lora"), 1)

            def project(b, i, src, name):
                for n in range(2):
                    for k in range(KT):
                        w = wmix[:, i, :].rearrange("p (k n) -> p k n", k=KT)[:, k, n * P:(n + 1) * P]
                        m = mm(bank[b][:, n * T:(n + 1) * T], w, src[:, k, :], k == 0, k == KT - 1)
                m.then_inc(S(name), 1)

            def unit(nn, h):
                return 2 * nn + h

            def turn_output(it):
                pe.wait_ge(S("dve_on"), it)
                for n in range(2):
                    for c in range(2):
                        m = pe.transpose(bank[6][:, (2 * n + c) * P:(2 * n + c + 1) * P], on[:, c, n, :], ident)
                m.then_inc(S("pe_on"), 1)

            def product_o(it):
                pe.wait_ge(S("dve_y"), it)
                pe.wait_ge(s_wm[3], it * 16)
                for r in range(RT):
                    for j in range(2):
                        for n in range(2):
                            w = wmix[:, 3, :].rearrange("p (n d) -> p n d", n=2)[:, n, j * 512:(j + 1) * 512]
                            m = mm(bank[WO_BANKS[2 * r + j]], yT[:, n, r * P:(r + 1) * P], w, n == 0, n == 1)
                        m.then_inc(S("pe_wo"), 1)

            def group(it, behind=True):
                pe.wait_ge(s_l2, it * 64 + 64)
                for n in range(2):
                    m = mm(bank[0][:, n * T:(n + 1) * T], w2s[:, n * P:(n + 1) * P], tw[0:LW, :])
                m.then_inc(S("pe_z"), 1)
                for n in range(2):
                    m = mm(bank[1][:, n * T:(n + 1) * T], a2s[:, n * P:(n + 1) * P], ta[0:LW, :])
                m.then_inc(S("pe_z"), 1)
                pe.wait_ge(s_wm[1], it * 16 + 16)
                project(2, 1, xk, "pe_k")
                if behind:
                    turn_output(it)
                pe.wait_ge(s_wm[0], it * 16 + 16)
                project(4, 0, xr, "pe_r")
                if behind:
                    pe.wait_ge(S("act_sa"), it + 1)
                    product_o(it)
                pe.wait_ge(S("act_sq"), it + 1)
                mm(bank[3], halves, sq.rearrange("p n t -> p (n t)")).then_inc(S("pe_ss"), 1)
                for n in range(2):
                    mm(bank[6][:, n * T:(n + 1) * T], g2s[:, 0, n * P:(n + 1) * P], tg[:, 0, :], True, False)
                    m = mm(bank[6][:, n * T:(n + 1) * T], g2s[0:LG - P, 1, n * P:(n + 1) * P], tg[0:LG - P, 1, :], False, True)
                m.then_inc(S("pe_g"), 1)
                pe.wait_ge(s_wm[2], it * 16 + 16)
                if behind:
                    pe.wait_ge(S("dve_xadd"), it * 4)
                project(5, 2, xv, "pe_v")
                pe.wait_ge(S("dve_rkr"), it + 1)
                mm(bank[7], halves, rkr.rearrange("p n t -> p (n t)")).then_inc(S("pe_bonus"), 1)
                pe.wait_ge(S("act_v"), it + 1)
                for c in range(2):
                    for n in range(2):
                        m = pe.transpose(bank[0][:, (2 * c + n) * P:(2 * c + n + 1) * P],
                                         vT[:, n * T + c * P:n * T + (c + 1) * P], ident)
                m.then_inc(S("pe_tv"), 1)
                pe.wait_ge(S("dve_scaled"), it + 1)
                for j, src in enumerate((kP, bP)):
                    for n in range(2):
                        m = pe.transpose(bank[1][:, (2 * j + n) * P:(2 * j + n + 1) * P], src[:, n, 0:P], ident)
                m.then_inc(S("pe_tk"), 1)

                for c in range(2):
                    for nn in range(2):
                        for h in range(2):
                            u = 4 * c + 2 * nn + h
                            if u >= 4:
                                pe.wait_ge(S("dve_mats"), it * 8 + u - 3)
                            b = bank[2 + u % 4]
                            hp = slice(h * HD, (h + 1) * HD)
                            rhs = ar[hp, nn, c, :, :].rearrange("p m t -> p (m t)")
                            mm(b[:, 0:256], bP[hp, nn, c * P:(c + 1) * P], rhs)
                            m = mm(b[:, 256:512], kP[hp, nn, c * P:(c + 1) * P], rhs)
                            m.then_inc(S("pe_mats"), 1)
                pe.wait_ge(S("act_vn"), it + 1)
                pe.wait_ge(S("dve_mats"), it * 8 + 4)
                pe.wait_ge(S("act_g"), it + 1)
                for u in range(4):
                    m = mm(bank[6][:, u * HD:(u + 1) * HD], M[:, u, 2, :], Vn[:, 0, u // 2, (u % 2) * HD:(u % 2 + 1) * HD])
                m.then_inc(S("pe_z0"), 1)

                for l in range(LEVELS):
                    for q in range(2) if l else ():
                        pe.wait_ge(S("act_T"), it * 12 + 2 * l + q - 1)
                        if l == 1:
                            pe.wait_ge(S("act_vn"), it + 1)
                            pe.wait_ge(S("act_kn"), it + 1)
                        for j in range(4):
                            u = 4 * q + j
                            m = mm(bank[q][:, j * P:(j + 1) * P], M[:, u, 0, :], Ts[:, u, :])
                        m.then_inc(S("pe_X"), 1)
                    for q in range(2) if l else ():
                        pe.wait_ge(S("dve_X"), it * 12 + 2 * l + q - 1)
                        for j in range(4):
                            u = 4 * q + j
                            m = mm(bank[2 + q][:, j * P:(j + 1) * P], Xs[:, u, :], Us[:, u, :])
                        m.then_inc(S("pe_U"), 1)
                    for q in range(2):
                        pe.wait_ge(S("dve_U"), it * 14 + 2 * l + q + 1)
                        if l == 0:
                            pe.wait_ge(S("dve_mats"), it * 8 + 8)
                        if l < LEVELS - 1:
                            for j in range(4):
                                u = 4 * q + j
                                m = pe.transpose(bank[4 + q][:, j * P:(j + 1) * P], Us[:, u, :], ident)
                            m.then_inc(S("pe_T"), 1)

                def hcols(v, u):
                    return v[:, u * HD:(u + 1) * HD]

                pe.wait_ge(S("act_z"), it * 2 + 1)
                for u in range(4):
                    m = mm(hcols(bank[1], u), Us[:, u, :], hcols(Zs, u))
                m.then_inc(S("pe_uu"), 1)
                pe.wait_ge(S("act_uu"), it * 2 + 1)
                for n in range(2):
                    mm(bank[2][:, n * P:(n + 1) * P], kPn[:, n, :], Vn[:, 0, n, :], True, False)
                    m = mm(bank[2][:, n * P:(n + 1) * P], bPn[:, n, :], UUs[:, 0, n, :], False, True)
                m.then_inc(S("pe_S"), 1)
                for u in range(4):
                    hh = slice((u % 2) * HD, (u % 2 + 1) * HD)
                    mm(hcols(bank[3], u), M[:, u, 3, :], Vn[:, 0, u // 2, hh], True, False)
                    mm(hcols(bank[3], u), M[:, u, 1, :], UUs[:, 0, u // 2, hh], False, True)
                pe.wait_ge(S("dve_S"), it + 1)
                for n in range(2):
                    mm(bank[4][:, n * P:(n + 1) * P], ar[:, n, 1, 0, :], St[:, n, :], True, False)
                    for h in range(2):
                        u = 2 * n + h
                        m = mm(hcols(bank[4], u), M[:, 4 + u, 2, :], Vn[:, 1, n, h * HD:(h + 1) * HD], False, h == 1)
                m.then_inc(S("pe_z1"), 1)
                pe.wait_ge(S("act_z"), it * 2 + 2)
                for u in range(4):
                    m = mm(hcols(bank[5], u), Us[:, 4 + u, :], hcols(Zs, u))
                m.then_inc(S("pe_uu"), 1)
                pe.wait_ge(S("act_uu"), it * 2 + 2)
                for n in range(2):
                    mm(bank[3][:, 256 + n * P:256 + (n + 1) * P], ar[:, n, 1, 1, :], St[:, n, :], True, False)
                    for h in range(2):
                        u = 2 * n + h
                        hh = slice(h * HD, (h + 1) * HD)
                        o = bank[3][:, 256 + u * HD:256 + (u + 1) * HD]
                        mm(o, M[:, 4 + u, 3, :], Vn[:, 1, n, hh], False, False)
                        m = mm(o, M[:, 4 + u, 1, :], UUs[:, 1, n, hh], False, h == 1)
                m.then_inc(S("pe_o"), 1)

            pe.wait_ge(S("act_lora"), 4)
            pe.wait_ge(S("dve_mix"), 3)
            pe.wait_ge(s_const, 16)
            group(0, behind=False)
            with pe.Fori(1, NGRP) as it:
                group(it)
            turn_output(NGRP)
            product_o(NGRP)

            def ffn(layer):
                base = layer * NF
                turn_rows((fhn, "dve_hn"), RT * (1 + layer))
                pe.wait_ge(S("dve_hsp"), 4 * (layer + 1))

                def gate_up(f, b, b_free=True):
                    pe.wait_ge(S("dve_gu_lo"), f + (base + 1))
                    if b_free:
                        pe.wait_ge(S("dve_act"), f + (base - 1))
                    for m_ in range(2):
                        o = bank[4 + b][:, m_ * T:(m_ + 1) * T]
                        for k in range(KT):
                            for n, (sw, sh) in enumerate(PASSES):
                                m = mm(o, gus[b][:, sw, k, m_, :], hparts[:, sh, k, :],
                                       k == 0 and n == 0, k == KT - 1 and n == 2)
                    m.then_inc(S("pe_gu"), 1)

                def down(f, b, first=False, last=False):
                    pe.wait_ge(S("dve_act"), f + (base + 1))
                    pe.wait_ge(S("dve_dn_lo"), f + (base + 1))
                    for r in range(RT):
                        for j in range(2):
                            for n, (sa_, sw) in enumerate(PASSES):
                                m = mm(bank[2 * r + j], asp[:, b, sa_, r * P:(r + 1) * P],
                                       dns[b][:, sw, j * 512:(j + 1) * 512], first and n == 0, last and n == 2)
                            if last:
                                m.then_inc(S("pe_sums"), 1)
                    if not last:
                        m.then_inc(S("pe_dn"), 1)

                gate_up(0, 0, False)
                gate_up(1, 1, False)
                down(0, 0, first=True)
                gate_up(2, 0)
                down(1, 1)
                with pe.Fori(1, NF // 2 - 1) as i:
                    gate_up(2 * i + 1, 1)
                    down(2 * i, 0)
                    gate_up(2 * i + 2, 0)
                    down(2 * i + 1, 1)
                f = NF - 2
                gate_up(f + 1, 1)
                down(f, 0)
                down(f + 1, 1, last=True)

            ffn(0)

            pe.wait_ge(S("dve_ffn"), 4)
            turn_rows((ahn, "dve_ahn"), 0)
            for r in range(RT):
                pe.wait_ge(S("dve_ahn"), RT + r + 1)
                for j in range(2):
                    for q in range(4):
                        k = 4 * j + q
                        m = pe.transpose(bank[4 + 2 * r + j][:, q * P:(q + 1) * P], ahn2[:, r, k * P:(k + 1) * P], ident)
                    m.then_inc(S("pe_turned"), 1)
            pe.wait_ge(S("dve_aturned"), 4)

            def heads(p, b):
                def project_half(u, tiles=range(RT)):
                    what, h = u // 2, u % 2
                    pe.wait_ge(S("dve_w_lo"), p * UNITS + (u + 1))
                    if u == 2 and b is None:
                        pe.wait_ge(S("dve_aturned"), 8)
                    src = qparts if what == 1 else kparts
                    for r in tiles:
                        if h == 0:
                            if what > 0:
                                pe.wait_ge(S("act_raw"), p * 4 + (2 * what - 1 + r))
                            elif b is not None:
                                pe.wait_ge(S("act_Vs"), b * 2 + (r + 1))
                        for k in range(KT // 2):
                            for n, (sh, sw) in enumerate(PASSES):
                                m = mm(bank[r][:, 0:384], src[:, sh, h * (KT // 2) + k, r * P:(r + 1) * P],
                                       wpj[:, h, sw, k * 384:(k + 1) * 384], h == 0 and k == 0 and n == 0,
                                       h == 1 and k == KT // 2 - 1 and n == 2)
                        m.then_inc(S("pe_half"), 1)

                def turn_qk(w, r):
                    pe.wait_ge(S("dve_kr"), p * 4 + (2 * w + r + 1))
                    if b is not None:
                        pe.wait_ge(S("act_pT"), b * 4 + (3 + w))
                    if w == 1:
                        pe.wait_ge(S("act_qkT"), p * 4 + (r + 1))
                    for g in range(NG):
                        m = pe.transpose(bank[5 + r][:, g * P:(g + 1) * P], akr[:, 2 * w + r, g * P:(g + 1) * P], ident)
                    m.then_inc(S("pe_qkT"), 1)

                def score(i):
                    h, r = i // 2, i % 2
                    if i == 0:
                        pe.wait_ge(S("act_qkT"), b * 4 + 4)
                    if i >= 2:
                        pe.wait_ge(S("dve_sm"), b * 4 + (i - 1))
                    hp = slice(h * HD, (h + 1) * HD)
                    for g in range(NG):
                        o = bank[2][:, g * P:(g + 1) * P] if r == 0 else wide[:, g * T:(g + 1) * T]
                        m = mm(o, qTt[hp, g, r * P:(r + 1) * P], kTt[hp, g, 0:(r + 1) * P])
                    m.then_inc(S("pe_s"), 1)

                def turn_p(i):
                    r = i % 2
                    pe.wait_ge(S("act_p"), b * 4 + (i + 1))
                    if i > 0:
                        pe.wait_ge(S("act_pT"), b * 4 + i)
                    if i == 3 and p is not None:
                        pe.wait_ge(S("act_qkT"), p * 4 + 2)
                    for j in range(NG * (r + 1)):
                        m = pe.transpose(bank[5 + j // 4][:, j % 4 * P:(j % 4 + 1) * P], pr[:, r, j * P:(j + 1) * P], ident)
                    m.then_inc(S("pe_pT"), 1)

                def weigh(i):
                    h, r = i // 2, i % 2
                    pe.wait_ge(S("act_pT"), b * 4 + (i + 1))
                    n = NG * (r + 1)
                    for j in range(n):
                        g, s = j // (r + 1), j % (r + 1)
                        m = mm(bank[7][:, i * HD:(i + 1) * HD], pT[:, r, j * P:(j + 1) * P],
                               Vs[:, s, g * P + h * HD:g * P + (h + 1) * HD], j == 0, j == n - 1)
                    if i == 3:
                        m.then_inc(S("pe_o2"), 1)

                def turn_out():
                    pe.wait_ge(S("act_ao"), b * 4 + 4)
                    for r in range(RT):
                        m = pe.transpose(bank[7][:, 256 + r * P:256 + (r + 1) * P], ao[:, r, :], ident)
                    m.then_inc(S("pe_oT"), 1)

                A, B = p is not None, b is not None
                if A: project_half(0)
                if B: score(0); score(1)
                if A: project_half(1)
                if B: turn_p(0); score(2)
                if A: project_half(2)
                if B: turn_p(1); weigh(0); score(3)
                if A: project_half(3)
                if B: turn_p(2); weigh(1)
                if A: turn_qk(0, 0); turn_qk(0, 1); project_half(4, [0])
                if B: turn_p(3); weigh(2)
                if A: project_half(4, [1])
                if B: weigh(3)
                if A: project_half(5)
                if A: turn_qk(1, 0); turn_qk(1, 1)
                if B: turn_out()

            heads(0, None)
            with pe.Fori(1, KT) as p:
                heads(p, p - 1)
            heads(None, KT - 1)
            pe.wait_ge(s_wo, 16)
            pe.wait_ge(S("act_oT"), KT)
            for r in range(RT):
                for j in range(2):
                    for k in range(KT):
                        m = mm(bank[2 * r + j], oT[:, k, r * P:(r + 1) * P], wo_v[:, k, j * 512:(j + 1) * 512], k == 0, k == KT - 1)
                    m.then_inc(S("pe_awo"), 1)
            ffn(1)

        @block.scalar
        def _(act):
            def A(o, i, f, **k):
                return act.activation(o, i, f, **k)

            def squares(n, scratch, rows_ready=None, count=0):
                for r in range(RT):
                    if rows_ready:
                        act.wait_ge(S(rows_ready), count + 2 * (r + 1))
                    if n or r:
                        act.wait_ge(S("act_ss"), n * RT + r)
                    A(scratch, x[:, r, :], ACT.Square, accum_out=small[:, r:r + 1]).then_inc(S("act_ss"), 1)

            act.wait_ge(s_x, 16)
            squares(0, scratch0)

            def turned(dst, b0, n0, done):
                for r in range(RT):
                    act.wait_ge(S("pe_turned"), n0 + 2 * r + 2)
                    A(dst[:, 4:8, r * P:(r + 1) * P], bank[b0 + 2 * r + 1].rearrange("p (q t) -> p q t", q=4), ACT.Copy).then_inc(S(done), 1)

            turned(hT, 0, 0, "act_turned")
            act.wait_ge(S("pe_lora"), 1)
            A(tw[0:LW, :], bank[0][0:LW, 0:T], ACT.Tanh).then_inc(S("act_lora"), 1)
            act.wait_ge(S("pe_lora"), 2)
            A(ta[0:LW, :], bank[1][0:LW, 0:T], ACT.Copy).then_inc(S("act_lora"), 1)
            act.wait_ge(S("pe_lora"), 3)
            A(tg[:, 0, :], bank[2][:, 0:T], ACT.Sigmoid).then_inc(S("act_lora"), 1)
            A(tg[0:LG - P, 1, :], bank[3][0:LG - P, 0:T], ACT.Sigmoid).then_inc(S("act_lora"), 1)

            def pgc(n, name):
                i = ROWS.index(name)
                return pg[:, n, i:i + 1]

            def square_output(it):
                act.wait_ge(S("dve_oc"), it)
                A(osq, oc, ACT.Square).then_inc(S("act_osq"), 1)

            def group(it, behind=True):
                if behind:
                    square_output(it)
                act.wait_ge(S("dve_pg"), it + 1)
                act.wait_ge(S("pe_z"), it * 2 + 1)
                for n in range(2):
                    m = A(sz[:, n, :], bank[0][:, n * T:(n + 1) * T], ACT.Sigmoid, bias=pgc(n, "w0"))
                m.then_inc(S("act_sz"), 1)
                act.wait_ge(S("pe_z"), it * 2 + 2)
                for n in range(2):
                    m = A(sa[:, n, :], bank[1][:, n * T:(n + 1) * T], ACT.Sigmoid, bias=pgc(n, "a0"))
                m.then_inc(S("act_sa"), 1)
                act.wait_ge(S("pe_k"), it + 1)
                if behind:
                    act.wait_ge(S("dve_on"), it)
                for n in range(2):
                    A(kkr[:, n, :], bank[2][:, n * T:(n + 1) * T], ACT.Copy, scale=pgc(n, "k_k"))
                    m = A(sq[:, n, :], bank[2][:, n * T:(n + 1) * T], ACT.Square, scale=pgc(n, "k_k"))
                m.then_inc(S("act_sq"), 1)
                act.wait_ge(S("dve_G"), it + 1)
                A(E1[:, :, :], Gc[:, :, :], ACT.Exp, scale=-KAPPA).then_inc(S("act_E"), 1)
                A(En.rearrange("p (q t) -> p q t", q=4), Gc[:, :, 1:129], ACT.Exp, scale=KAPPA).then_inc(S("act_E"), 1)
                A(gsm[:, 2:4], gsm[:, 0:2], ACT.Exp, scale=-KAPPA).then_inc(S("act_E"), 1)
                act.wait_ge(S("dve_ssm"), it + 1)
                A(nrm, rn, ACT.Sqrt).then_inc(S("act_nrm"), 1)
                act.wait_ge(S("pe_g"), it + 1)
                A(gT, bank[6], ACT.Copy).then_inc(S("act_g"), 1)
                act.wait_ge(S("pe_v"), it + 1)
                A(vT, bank[5], ACT.Copy).then_inc(S("act_v"), 1)
                act.wait_ge(S("pe_tv"), it + 1)
                A(Vn.rearrange("p c n i -> p (c n i)"), bank[0], ACT.Copy).then_inc(S("act_vn"), 1)
                act.wait_ge(S("pe_tk"), it + 1)
                A(kPn.rearrange("p n i -> p (n i)"), bank[1][:, 0:256], ACT.Copy)
                A(bPn.rearrange("p n i -> p (n i)"), bank[1][:, 256:512], ACT.Copy).then_inc(S("act_kn"), 1)
                act.wait_ge(S("pe_z0"), it + 1)
                A(Zs, bank[6][:, 0:256], ACT.Copy).then_inc(S("act_z"), 1)
                for l in range(LEVELS - 1):
                    for q in range(2):
                        act.wait_ge(S("pe_T"), it * 12 + 2 * l + q + 1)
                        A(Ts[:, 4 * q:4 * q + 4, :], bank[4 + q].rearrange("p (u t) -> p u t", u=4), ACT.Copy).then_inc(S("act_T"), 1)
                for c in range(2):
                    if c == 1:
                        act.wait_ge(S("pe_z1"), it + 1)
                        A(Zs, bank[4][:, 0:256], ACT.Copy).then_inc(S("act_z"), 1)
                    act.wait_ge(S("pe_uu"), it * 2 + c + 1)
                    A(UUs[:, c, :, :].rearrange("p n i -> p (n i)"), bank[(1, 5)[c]][:, 0:256], ACT.Copy).then_inc(S("act_uu"), 1)

            group(0, behind=False)
            with act.Fori(1, NGRP) as it:
                group(it)
            square_output(NGRP)

            def ffn(layer):
                base = layer * NF
                squares((1, 3)[layer], squared[:, :], ("dve_xadd", "dve_awo")[layer], (4 * NGRP - 4, 0)[layer])

                def gu_hi(f, b, n):
                    act.wait_ge(s_gu[b], n * 32)
                    A(wsp[:, b, 0, 0:2048], raw[b][:, 0:2048], ACT.Copy).then_inc(S("act_gu_hi"), 1)

                def dn_hi(f, b, n, used=True):
                    act.wait_ge(s_dn[b], n * 16)
                    if used:
                        act.wait_ge(S("pe_dn"), f + (layer * (NF - 1) - 1))
                    A(wsp[:, b, 0, 2048:3072], raw[b][:, 2048:3072], ACT.Copy).then_inc(S("act_dn_hi"), 1)

                def silu(f, b):
                    act.wait_ge(S("pe_gu"), f + (base + 1))
                    A(sg[:, b, :], bank[4 + b][:, 0:T], ACT.Silu).then_inc(S("act_sg"), 1)

                n0 = layer * (NF // 2)
                gu_hi(0, 0, n0 + 1)
                for r in range(RT):
                    for j in range(2):
                        act.wait_ge(S("pe_turned"), (4, 16)[layer] + 2 * r + j + 1)
                        A(hparts[:, 0, 4 * j:4 * j + 4, r * P:(r + 1) * P],
                          bank[2 * r + j].rearrange("p (q t) -> p q t", q=4), ACT.Copy).then_inc(S("act_hsp"), 1)
                gu_hi(1, 1, n0 + 1)
                dn_hi(0, 0, n0 + 1, False)

                def tile(f, b, n, n2, more=True, used=True):
                    silu(f, b)
                    if more:
                        gu_hi(f + 2, b, n2)
                    dn_hi(f + 1, 1 - b, n, used)

                tile(0, 0, n0 + 1, n0 + 2, used=False)
                tile(1, 1, n0 + 2, n0 + 2)
                with act.Fori(1, NF // 2 - 1) as i:
                    tile(2 * i, 0, i + (n0 + 1), i + (n0 + 2))
                    tile(2 * i + 1, 1, i + (n0 + 2), i + (n0 + 2))
                n = n0 + NF // 2
                tile(NF - 2, 0, n, None, more=False)
                silu(NF - 1, 1)

            ffn(0)
            squares(2, pr[:, :, :].rearrange("p b n -> p (b n)")[:, 0:D], "dve_ffn")

            def rows_hi(parts, b0, n0):
                for i in range(4):
                    act.wait_ge(S("pe_turned"), n0 + i + 1)
                    r, j = i // 2, i % 2
                    A(parts[:, 0, 4 * j:4 * j + 4, r * P:(r + 1) * P],
                      bank[b0 + i].rearrange("p (q t) -> p q t", q=4), ACT.Copy).then_inc(S("act_aturned"), 1)

            def half_hi(p, u, used=True):
                act.wait_ge(s_raw[u % RAWS], p * (32 * 3) + 16 * NG * (u // RAWS + 1))
                if used:
                    act.wait_ge(S("pe_half"), p * (2 * UNITS) + 2 * (u - 1))
                A(wpj[:, u % 2, 0, :], rawh[u % RAWS], ACT.Copy).then_inc(S("act_w_hi"), 1)

            rows_hi(kparts, 0, 8)
            half_hi(0, 0, False)
            rows_hi(qparts, 4, 12)
            half_hi(0, 1, False)

            def heads(p, b, follow=True):
                def copy_raw(w, r):
                    act.wait_ge(S("pe_half"), p * (2 * UNITS) + (4 * w + r + 3))
                    A(akr[:, 2 * w + r, :], bank[r][:, 0:384], ACT.Copy).then_inc(S("act_raw"), 1)

                def square(w, r):
                    act.wait_ge(S("act_raw"), p * 4 + (2 * w + r + 1))
                    if b is not None or w or r:
                        act.wait_ge(S("dve_ass"), p * 4 + (2 * w + r))
                    A(asq, akr[:, 2 * w + r, :], ACT.Square).then_inc(S("act_asq"), 1)

                def probs(i):
                    r = i % 2
                    n = NG * (r + 1) * P
                    act.wait_ge(S("dve_nm"), b * 4 + (i + 1))
                    A(pr[:, r, 0:n], pr[:, r, 0:n], ACT.Exp, bias=asm[:, 4 + i:5 + i], scale=SCALE,
                      accum_out=asm[:, 8 + i:9 + i]).then_inc(S("act_p"), 1)

                def copy_p(i):
                    r = i % 2
                    act.wait_ge(S("pe_pT"), b * 4 + (i + 1))
                    n = NG * (r + 1) * P
                    m = A(pT[:, r, 0:min(n, 512)], bank[5][:, 0:min(n, 512)], ACT.Copy)
                    if n > 512:
                        m = A(pT[:, r, 512:n], bank[6][:, 0:n - 512], ACT.Copy)
                    m.then_inc(S("act_pT"), 1)

                def copy_qk(w, dst):
                    for r in range(RT):
                        act.wait_ge(S("pe_qkT"), p * 4 + (2 * w + r + 1))
                        A(dst[:, :, r * P:(r + 1) * P], bank[5 + r][:, 0:384].rearrange("p (g t) -> p g t", g=3),
                          ACT.Copy).then_inc(S("act_qkT"), 1)

                def copy_v(r):
                    act.wait_ge(S("pe_half"), p * (2 * UNITS) + (r + 11))
                    A(Vs[:, r, :], bank[r][:, 0:384], ACT.Copy).then_inc(S("act_Vs"), 1)

                def scale_out():
                    act.wait_ge(S("pe_o2"), b + 1)
                    act.wait_ge(S("dve_rden"), b + 1)
                    for i in range(4):
                        h, r = i // 2, i % 2
                        A(ao[:, r, h * HD:(h + 1) * HD], bank[7][:, i * HD:(i + 1) * HD], ACT.Copy,
                          scale=asm[:, 12 + i:13 + i]).then_inc(S("act_ao"), 1)

                X, B = p is not None, b is not None
                if X: half_hi(p, 2)
                if B: probs(0)
                if X: copy_raw(0, 0); square(0, 0); copy_raw(0, 1)
                if B: probs(1)
                if X: square(0, 1); half_hi(p, 3)
                if B: copy_p(0)
                if X: half_hi(p, 4)
                if B: probs(2); copy_p(1)
                if X: copy_raw(1, 0); square(1, 0); copy_raw(1, 1)
                if B: copy_p(2); probs(3)
                if X: square(1, 1); half_hi(p, 5)
                if X: copy_qk(0, kTt)
                if B: copy_p(3)
                if X and follow: half_hi(p + 1, 0)
                if B: scale_out()
                if X: copy_v(0); copy_v(1); copy_qk(1, qTt)
                if X and follow: half_hi(p + 1, 1)
                if B:
                    act.wait_ge(S("pe_oT"), b + 1)
                    dst = oT[:, bass.ds(b, 1), :].rearrange("p k t -> p (k t)")
                    A(dst, bank[7][:, 256:512], ACT.Copy).then_inc(S("act_oT"), 1)

            heads(0, None)
            with act.Fori(1, KT - 1) as p:
                heads(p, p - 1)
            heads(KT - 1, KT - 2, follow=False)
            heads(None, KT - 1)
            ffn(1)

        @block.vector
        def _(dve):
            def tt(o, a, b, op):
                return dve.tensor_tensor(o, a, b, op)

            def stt(o, a, s, b, op0, op1):
                return dve.scalar_tensor_tensor(o, a, s, b, op0, op1)

            chain = S("dve_step")
            steps = [0]

            def then(m, it=None, n=0):
                m.then_inc(chain, 1)

            class Seq:
                def __init__(self, base=0):
                    self.n = base
                    self.per = 0
                    self.it = None

                def start(self, it, per):
                    self.it, self.per, self.k = it, per, 0

                def mark(self, m):
                    m.then_inc(chain, 1)
                    if self.it is None:
                        self.n += 1
                    else:
                        self.k += 1

                def sync(self):
                    if self.it is None:
                        dve.wait_ge(chain, self.n)
                    else:
                        dve.wait_ge(chain, self.it * self.per + (self.n + self.k))

                def end(self, count):
                    assert self.k == self.per, (self.k, self.per)
                    self.n += count * self.per
                    self.it = None

            q = Seq()

            def step(m):
                q.mark(m)
                q.sync()

            step(dve.memset(onec[:, :], 1.0))
            dve.memset(mhalf[:, :], -0.5).then_inc(S("dve_mhalf"), 1)

            def rstd(n, outs, name, first_gain):
                def scale_rows(o, gi, r):
                    stt(o[:, r, :], x[:, r, :], small[:, 4 + r:5 + r], gain[:, gi, :], ALU.mult, ALU.mult).then_inc(S(name), 1)

                (o, gi), more = outs[0], outs[1:]
                for r in range(RT):
                    dve.wait_ge(S("act_ss"), n * RT + r + 1)
                    dve.tensor_scalar(small[:, 2 + r:3 + r], small[:, r:r + 1], 1.0 / D, RMS_EPS, ALU.mult, ALU.add).then_inc(S("dve_ms"), 1)
                    dve.wait_ge(S("pool_rs"), n * RT + r + 1)
                    dve.wait_ge(s_gain[gi], first_gain[gi])
                    scale_rows(o, gi, r)
                for o, gi in more:
                    dve.wait_ge(s_gain[gi], first_gain[gi])
                    for r in range(RT):
                        scale_rows(o, gi, r)

            def turned(dst, b0, n0, done):
                for r in range(RT):
                    dve.wait_ge(S("pe_turned"), n0 + 2 * r + 1)
                    dve.tensor_copy(dst[:, 0:4, r * P:(r + 1) * P], bank[b0 + 2 * r].rearrange("p (q t) -> p q t", q=4)).then_inc(S(done), 1)

            rstd(0, [(hn, 0)], "dve_hn", (16, 16))
            dve.wait_ge(S("pe_par"), 1)
            step(dve.tensor_copy(par[:, :, :], bank[7][:, 0:KT * NR].rearrange("p (k n) -> p k n", k=KT)))
            ka = ROWS.index("k_a")
            step(dve.tensor_scalar(omk[:, :], par[:, :, ka], -1.0, 1.0, ALU.mult, ALU.add))
            turned(hT, 0, 0, "dve_turned")
            dve.wait_ge(S("dve_turned"), 2)
            dve.wait_ge(S("act_turned"), 2)
            dve.tensor_scalar(dT[:, :, 0:1], hT[:, :, 0:1], -1.0, None, ALU.mult)
            step(tt(dT[:, :, 1:T], hT[:, :, 0:T - 1], hT[:, :, 1:T], ALU.subtract))
            for i, dst, name in ((1, xs[0], "dve_xs"), (4, xs[1], "dve_xs"), (5, xs[2], "dve_xs"),
                                 (2, xk, "dve_mix"), (0, xr, "dve_mix"), (3, xv, "dve_mix")):
                for k in range(KT):
                    m = stt(dst[:, k, :], dT[:, k, :], par[:, k, i:i + 1], hT[:, k, :], ALU.mult, ALU.add)
                m.then_inc(S(name), 1)
            dve.wait_ge(S("dve_mix"), 3)
            dve.wait_ge(S("pe_lora"), 3)
            q.mark(dve.memset(work[:, 0:8 * 512], 0.0))
            step(dve.memset(Gs[:, :, 0:1], 0.0))
            dve.wait_ge(s_const, 16)
            tri_f = C("tri").rearrange("p (m t) -> p m t", m=4)
            step(dve.tensor_copy(trib[:, :, :], tri_f))

            def pgc(n, name):
                i = ROWS.index(name)
                return pg[:, n, i:i + 1]

            def v4(a):
                return a.rearrange("p (q t) -> p q t", q=4)

            def v8(a):
                return a.rearrange("p (u i) -> p u i", u=8)

            def flat(a):
                return a.rearrange("p n t -> p (n t)")

            def norm_output(it):
                dve.wait_ge(S("pe_o"), it)
                step(dve.tensor_reduce(gsm[:, 8:16], v8(bank[3]), AX.X, ALU.add))
                step(dve.tensor_scalar(gsm[:, 16:24], gsm[:, 8:16], 1.0 / HD, None, ALU.mult))
                mu = gsm[:, 16:24].rearrange("p (u o) -> p u o", o=1).broadcast_to([P, 8, HD])
                tt(v8(oc), v8(bank[3]), mu, ALU.subtract).then_inc(S("dve_oc"), 1)
                dve.wait_ge(S("act_osq"), it)
                step(dve.tensor_reduce(gsm[:, 24:32], v8(osq), AX.X, ALU.add))
                dve.tensor_scalar(gsm[:, 32:40], gsm[:, 24:32], 1.0 / HD, LNX_EPS, ALU.mult, ALU.add).then_inc(S("dve_var"), 1)
                dve.wait_ge(S("pool_ors"), it)
                rs = gsm[:, 40:48].rearrange("p (u o) -> p u o", o=1).broadcast_to([P, 8, HD])
                tt(v8(on.rearrange("p c n i -> p (c n i)")), v8(oc), rs, ALU.mult).then_inc(S("dve_on"), 1)

            def gate_output(it):
                dve.wait_ge(S("pe_on"), it)
                for n in range(2):
                    m = dve.tensor_scalar(yT[:, n, :], bank[6][:, n * T:(n + 1) * T], pl[:, n, 0:1], pl[:, n, 1:2], ALU.mult, ALU.add)
                step(m)
                step(tt(flat(yT), flat(yT), bv, ALU.add))
                tt(flat(yT), flat(yT), gT, ALU.mult).then_inc(S("dve_y"), 1)

            def add_output(it):
                for i in range(4):
                    dve.wait_ge(S("pe_wo"), it * 4 + (i - 3))
                    xv_ = x[:, i // 2, (i % 2) * 512:(i % 2 + 1) * 512]
                    tt(xv_, bank[WO_BANKS[i]], xv_, ALU.add).then_inc(S("dve_xadd"), 1)

            def group(it, behind=True):
                two = bass.ds(it * 2, 2)
                q.mark(dve.tensor_copy(pg[:, :, 0:NR], par[:, two, :]))
                q.sync()
                dve.tensor_copy(pg[:, :, NR:NR + 1].rearrange("p n o -> p (n o)"), omk[:, two]).then_inc(S("dve_pg"), 1)
                if behind:
                    norm_output(it)
                dve.wait_ge(S("dve_pg"), it + 1)
                dve.wait_ge(S("act_sz"), it + 1)
                for n in range(2):
                    for c in range(2):
                        m = dve.tensor_tensor_scan(Gs[:, 2 * n + c, 1:129], onec[:, :], sz[:, n, c * P:(c + 1) * P], 0.0, ALU.mult, ALU.add)
                step(m)
                step(tt(Gc[:, :, :], Gs[:, :, :], Gs[:, :, 64:65].broadcast_to([P, 4, 129]), ALU.subtract))
                g0 = Gc.rearrange("p (n c) t -> p n c t", n=2)
                g1 = Gs.rearrange("p (n c) t -> p n c t", n=2)
                tt(gsm[:, 0:2], g0[:, :, 0, 128], g1[:, :, 1, 64], ALU.add).then_inc(S("dve_G"), 1)
                dve.wait_ge(S("act_sa"), it + 1)
                for n in range(2):
                    m = dve.tensor_scalar(t1[:, n, :], sa[:, n, :], pgc(n, "k_a"), pg[:, n, NR:NR + 1], ALU.mult, ALU.add)
                step(m)
                dve.wait_ge(S("pe_k"), it + 1)
                dve.wait_ge(S("act_sq"), it + 1)
                step(tt(flat(kT_), bank[2], flat(t1), ALU.mult))
                dve.wait_ge(S("act_E"), it * 3 + 3)
                tt(v4(flat(kP)), v4(flat(kT_)), v4(En), ALU.mult)
                if behind:
                    gate_output(it)
                lg = ROWS.index("lnx_g")
                q.mark(dve.tensor_copy(pl[:, :, :], par[:, two, lg:lg + 2]))
                dve.wait_ge(S("pe_r"), it + 1)
                for n in range(2):
                    m = stt(rkr[:, n, :], bank[4][:, n * T:(n + 1) * T], pgc(n, "r_k"), kT_[:, n, :], ALU.mult, ALU.mult)
                m.then_inc(S("dve_rkr"), 1)
                arf = ar.rearrange("p n c m t -> p (n c) m t")
                tt(arf[:, :, 1, :], v4(bank[4]), E1[:, :, 1:129], ALU.mult)
                if behind:
                    add_output(it)
                dve.wait_ge(S("pe_ss"), it + 1)
                dve.tensor_scalar(rn, bank[3], 1e-24, None, ALU.max).then_inc(S("dve_ssm"), 1)
                dve.wait_ge(S("act_nrm"), it + 1)
                step(dve.reciprocal(rn, nrm))
                step(tt(kn, flat(kkr), rn, ALU.mult))
                q.mark(tt(bb, kn, flat(sa), ALU.mult))
                stt(arf[:, :, 0, :], v4(kn), -1.0, E1[:, :, 0:128], ALU.mult, ALU.mult)
                q.sync()
                tt(flat(bP), bb, En, ALU.mult).then_inc(S("dve_scaled"), 1)
                dve.wait_ge(S("pe_bonus"), it + 1)
                dve.wait_ge(S("act_v"), it + 1)
                tt(bv, bank[7], vT, ALU.mult)
                idb = ident.rearrange("p (o t) -> p o t", o=1).broadcast_to([P, 4, P])
                for u in range(8):
                    dve.wait_ge(S("pe_mats"), it * 8 + (u + 1))
                    dve.memset(gsm[:, 48 + u:49 + u], 0.0)
                    dve.copy_predicated(M[:, u, :, :], trib[:, :, :], bank[2 + u % 4].rearrange("p (m t) -> p m t", m=4)).then_inc(S("dve_mats"), 1)
                    if u % 4 == 3:
                        h = u // 4
                        dve.wait_ge(S("dve_mats"), it * 8 + (u + 1))
                        step(tt(Us[:, 4 * h:4 * h + 4, :], M[:, 4 * h:4 * h + 4, 0, :],
                                levels[:, 0:1, :].broadcast_to([P, 4, P]), ALU.mult))
                        tt(Us[:, 4 * h:4 * h + 4, :], Us[:, 4 * h:4 * h + 4, :], idb, ALU.add).then_inc(S("dve_U"), 1)
                for l in range(1, LEVELS):
                    for h in range(2):
                        dve.wait_ge(S("pe_X"), it * 12 + 2 * l + h - 1)
                        tt(Xs[:, 4 * h:4 * h + 4, :], bank[h].rearrange("p (u t) -> p u t", u=4),
                           levels[:, l:l + 1, :].broadcast_to([P, 4, P]), ALU.mult).then_inc(S("dve_X"), 1)
                    for h in range(2):
                        dve.wait_ge(S("pe_U"), it * 12 + 2 * l + h - 1)
                        tt(Us[:, 4 * h:4 * h + 4, :], bank[2 + h].rearrange("p (u t) -> p u t", u=4),
                           Us[:, 4 * h:4 * h + 4, :], ALU.add).then_inc(S("dve_U"), 1)
                dve.wait_ge(S("pe_S"), it + 1)
                for n in range(2):
                    m = stt(St[:, n, :], bank[2][:, n * P:(n + 1) * P], gsm[:, 2 + n:3 + n], halves, ALU.mult, ALU.mult)
                m.then_inc(S("dve_S"), 1)
            HEAD, TAIL = 11, 5
            marks = q.n
            group(0, behind=False)
            assert q.n - marks == HEAD, q.n - marks
            with dve.Fori(1, NGRP) as it:
                q.start(it - 1, HEAD + TAIL)
                group(it)
            q.end(NGRP - 1)
            norm_output(NGRP)
            gate_output(NGRP)
            add_output(NGRP)

            def low_part(dst, src, hi, done):
                tt(dst, src, hi.bitcast(F32), ALU.subtract).then_inc(S(done), 1)

            def ffn(layer):
                base = layer * NF
                rstd((1, 3)[layer], [(fhn, (1, 0)[layer])], "dve_hn", ((16, 16), (48, 32))[layer])

                def gu_lo(f, b):
                    dve.wait_ge(S("act_gu_hi"), f + (base + 1))
                    low_part(wsp[:, b, 1, 0:2048], raw[b][:, 0:2048], wsp[:, b, 0, 0:2048], "dve_gu_lo")

                def dn_lo(f, b):
                    dve.wait_ge(S("act_dn_hi"), f + (base + 1))
                    low_part(wsp[:, b, 1, 2048:3072], raw[b][:, 2048:3072], wsp[:, b, 0, 2048:3072], "dve_dn_lo")

                def product(f, b, later=True):
                    if later:
                        dve.wait_ge(S("dve_act"), f + base)
                    dve.wait_ge(S("act_sg"), f + (base + 1))
                    step(tt(am[:, :], sg[:, b, :], bank[4 + b][:, T:2 * T], ALU.mult))
                    step(dve.tensor_copy(asp[:, b, 0, :], am[:, :]))
                    low_part(asp[:, b, 1, :], am[:, :], asp[:, b, 0, :], "dve_act")

                gu_lo(0, 0)
                for r in range(RT):
                    for j in range(2):
                        dve.wait_ge(S("act_hsp"), 4 * layer + 2 * r + j + 1)
                        part = [hparts[:, s_, 4 * j:4 * j + 4, r * P:(r + 1) * P] for s_ in range(2)]
                        low_part(part[1], bank[2 * r + j].rearrange("p (q t) -> p q t", q=4), part[0], "dve_hsp")
                gu_lo(1, 1)
                dn_lo(0, 0)

                def tile(f, b, more=True, later=True):
                    product(f, b, later)
                    if more:
                        gu_lo(f + 2, b)
                    dn_lo(f + 1, 1 - b)

                q.start(None, 0)
                tile(0, 0, later=layer > 0)
                tile(1, 1)
                with dve.Fori(1, NF // 2 - 1) as i:
                    q.start(i - 1, 4)
                    tile(2 * i, 0)
                    tile(2 * i + 1, 1)
                q.end(NF // 2 - 2)
                tile(NF - 2, 0, more=False)
                product(NF - 1, 1)
                for i in range(4):
                    dve.wait_ge(S("pe_sums"), 4 * layer + i + 1)
                    xv_ = x[:, i // 2, (i % 2) * 512:(i % 2 + 1) * 512]
                    tt(xv_, bank[i], xv_, ALU.add).then_inc(S("dve_ffn"), 1)

            ffn(0)
            rstd(2, [(ahn, 0), (ahn2, 1)], "dve_ahn", (32, 32))

            def rows_lo(parts, b0, n0):
                for i in range(4):
                    dve.wait_ge(S("act_aturned"), n0 + i + 1)
                    r, j = i // 2, i % 2
                    part = [parts[:, s_, 4 * j:4 * j + 4, r * P:(r + 1) * P] for s_ in range(2)]
                    low_part(part[1], bank[b0 + i].rearrange("p (q t) -> p q t", q=4), part[0], "dve_aturned")

            def half_lo(p, u):
                dve.wait_ge(S("act_w_hi"), p * UNITS + (u + 1))
                low_part(wpj[:, u % 2, 1, :], rawh[u % RAWS], wpj[:, u % 2, 0, :], "dve_w_lo")

            rows_lo(kparts, 0, 0)
            half_lo(0, 0)
            rows_lo(qparts, 4, 4)
            half_lo(0, 1)
            dve.wait_ge(s_qkg, 32)
            for w in range(2):
                for r in range(RT):
                    cosr = C("cos")[:, r * HD:(r + 1) * HD].rearrange("p (o d) -> p o d", o=1)
                    sinr = C("sin")[:, r * HD:(r + 1) * HD].rearrange("p (o d) -> p o d", o=1)
                    tt(rot[:, w, 0, r, :, :], qkg[:, w, :, :], cosr.broadcast_to([P, NG, HD]), ALU.mult)
                    for a, b in ((0, 32), (32, 0)):
                        m = tt(rot[:, w, 1, r, :, a:a + 32], qkg[:, w, :, b:b + 32],
                               sinr[:, :, a:a + 32].broadcast_to([P, NG, 32]), ALU.mult)
            m.then_inc(S("dve_rot"), 1)
            dve.wait_ge(S("dve_rot"), 1)

            def heads(p, b, follow=True):
                def mean_squares(w, r):
                    j = 2 * w + r
                    dve.wait_ge(S("act_asq"), p * 4 + (j + 1))
                    dve.tensor_reduce(asm[:, 16:22], asq.rearrange("p (g d) -> p g d", g=6), AX.X, ALU.add).then_inc(S("dve_ass"), 1)
                    dve.wait_ge(S("dve_ass"), p * 4 + (j + 1))
                    dve.tensor_scalar(asm[:, 24:30], asm[:, 16:22], 1.0 / HD, RMS_EPS, ALU.mult, ALU.add).then_inc(S("dve_av"), 1)

                def norm_rotate(w, r):
                    j = 2 * w + r
                    dve.wait_ge(S("pool_ars"), p * 4 + (j + 1))
                    rs = asm[:, 32:38].rearrange("p (g o) -> p g o", o=1).broadcast_to([P, 6, HD])
                    tt(akn.rearrange("p g h d -> p (g h) d"), akr[:, j, :].rearrange("p (g d) -> p g d", g=6),
                       rs, ALU.mult).then_inc(S("dve_kn"), 1)
                    dve.wait_ge(S("dve_kn"), p * 4 + (j + 1))
                    cosb = rot[:, w, 0, r, :, :].rearrange("p g (o d) -> p g o d", o=1).broadcast_to([P, NG, 2, HD])
                    q.mark(tt(am1[:, :, :, :], akn[:, :, :, :], cosb, ALU.mult))
                    for c, d in ((0, 32), (32, 0)):
                        sinb = rot[:, w, 1, r, :, c:c + 32].rearrange("p g (o d) -> p g o d", o=1).broadcast_to([P, NG, 2, 32])
                        m = tt(am2[:, :, :, c:c + 32], akn[:, :, :, d:d + 32], sinb, ALU.mult)
                    step(m)
                    tt(akr[:, j, :], am1.rearrange("p g h d -> p (g h d)"), am2.rearrange("p g h d -> p (g h d)"), ALU.add).then_inc(S("dve_kr"), 1)

                def mask_max(i):
                    r = i % 2
                    n = NG * (r + 1) * P
                    dve.wait_ge(S("pe_s"), b * 4 + (i + 1))
                    if i >= 2:
                        dve.wait_ge(S("pe_pT"), b * 4 + (i - 1))
                    dve.memset(asm[:, 48 + i:49 + i], 0.0)
                    src = bank[2][:, 0:n] if r == 0 else wide[:, 0:n]
                    dve.tensor_tensor_reduce(pr[:, r, 0:n], src, C(f"mask{r}"), 1.0, 3.0 * NEG, ALU.add, ALU.max,
                                             asm[:, i:i + 1]).then_inc(S("dve_sm"), 1)
                    dve.wait_ge(S("dve_sm"), b * 4 + (i + 1))
                    dve.tensor_scalar(asm[:, 4 + i:5 + i], asm[:, i:i + 1], -SCALE, None, ALU.mult).then_inc(S("dve_nm"), 1)

                X, B = p is not None, b is not None
                if B: mask_max(0)
                if X: half_lo(p, 2)
                if B: mask_max(1)
                if X: mean_squares(0, 0); norm_rotate(0, 0); mean_squares(0, 1); half_lo(p, 3); norm_rotate(0, 1)
                if B: mask_max(2); mask_max(3)
                if X: half_lo(p, 4); mean_squares(1, 0); norm_rotate(1, 0)
                if X: mean_squares(1, 1); half_lo(p, 5); norm_rotate(1, 1)
                if B:
                    dve.wait_ge(S("act_p"), b * 4 + 4)
                    dve.reciprocal(asm[:, 12:16], asm[:, 8:12]).then_inc(S("dve_rden"), 1)
                if X and follow: half_lo(p + 1, 0); half_lo(p + 1, 1)

            MARKS = 8
            marks = q.n
            heads(0, None)
            assert q.n - marks == MARKS, q.n - marks
            with dve.Fori(1, KT - 1) as p:
                q.start(p - 1, MARKS)
                heads(p, p - 1)
            q.end(KT - 2)
            heads(KT - 1, KT - 2, follow=False)
            heads(None, KT - 1)
            for i in range(4):
                dve.wait_ge(S("pe_awo"), i + 1)
                xv_ = x[:, i // 2, (i % 2) * 512:(i % 2 + 1) * 512]
                tt(xv_, bank[i], xv_, ALU.add).then_inc(S("dve_awo"), 1)
            ffn(1)

        @block.gpsimd
        def _(pool):
            pool.wait_ge(S("dve_mhalf"), 1)

            def root(dst, src, n):
                return pool.tensor_tensor(dst, src, mhalf[:, 0:n], ALU.pow)

            def norm_root(n):
                for r in range(RT):
                    pool.wait_ge(S("dve_ms"), n * RT + r + 1)
                    root(small[:, 4 + r:5 + r], small[:, 2 + r:3 + r], 1).then_inc(S("pool_rs"), 1)

            norm_root(0)
            with pool.Fori(0, NGRP) as it:
                pool.wait_ge(S("dve_var"), it + 1)
                root(gsm[:, 40:48], gsm[:, 32:40], 8).then_inc(S("pool_ors"), 1)
            norm_root(1)
            norm_root(2)
            with pool.Fori(0, KT) as p:
                for j in range(4):
                    pool.wait_ge(S("dve_av"), p * 4 + j + 1)
                    root(asm[:, 32:38], asm[:, 24:30], 6).then_inc(S("pool_ars"), 1)
            norm_root(3)


ROW_INPUTS = ["a_mu", "a_w0", "a_a0", "a_k_k", "a_k_a", "a_r_k", "a_lnx_g", "a_lnx_b"]
INS = ["x", "a_norm_g", "a_w_r", "a_w_k", "a_w_v", "a_w1", "a_w2", "a_a1", "a_a2", "a_g1", "a_g2", "a_w_o", "kv_norm_g", "w_kv", "k_norm_g",
       "b_norm_g", "b_w_q", "b_q_norm_g", "b_w_o", "f_norm_g", "f_w_gu", "f_w_down"]


def kernel(**inputs):
    import concourse.bacc as bacc
    from concourse.bass_utils import run_bass_kernel_spmd

    nc = bacc.Bacc("TRN2", target_bir_lowering=False, num_devices=1)
    arrays, args = {}, {}
    table = np.concatenate([CONSTS[n] for n in CAT], 1)
    rows = np.concatenate([np.asarray(inputs[n]).reshape(-1, D) for n in ROW_INPUTS], 0)
    for name in INS + ["const", "rows"]:
        a = {"const": table, "rows": rows}.get(name)
        if a is None:
            a = np.ascontiguousarray(inputs[name])
        arrays[f"in_{name}"] = a
        args[name] = nc.dram_tensor(f"in_{name}", a.shape, mybir.dt.from_np(a.dtype), kind="ExternalInput").ap()
    out = nc.dram_tensor("out", (1, T, D), F32, kind="ExternalOutput").ap()
    program(nc, args, out)
    r = run_bass_kernel_spmd(nc, [arrays], core_ids=[0])
    return r.results[0]["out"]
```

```python
import math

import numpy as np
import concourse.bass as bass
from concourse import mybir
from contextlib import ExitStack

F32 = mybir.dt.float32
I32 = mybir.dt.int32
F32R = mybir.dt.float32r
ALU = mybir.AluOpType
ACT = mybir.ActivationFunctionType
AX = mybir.AxisListType

P = 128
D, T = 1024, 256
KT, RT = D // P, T // P
HD = 64
LW, LG = 64, 160
FF = -(-8 * D // (3 * 256)) * 256
NF = FF // P
GROUPS = ((128, 1), (512, 4), (2048, 16))
NG = len(GROUPS)
KAPPA = math.exp(-0.5)
RMS_EPS, LNX_EPS = 1e-6, 64e-5
LEVELS = 7
NEG = -1e30
SCALE = HD ** -0.5

ROWS = ["mu0", "mu1", "mu2", "mu3", "mu4", "mu5", "w0", "a0", "k_k", "k_a", "r_k", "lnx_g", "lnx_b"]
NR = len(ROWS)


def constants():
    p = np.arange(P)[:, None]
    f = np.arange(P)[None, :]
    out = {"ident": (p == f).astype(np.float32)}
    out["halves"] = (p // HD == f // HD).astype(np.float32)
    strict, incl = (p < f), (p <= f)
    out["tri"] = np.concatenate([strict, incl, strict, incl], 1).astype(np.float32)
    lev = []
    for l in range(LEVELS):
        m = 1 << l
        lev.append(((p // (2 * m) == f // (2 * m)) & (p // m % 2 == 1) & (f // m % 2 == 0)).astype(np.float32))
    lev[0] = lev[0].T
    out["levels"] = np.concatenate(lev, 1)
    for r in range(RT):
        t = p + r * P
        s = np.arange((r + 1) * P)[None, :]
        parts = []
        for window, dil in GROUPS:
            ok = (t >= s) & ((t - s) % dil == 0) & (t - s <= window)
            parts.append(np.where(ok, 0.0, NEG).astype(np.float32))
        out[f"mask{r}"] = np.concatenate(parts, 1)
    inv = (10000.0 ** (-np.arange(0, HD, 2, dtype=np.float32) / HD)).astype(np.float32)
    ang = np.arange(T, dtype=np.float32)[:, None] * inv[None, :]
    cos, sin = np.cos(ang).astype(np.float32), np.sin(ang).astype(np.float32)
    c = np.concatenate([cos, cos], 1).reshape(RT, P, HD)
    s = np.concatenate([-sin, sin], 1).reshape(RT, P, HD)
    out["cos"] = np.concatenate([c[r] for r in range(RT)], 1)
    out["sin"] = np.concatenate([s[r] for r in range(RT)], 1)
    return out


CONSTS = constants()
CAT = {}
_at = 0
for _n, _v in CONSTS.items():
    CAT[_n] = (_at, _v.shape[1])
    _at += _v.shape[1]
NCONST = _at


def program(nc, ins, out):
    ctx = ExitStack()
    with ctx:
        def sb(name, shape, dt=F32):
            return ctx.enter_context(nc.sbuf_tensor(name, shape, dt))

        def sem(name):
            return ctx.enter_context(nc.semaphore(name))

        x = sb("x", [P, RT, D])
        cst = sb("cst", [P, NCONST])
        trib = sb("trib", [P, 4, P], I32)
        gain = sb("gain", [P, 2, D])
        rows = sb("rows", [NR, D])
        par = sb("par", [P, KT, NR])
        omk = sb("omk", [P, KT])
        onec = sb("onec", [P, P])
        mhalf = sb("mhalf", [P, 16])
        small = sb("small", [P, 64])
        ring = sb("ring", [P, 6144])
        wmix = sb("wmix", [P, 4, KT * 256])
        WORK = 28000
        pg = sb("pg", [P, 2, NR + 1])
        pl = sb("pl", [P, 2, 2])
        w2s = sb("w2s", [LW, 256])
        a2s = sb("a2s", [LW, 256])
        g2s = sb("g2s", [P, 2, 256])
        gsm = sb("gsm", [P, 64])
        first = ExitStack()
        work = first.enter_context(nc.sbuf_tensor("work", [P, WORK], F32))

        def C(name):
            a, n = CAT[name]
            return cst[:, a:a + n]

        ident, halves = C("ident"), C("halves")

        class Carve:
            def __init__(self, at=0):
                self.at = at

            def take(self, size, pattern=None, **k):
                v = work[:, self.at:self.at + size]
                self.at += size
                assert self.at <= WORK, self.at
                return v.rearrange(pattern, **k) if pattern else v

        bank = [ctx.enter_context(nc.psum_tensor(f"bank{i}", [P, 512], F32)) for i in range(3)]
        wide = ctx.enter_context(nc.psum_tensor("wide", [P, 1024], F32))
        bank += [wide[:, 0:512], wide[:, 512:1024]]
        bank += [ctx.enter_context(nc.psum_tensor(f"bank{i}", [P, 512], F32)) for i in range(5, 8)]
        bank = [b[:, :] for b in bank]

        names = {}

        def S(name):
            if name not in names:
                names[name] = sem(name)
            return names[name]

        cv = Carve()
        hT = cv.take(KT * T, "p (k t) -> p k t", k=KT)
        dT = cv.take(KT * T, "p (k t) -> p k t", k=KT)
        M = work[:, 0:8 * 512].rearrange("p (u m t) -> p u m t", u=8, m=4)
        xr, xk, xv = (cv.take(KT * T, "p (k t) -> p k t", k=KT) for _ in range(3))
        tw = cv.take(T)
        ta = cv.take(T)
        tg = cv.take(2 * T, "p (k t) -> p k t", k=2)
        gat = cv.at
        xs = [cv.take(KT * T, "p (k t) -> p k t", k=KT) for _ in range(3)]
        hn = cv.take(RT * D, "p (r d) -> p r d", r=RT)
        w1s = cv.take(KT * LW, "p (k n) -> p k n", k=KT)
        a1s = cv.take(KT * LW, "p (k n) -> p k n", k=KT)
        g1s = cv.take(KT * LG, "p (k n) -> p k n", k=KT)
        cg = Carve(gat)
        Us = cg.take(8 * P, "p (u t) -> p u t", u=8)
        Ts = cg.take(8 * P, "p (u t) -> p u t", u=8)
        Xs = cg.take(8 * P, "p (u t) -> p u t", u=8)
        ar = cg.take(8 * P, "p (n c m t) -> p n c m t", n=2, c=2, m=2)
        sz = cg.take(512, "p (n t) -> p n t", n=2)
        sa = cg.take(512, "p (n t) -> p n t", n=2)
        Gs = cg.take(4 * 129, "p (q t) -> p q t", q=4)
        Gc = cg.take(4 * 129, "p (q t) -> p q t", q=4)
        E1 = cg.take(4 * 129, "p (q t) -> p q t", q=4)
        En = sz.rearrange("p n t -> p (n t)")
        over_X = Xs.rearrange("p u t -> p (u t)")
        kkr = over_X[:, 0:512].rearrange("p (n t) -> p n t", n=2)
        sq = cg.take(512, "p (n t) -> p n t", n=2)
        nrm = cg.take(512)
        rn = over_X[:, 512:1024]
        kn = cg.take(512)
        t1 = cg.take(512, "p (n t) -> p n t", n=2)
        kT_ = cg.take(512, "p (n t) -> p n t", n=2)
        rkr = cg.take(512, "p (n t) -> p n t", n=2)
        bb = sq.rearrange("p n t -> p (n t)")
        kP = cg.take(512, "p (n t) -> p n t", n=2)
        bP = cg.take(512, "p (n t) -> p n t", n=2)
        vT = cg.take(512)
        gT = cg.take(512)
        bv = nrm
        Vn = cg.take(512, "p (c n i) -> p c n i", c=2, n=2)
        kPn = cg.take(256, "p (n i) -> p n i", n=2)
        bPn = cg.take(256, "p (n i) -> p n i", n=2)
        Zs = cg.take(256)
        UUs = cg.take(512, "p (c n i) -> p c n i", c=2, n=2)
        St = cg.take(256, "p (n i) -> p n i", n=2)
        oc = kkr.rearrange("p n t -> p (n t)")
        osq = kn
        on = cg.take(512, "p (c n i) -> p c n i", c=2, n=2)
        yT = cg.take(512, "p (n t) -> p n t", n=2)
        scratch0 = work[:, WORK - D:WORK]
        levels = C("levels").rearrange("p (l t) -> p l t", l=LEVELS)
        NGRP = D // 256
        WO_BANKS = (0, 1, 2, 7)
        EARLY = 3

        first.close()
        second = ExitStack()

        def sb2(name, shape, dt=F32):
            return second.enter_context(nc.sbuf_tensor(name, shape, dt))

        wsp = sb2("wsp", [P, 2, 2, 3072], F32R)
        hsp = sb2("hsp", [P, 2, KT * T], F32R)
        asp = sb2("asp", [P, 2, 2, T], F32R)
        fhn = sb2("fhn", [P, RT, D])
        sg = sb2("sg", [P, 2, T])
        am = sb2("am", [P, T])
        squared = sb2("squared", [P, D])
        PASSES = ((0, 0), (0, 1), (1, 0))
        gus = [wsp[:, b, :, 0:2048].rearrange("p s (k m n) -> p s k m n", k=KT, m=2) for b in range(2)]
        dns = [wsp[:, b, :, 2048:3072] for b in range(2)]
        raw = [ring[:, b * 3072:(b + 1) * 3072] for b in range(2)]
        hparts = hsp[:, :, :].rearrange("p s (k t) -> p s k t", k=KT)

        second.close()

        def sbv(name, shape):
            h = sb(name, shape)
            return h[tuple(slice(0, n) for n in shape)]

        hkq = ctx.enter_context(nc.sbuf_tensor("hkq", [P, 2, 2, KT * T], F32R))
        kparts, qparts = (hkq[:, w, :, :].rearrange("p s (k t) -> p s k t", k=KT) for w in range(2))
        rot = sbv("rot", [P, 2, 2, RT, NG, HD])
        qkg = sbv("qkg", [P, 2, NG, HD])
        asq = sbv("asq", [P, 384])
        akn, am1, am2 = (sbv(n, [P, NG, 2, HD]) for n in ("akn", "am1", "am2"))
        ao = sbv("ao", [P, RT, P])
        used = 2 * 2 * KT * T + 8 * RT // 2 * NG * HD + 2 * NG * HD + 384 + 3 * NG * 2 * HD + RT * P
        sb("to_hsp", [P, 2 * 2 * 3072 - used])
        oT = sbv("oT", [P, KT, T])
        once = sbv("once", [P, 4608])
        ahn, ahn2 = (once[:, w * RT * D:(w + 1) * RT * D].rearrange("p (r d) -> p r d", r=RT) for w in range(2))
        akr = once[:, 0:1536].rearrange("p (j n) -> p j n", j=4)
        pr, pT = (once[:, 1536 * (i + 1):1536 * (i + 2)].rearrange("p (b n) -> p b n", b=2) for i in range(2))
        turned_qk = sbv("turned_qk", [P, 2 * NG * T])
        kTt, qTt = (turned_qk[:, w * NG * T:(w + 1) * NG * T].rearrange("p (g t) -> p g t", g=NG) for w in range(2))
        Vs = sbv("Vs", [P, RT, 384])
        HALF = KT // 2 * NG * P
        UNITS, RAWS = 6, 3
        wpj = ctx.enter_context(nc.sbuf_tensor("wpj", [P, 2, 2, HALF], F32R))
        rawh = [ring[:, i * HALF:(i + 1) * HALF] for i in range(RAWS)]
        asm = gsm
        wo_v = wmix[:, :, :].rearrange("p a (b n) -> p (a b) n", n=D)

        s_ident, s_const, s_rows, s_lora = S("ident_loaded"), S("const_loaded"), S("rows_loaded"), S("lora_loaded")
        s_x = [S(f"x{r}_loaded") for r in range(RT)]
        s_gain = [S("gain0_loaded"), S("gain1_loaded")]
        s_wm = [S(f"wmix{i}_loaded") for i in range(4)]
        s_l2 = S("lora2_loaded")
        s_gu = [S(f"gate_up{i}_loaded") for i in range(2)]
        s_dn = [S(f"down{i}_loaded") for i in range(2)]
        s_raw = [S(f"projection_weights{i}_loaded") for i in range(RAWS)]
        s_wo, s_qkg, s_out = S("wo_loaded"), S("qk_gains_loaded"), S("stored")

        block = ctx.enter_context(nc.Block())

        @block.sync
        def _(sp):
            for r in range(RT):
                sp.dma_start(x[:, r, :], ins["x"][0][r * P:(r + 1) * P, :]).then_inc(s_x[r], 16)

            def load_gain(i, src):
                sp.dma_start(gain[:, i, :], src.partition_broadcast(P)).then_inc(s_gain[i], 16)

            sp.dma_start(ident, ins["const"][:, 0:P]).then_inc(s_ident, 16)
            load_gain(0, ins["a_norm_g"][0])
            sp.dma_start(rows[:, :], ins["rows"]).then_inc(s_rows, 16)
            for dst, n in ((w1s, "a_w1"), (a1s, "a_a1"), (g1s, "a_g1")):
                sp.dma_start(dst, ins[n][0].rearrange("(k p) n -> p k n", p=P)).then_inc(s_lora, 16)

            cols = [ins[n][0].rearrange("(k p) n -> p k n", p=P) for n in ("a_w_r", "a_w_k", "a_w_v")]
            wo_rows = ins["a_w_o"][0].rearrange("(g n p) d -> g p n d", p=P, n=2)

            def load_mix(it):
                for i, free in ((1, "pe_k"), (0, "pe_r"), (2, "pe_v")):
                    if it is not None:
                        sp.wait_ge(S(free), it)
                    c0 = 0 if it is None else it * 256
                    sp.dma_start(wmix[:, i, :].rearrange("p (k n) -> p k n", k=KT),
                                 cols[i][:, :, bass.ds(c0, 256)]).then_inc(s_wm[i], 16)
                    if it is None and i == 1:
                        sp.dma_start(cst[:, P:NCONST], ins["const"][:, P:NCONST]).then_inc(s_const, 16)
                if it is not None:
                    sp.wait_ge(S("pe_z"), it * 2)
                    sp.wait_ge(S("pe_g"), it)
                c0 = 0 if it is None else it * 256
                sp.dma_start(w2s[:, :], ins["a_w2"][0][:, bass.ds(c0, 256)]).then_inc(s_l2, 16)
                sp.dma_start(a2s[:, :], ins["a_a2"][0][:, bass.ds(c0, 256)]).then_inc(s_l2, 16)
                sp.dma_start(g2s[:, 0, :], ins["a_g2"][0][0:P, bass.ds(c0, 256)]).then_inc(s_l2, 16)
                sp.dma_start(g2s[0:LG - P, 1, :], ins["a_g2"][0][P:LG, bass.ds(c0, 256)]).then_inc(s_l2, 16)
                if it is not None:
                    sp.wait_ge(S("pe_wo"), it * 4)
                sp.dma_start(wmix[:, 3, :].rearrange("p (n d) -> p n d", n=2),
                             wo_rows[0 if it is None else bass.ds(it, 1)] if it is None
                             else wo_rows[bass.ds(it, 1)].rearrange("a p n d -> p (a n) d")).then_inc(s_wm[3], 16)

            load_mix(None)
            load_gain(1, ins["f_norm_g"][0])
            with sp.Fori(1, NGRP) as it:
                load_mix(it)

            def load_ffn(layer, f, b, n, first):
                gu = ins["f_w_gu"][layer].rearrange("(k p) (m n) -> p m k n", p=P, m=2)
                if not first:
                    sp.wait_ge(S("dve_gu_lo"), n)
                for m in range(2):
                    sp.dma_start(raw[b][:, 0:2048].rearrange("p (k m n) -> p k m n", k=KT, m=2)[:, :, m, :],
                                 gu[:, m, :, bass.ds(f * P, P)]).then_inc(s_gu[b], 16)
                if not first:
                    sp.wait_ge(S("dve_dn_lo"), n)
                sp.dma_start(raw[b][:, 2048:3072], ins["f_w_down"][layer][bass.ds(f * P, P), :]).then_inc(s_dn[b], 16)

            def ffn(layer):
                base = layer * NF
                for b in range(2):
                    load_ffn(layer, b, b, None, True)
                with sp.Fori(1, NF // 2) as i:
                    for b in range(2):
                        done = i * 2 + (base + b - 1)
                        load_ffn(layer, i * 2 + b, b, done, False)

            ffn(0)
            sp.wait_ge(S("dve_hn"), 2 * RT)
            load_gain(0, ins["kv_norm_g"])
            load_gain(1, ins["b_norm_g"][0])
            kvw = ins["w_kv"].rearrange("(k p) (m g n) -> p m k g n", p=P, m=2, g=NG)
            qw = ins["b_w_q"][0].rearrange("(k p) (g n) -> p k g n", p=P, g=NG)
            srcs = [kvw[:, 0], qw, kvw[:, 1]]

            def load_half(p, u, fresh):
                if not fresh:
                    sp.wait_ge(S("dve_w_lo"), p * UNITS + (u + 1 - RAWS))
                c0 = p * P
                k0 = u % 2 * (KT // 2)
                for g in range(NG):
                    sp.dma_start(rawh[u % RAWS].rearrange("p (k g n) -> p k g n", g=NG, n=P)[:, :, g, :],
                                 srcs[u // 2][:, k0:k0 + KT // 2, g, bass.ds(c0, P)]).then_inc(s_raw[u % RAWS], 16)

            sp.wait_ge(S("dve_gu_lo"), NF)
            sp.wait_ge(S("dve_dn_lo"), NF)
            for u in range(RAWS):
                load_half(0, u, True)
            sp.wait_ge(S("dve_ffn"), 4)
            for w, n in ((0, "k_norm_g"), (1, "b_q_norm_g")):
                src = ins[n] if w == 0 else ins[n][0]
                sp.dma_start(qkg[:, w], src.partition_broadcast(P)).then_inc(s_qkg, 16)
            for u in range(RAWS, UNITS):
                load_half(0, u, False)
            sp.dma_start(wo_v, ins["b_w_o"][0].rearrange("(k p) d -> p k d", p=P)).then_inc(s_wo, 16)
            with sp.Fori(1, KT) as p:
                for u in range(UNITS):
                    load_half(p, u, False)
            sp.wait_ge(S("dve_ahn"), 2 * RT)
            load_gain(0, ins["f_norm_g"][1])
            sp.wait_ge(S("dve_w_lo"), KT * UNITS)
            ffn(1)
            for r in range(RT):
                sp.wait_ge(S("dve_ffn"), 4 + 2 * (r + 1))
                sp.dma_start(out[0][r * P:(r + 1) * P, :], x[:, r, :]).then_inc(s_out, 16)
            sp.wait_ge(s_out, 16 * RT)

        @block.tensor
        def _(pe):
            def mm(o, a, b, start=True, stop=True):
                return pe.matmul(o, a, b, start=start, stop=stop)

            def turn_rows(src, n0):
                for r in range(RT):
                    pe.wait_ge(S(src[1]), n0 + r + 1)
                    for j in range(2):
                        for q in range(4):
                            k = 4 * j + q
                            m = pe.transpose(bank[2 * r + j][:, q * P:(q + 1) * P], src[0][:, r, k * P:(k + 1) * P], ident)
                        m.then_inc(S("pe_turned"), 1)

            pe.wait_ge(s_ident, 16)
            pe.wait_ge(s_rows, 16)
            for k in range(KT):
                m = pe.transpose(bank[7][:, k * NR:(k + 1) * NR], rows[0:NR, k * P:(k + 1) * P], ident[0:NR, 0:NR])
            m.then_inc(S("pe_par"), 1)
            turn_rows((hn, "dve_hn"), 0)
            pe.wait_ge(s_lora, 48)
            pe.wait_ge(S("act_turned"), 2)
            pe.wait_ge(S("dve_turned"), 2)
            pe.wait_ge(S("dve_xs"), 1)
            for k in range(KT):
                if k == KT // 2:
                    pe.wait_ge(S("dve_xs"), 2)
                m = mm(bank[0][0:LW, 0:T], w1s[:, k, :], xs[0][:, k, :], k == 0, k == KT - 1)
            m.then_inc(S("pe_lora"), 1)
            pe.wait_ge(S("dve_xs"), 3)
            for k in range(KT):
                m = mm(bank[1][0:LW, 0:T], a1s[:, k, :], xs[1][:, k, :], k == 0, k == KT - 1)
            m.then_inc(S("pe_lora"), 1)
            pe.wait_ge(S("dve_xs"), 4)
            for k in range(KT):
                mm(bank[2][:, 0:T], g1s[:, k, 0:P], xs[2][:, k, :], k == 0, k == KT - 1)
            for k in range(KT):
                m = mm(bank[3][0:LG - P, 0:T], g1s[:, k, P:LG], xs[2][:, k, :], k == 0, k == KT - 1)
            m.then_inc(S("pe_lora"), 1)

            def project(b, i, src, name, quarters=range(4)):
                for n, k0 in ((v // 2, v % 2 * (KT // 2)) for v in quarters):
                    for k in range(k0, k0 + KT // 2):
                        w = wmix[:, i, :].rearrange("p (k n) -> p k n", k=KT)[:, k, n * P:(n + 1) * P]
                        m = mm(bank[b][:, n * T:(n + 1) * T], w, src[:, k, :], k == 0, k == KT - 1)
                if 3 in quarters:
                    m.then_inc(S(name), 1)

            def turn_output(it, chunks=range(2), b=2):
                pe.wait_ge(S("dve_on"), it * 2 + (chunks[-1] - 1))
                for n in range(2):
                    for c in chunks:
                        m = pe.transpose(bank[b][:, (2 * n + c) * P:(2 * n + c + 1) * P], on[:, c, n, :], ident)
                m.then_inc(S("pe_on"), 1)

            def product_o(it, tiles=range(RT), done=0):
                pe.wait_ge(S("dve_y"), it + done)
                if tiles[0] == 0:
                    pe.wait_ge(s_wm[3], it * 16)
                for r in tiles:
                    for j in range(2):
                        for n in range(2):
                            w = wmix[:, 3, :].rearrange("p (n d) -> p n d", n=2)[:, n, j * 512:(j + 1) * 512]
                            m = mm(bank[WO_BANKS[2 * r + j]], yT[:, n, r * P:(r + 1) * P], w, n == 0, n == 1)
                        m.then_inc(S("pe_wo"), 1)

            def group(it, behind=True, ahead=True):
                def next_keys(v):
                    if ahead:
                        if v == 0:
                            pe.wait_ge(s_wm[1], it * 16 + 32)
                        project(7, 1, xk, "pe_k", [v])

                pe.wait_ge(s_l2, it * 64 + 64)
                for n in range(2):
                    m = mm(bank[0][:, n * T:(n + 1) * T], w2s[:, n * P:(n + 1) * P], tw[0:LW, :])
                m.then_inc(S("pe_z"), 1)
                for n in range(2):
                    m = mm(bank[1][:, n * T:(n + 1) * T], a2s[:, n * P:(n + 1) * P], ta[0:LW, :])
                m.then_inc(S("pe_z"), 1)
                pe.wait_ge(s_wm[0], it * 16 + 16)
                project(4, 0, xr, "pe_r")
                if behind:
                    turn_output(it)
                pe.wait_ge(S("act_sq"), it + 1)
                mm(bank[3], halves, sq.rearrange("p n t -> p (n t)")).then_inc(S("pe_ss"), 1)
                for n in range(2):
                    mm(bank[5][:, n * T:(n + 1) * T], g2s[:, 0, n * P:(n + 1) * P], tg[:, 0, :], True, False)
                    m = mm(bank[5][:, n * T:(n + 1) * T], g2s[0:LG - P, 1, n * P:(n + 1) * P], tg[0:LG - P, 1, :], False, True)
                m.then_inc(S("pe_g"), 1)
                pe.wait_ge(s_wm[2], it * 16 + 16)
                early = EARLY if behind else 4
                project(6, 2, xv, "pe_v", range(early - 1))
                if behind:
                    pe.wait_ge(S("act_sa"), it + 1)
                    product_o(it)
                project(6, 2, xv, "pe_v", [early - 1])
                if behind:
                    pe.wait_ge(S("dve_xadd"), it * 4)
                pe.wait_ge(S("dve_rkr"), it + 1)
                mm(bank[7], halves, rkr.rearrange("p n t -> p (n t)")).then_inc(S("pe_bonus"), 1)
                pe.wait_ge(S("dve_scaled"), it + 1)
                for j, src in enumerate((kP, bP)):
                    for n in range(2):
                        m = pe.transpose(bank[1][:, (2 * j + n) * P:(2 * j + n + 1) * P], src[:, n, 0:P], ident)
                m.then_inc(S("pe_tk"), 1)

                pe.wait_ge(S("act_g"), it + 1)
                for c in range(2):
                    for nn in range(2):
                        for h in range(2):
                            u = 4 * c + 2 * nn + h
                            if u >= 4:
                                pe.wait_ge(S("dve_mats"), it * 8 + u - 3)
                            b = bank[2 + u % 4]
                            hp = slice(h * HD, (h + 1) * HD)
                            rhs = ar[hp, nn, c, :, :].rearrange("p m t -> p (m t)")
                            mm(b[:, 0:256], bP[hp, nn, c * P:(c + 1) * P], rhs)
                            m = mm(b[:, 256:512], kP[hp, nn, c * P:(c + 1) * P], rhs)
                            m.then_inc(S("pe_mats"), 1)
                def values_fill(l):
                    if l + early < 4:
                        project(6, 2, xv, "pe_v", [l + early])
                    elif l == 4:
                        pe.wait_ge(S("act_v"), it + 1)
                        for c in range(2):
                            for n in range(2):
                                m = pe.transpose(bank[6][:, (2 * c + n) * P:(2 * c + n + 1) * P],
                                                 vT[:, n * T + c * P:n * T + (c + 1) * P], ident)
                        m.then_inc(S("pe_tv"), 1)
                    elif l == 5:
                        pe.wait_ge(S("act_vn"), it + 1)
                        for u in range(4):
                            m = mm(bank[6][:, u * HD:(u + 1) * HD], M[:, u, 2, :], Vn[:, 0, u // 2, (u % 2) * HD:(u % 2 + 1) * HD])
                        m.then_inc(S("pe_z0"), 1)

                values_fill(0)
                for l in range(LEVELS):
                    for q in range(2) if l else ():
                        pe.wait_ge(S("act_T"), it * 12 + 2 * l + q - 1)
                        if l == 1:
                            pe.wait_ge(S("act_kn"), it + 1)
                        for j in range(4):
                            u = 4 * q + j
                            m = mm(bank[q][:, j * P:(j + 1) * P], M[:, u, 0, :], Ts[:, u, :])
                        m.then_inc(S("pe_X"), 1)
                    for q in range(2) if l else ():
                        pe.wait_ge(S("dve_X"), it * 12 + 2 * l + q - 1)
                        for j in range(4):
                            u = 4 * q + j
                            m = mm(bank[2 + q][:, j * P:(j + 1) * P], Xs[:, u, :], Us[:, u, :])
                        m.then_inc(S("pe_U"), 1)
                    if l == LEVELS - 1:
                        next_keys(0)
                    for q in range(2):
                        pe.wait_ge(S("dve_U"), it * 14 + 2 * l + q + 1)
                        if l == 0:
                            pe.wait_ge(S("dve_mats"), it * 8 + 8)
                        if l < LEVELS - 1:
                            for j in range(4):
                                u = 4 * q + j
                                m = pe.transpose(bank[4 + q][:, j * P:(j + 1) * P], Us[:, u, :], ident)
                            m.then_inc(S("pe_T"), 1)
                        if l > 0 and q == 0:
                            values_fill(l)

                def hcols(v, u):
                    return v[:, u * HD:(u + 1) * HD]

                pe.wait_ge(S("act_z"), it * 2 + 1)
                for u in range(4):
                    m = mm(hcols(bank[1], u), Us[:, u, :], hcols(Zs, u))
                m.then_inc(S("pe_uu"), 1)
                next_keys(1)
                pe.wait_ge(S("act_uu"), it * 2 + 1)
                for n in range(2):
                    mm(bank[2][:, n * P:(n + 1) * P], kPn[:, n, :], Vn[:, 0, n, :], True, False)
                    m = mm(bank[2][:, n * P:(n + 1) * P], bPn[:, n, :], UUs[:, 0, n, :], False, True)
                m.then_inc(S("pe_S"), 1)
                for u in range(4):
                    hh = slice((u % 2) * HD, (u % 2 + 1) * HD)
                    mm(hcols(bank[3], u), M[:, u, 3, :], Vn[:, 0, u // 2, hh], True, False)
                    m = mm(hcols(bank[3], u), M[:, u, 1, :], UUs[:, 0, u // 2, hh], False, True)
                m.then_inc(S("pe_o"), 1)
                pe.wait_ge(S("dve_S"), it + 1)
                for n in range(2):
                    mm(bank[4][:, n * P:(n + 1) * P], ar[:, n, 1, 0, :], St[:, n, :], True, False)
                    for h in range(2):
                        u = 2 * n + h
                        m = mm(hcols(bank[4], u), M[:, 4 + u, 2, :], Vn[:, 1, n, h * HD:(h + 1) * HD], False, h == 1)
                m.then_inc(S("pe_z1"), 1)
                next_keys(2)
                pe.wait_ge(S("act_z"), it * 2 + 2)
                for u in range(4):
                    m = mm(hcols(bank[5], u), Us[:, 4 + u, :], hcols(Zs, u))
                m.then_inc(S("pe_uu"), 1)
                next_keys(3)
                pe.wait_ge(S("act_uu"), it * 2 + 2)
                for n in range(2):
                    mm(bank[6][:, n * P:(n + 1) * P], ar[:, n, 1, 1, :], St[:, n, :], True, False)
                    for h in range(2):
                        u = 2 * n + h
                        hh = slice(h * HD, (h + 1) * HD)
                        o = hcols(bank[6], u)
                        mm(o, M[:, 4 + u, 3, :], Vn[:, 1, n, hh], False, False)
                        m = mm(o, M[:, 4 + u, 1, :], UUs[:, 1, n, hh], False, h == 1)
                m.then_inc(S("pe_o"), 1)

            pe.wait_ge(s_wm[1], 16)
            pe.wait_ge(S("dve_mix"), 1)
            project(7, 1, xk, "pe_k")
            pe.wait_ge(S("act_lora"), 4)
            pe.wait_ge(S("dve_mix"), 3)
            pe.wait_ge(s_const, 16)
            group(0, behind=False)
            with pe.Fori(1, NGRP - 1) as it:
                group(it)
            group(NGRP - 1, ahead=False)
            turn_output(NGRP, [0])
            product_o(NGRP, [0])
            turn_output(NGRP, [1], 3)
            product_o(NGRP, [1], 1)

            def ffn(layer):
                base = layer * NF
                turn_rows((fhn, "dve_hn"), RT * (1 + layer))
                pe.wait_ge(S("dve_hsp"), 4 * (layer + 1))

                def gate_up(f, b, b_free=True):
                    pe.wait_ge(S("dve_gu_lo"), f + (base + 1))
                    if b_free:
                        pe.wait_ge(S("dve_act"), f + (base - 1))
                    for m_ in range(2):
                        o = bank[4 + b][:, m_ * T:(m_ + 1) * T]
                        for k in range(KT):
                            for n, (sw, sh) in enumerate(PASSES):
                                m = mm(o, gus[b][:, sw, k, m_, :], hparts[:, sh, k, :],
                                       k == 0 and n == 0, k == KT - 1 and n == 2)
                    m.then_inc(S("pe_gu"), 1)

                def down(f, b, first=False, last=False):
                    pe.wait_ge(S("dve_act"), f + (base + 1))
                    pe.wait_ge(S("dve_dn_lo"), f + (base + 1))
                    for r in range(RT):
                        for j in range(2):
                            for n, (sa_, sw) in enumerate(PASSES):
                                m = mm(bank[2 * r + j], asp[:, b, sa_, r * P:(r + 1) * P],
                                       dns[b][:, sw, j * 512:(j + 1) * 512], first and n == 0, last and n == 2)
                            if last:
                                m.then_inc(S("pe_sums"), 1)
                    if not last:
                        m.then_inc(S("pe_dn"), 1)

                gate_up(0, 0, False)
                gate_up(1, 1, False)
                down(0, 0, first=True)
                gate_up(2, 0)
                down(1, 1)
                with pe.Fori(1, NF // 2 - 1) as i:
                    gate_up(2 * i + 1, 1)
                    down(2 * i, 0)
                    gate_up(2 * i + 2, 0)
                    down(2 * i + 1, 1)
                f = NF - 2
                gate_up(f + 1, 1)
                down(f, 0)
                down(f + 1, 1, last=True)

            ffn(0)

            pe.wait_ge(S("dve_ffn"), 4)
            turn_rows((ahn, "dve_ahn"), 0)
            for r in range(RT):
                pe.wait_ge(S("dve_ahn"), RT + r + 1)
                for j in range(2):
                    for q in range(4):
                        k = 4 * j + q
                        m = pe.transpose(bank[4 + 2 * r + j][:, q * P:(q + 1) * P], ahn2[:, r, k * P:(k + 1) * P], ident)
                    m.then_inc(S("pe_turned"), 1)
            pe.wait_ge(S("dve_aturned"), 4)

            def heads(p, b):
                def project_half(u, tiles=range(RT)):
                    what, h = u // 2, u % 2
                    pe.wait_ge(S("dve_w_lo"), p * UNITS + (u + 1))
                    if u == 2 and b is None:
                        pe.wait_ge(S("dve_aturned"), 8)
                    src = qparts if what == 1 else kparts
                    for r in tiles:
                        if h == 0:
                            if what > 0:
                                pe.wait_ge(S("act_raw"), p * 4 + (2 * what - 1 + r))
                            elif b is not None:
                                pe.wait_ge(S("act_Vs"), b * 2 + (r + 1))
                        for k in range(KT // 2):
                            for n, (sh, sw) in enumerate(PASSES):
                                m = mm(bank[r][:, 0:384], src[:, sh, h * (KT // 2) + k, r * P:(r + 1) * P],
                                       wpj[:, h, sw, k * 384:(k + 1) * 384], h == 0 and k == 0 and n == 0,
                                       h == 1 and k == KT // 2 - 1 and n == 2)
                        m.then_inc(S("pe_half"), 1)

                def turn_qk(w, r):
                    pe.wait_ge(S("dve_kr"), p * 4 + (2 * w + r + 1))
                    if b is not None:
                        pe.wait_ge(S("act_pT"), b * 4 + (3 + w))
                    if w == 1:
                        pe.wait_ge(S("act_qkT"), p * 4 + (r + 1))
                    for g in range(NG):
                        m = pe.transpose(bank[5 + r][:, g * P:(g + 1) * P], akr[:, 2 * w + r, g * P:(g + 1) * P], ident)
                    m.then_inc(S("pe_qkT"), 1)

                def score(i):
                    h, r = i // 2, i % 2
                    if i == 0:
                        pe.wait_ge(S("act_qkT"), b * 4 + 4)
                    if i >= 2:
                        pe.wait_ge(S("dve_sm"), b * 4 + (i - 1))
                    hp = slice(h * HD, (h + 1) * HD)
                    for g in range(NG):
                        o = bank[2][:, g * P:(g + 1) * P] if r == 0 else wide[:, g * T:(g + 1) * T]
                        m = mm(o, qTt[hp, g, r * P:(r + 1) * P], kTt[hp, g, 0:(r + 1) * P])
                    m.then_inc(S("pe_s"), 1)

                def turn_p(i):
                    r = i % 2
                    pe.wait_ge(S("act_p"), b * 4 + (i + 1))
                    if i > 0:
                        pe.wait_ge(S("act_pT"), b * 4 + i)
                    if i == 3 and p is not None:
                        pe.wait_ge(S("act_qkT"), p * 4 + 2)
                    for j in range(NG * (r + 1)):
                        m = pe.transpose(bank[5 + j // 4][:, j % 4 * P:(j % 4 + 1) * P], pr[:, r, j * P:(j + 1) * P], ident)
                    m.then_inc(S("pe_pT"), 1)

                def weigh(i):
                    h, r = i // 2, i % 2
                    pe.wait_ge(S("act_pT"), b * 4 + (i + 1))
                    n = NG * (r + 1)
                    for j in range(n):
                        g, s = j // (r + 1), j % (r + 1)
                        m = mm(bank[7][:, i * HD:(i + 1) * HD], pT[:, r, j * P:(j + 1) * P],
                               Vs[:, s, g * P + h * HD:g * P + (h + 1) * HD], j == 0, j == n - 1)
                    if i == 3:
                        m.then_inc(S("pe_o2"), 1)

                def turn_out():
                    pe.wait_ge(S("act_ao"), b * 4 + 4)
                    for r in range(RT):
                        m = pe.transpose(bank[7][:, 256 + r * P:256 + (r + 1) * P], ao[:, r, :], ident)
                    m.then_inc(S("pe_oT"), 1)

                A, B = p is not None, b is not None
                if A: project_half(0)
                if B: score(0); score(1)
                if A: project_half(1)
                if B: turn_p(0); score(2)
                if A: project_half(2)
                if B: turn_p(1); weigh(0); score(3)
                if A: project_half(3)
                if B: turn_p(2); weigh(1)
                if A: turn_qk(0, 0); turn_qk(0, 1); project_half(4, [0])
                if B: turn_p(3); weigh(2)
                if A: project_half(4, [1])
                if B: weigh(3)
                if A: project_half(5)
                if A: turn_qk(1, 0); turn_qk(1, 1)
                if B: turn_out()

            heads(0, None)
            with pe.Fori(1, KT) as p:
                heads(p, p - 1)
            heads(None, KT - 1)
            pe.wait_ge(s_wo, 16)
            pe.wait_ge(S("act_oT"), KT)
            for r in range(RT):
                for j in range(2):
                    for k in range(KT):
                        m = mm(bank[2 * r + j], oT[:, k, r * P:(r + 1) * P], wo_v[:, k, j * 512:(j + 1) * 512], k == 0, k == KT - 1)
                    m.then_inc(S("pe_awo"), 1)
            ffn(1)

        @block.scalar
        def _(act):
            def A(o, i, f, **k):
                return act.activation(o, i, f, **k)

            def squares(n, scratch, rows_ready=None, count=0):
                for r in range(RT):
                    if n == 0:
                        act.wait_ge(s_x[r], 16)
                    if rows_ready:
                        act.wait_ge(S(rows_ready), count + 2 * (r + 1))
                    if n or r:
                        act.wait_ge(S("act_ss"), n * RT + r)
                    A(scratch, x[:, r, :], ACT.Square, accum_out=small[:, r:r + 1]).then_inc(S("act_ss"), 1)

            squares(0, scratch0)

            def turned(dst, b0, n0, done):
                for r in range(RT):
                    act.wait_ge(S("pe_turned"), n0 + 2 * r + 2)
                    A(dst[:, 4:8, r * P:(r + 1) * P], bank[b0 + 2 * r + 1].rearrange("p (q t) -> p q t", q=4), ACT.Copy).then_inc(S(done), 1)

            turned(hT, 0, 0, "act_turned")
            act.wait_ge(S("pe_lora"), 1)
            A(tw[0:LW, :], bank[0][0:LW, 0:T], ACT.Tanh).then_inc(S("act_lora"), 1)
            act.wait_ge(S("pe_lora"), 2)
            A(ta[0:LW, :], bank[1][0:LW, 0:T], ACT.Copy).then_inc(S("act_lora"), 1)
            act.wait_ge(S("pe_lora"), 3)
            A(tg[:, 0, :], bank[2][:, 0:T], ACT.Sigmoid).then_inc(S("act_lora"), 1)
            A(tg[0:LG - P, 1, :], bank[3][0:LG - P, 0:T], ACT.Sigmoid).then_inc(S("act_lora"), 1)

            def pgc(n, name):
                i = ROWS.index(name)
                return pg[:, n, i:i + 1]

            def square_output(it, c):
                act.wait_ge(S("dve_oc"), it * 2 + (c - 1))
                A(osq[:, c * T:(c + 1) * T], oc[:, c * T:(c + 1) * T], ACT.Square).then_inc(S("act_osq"), 1)

            def group(it, behind=True):
                if behind:
                    square_output(it, 1)
                act.wait_ge(S("dve_pg"), it + 1)
                act.wait_ge(S("pe_z"), it * 2 + 1)
                for n in range(2):
                    m = A(sz[:, n, :], bank[0][:, n * T:(n + 1) * T], ACT.Sigmoid, bias=pgc(n, "w0"))
                m.then_inc(S("act_sz"), 1)
                act.wait_ge(S("pe_z"), it * 2 + 2)
                for n in range(2):
                    m = A(sa[:, n, :], bank[1][:, n * T:(n + 1) * T], ACT.Sigmoid, bias=pgc(n, "a0"))
                m.then_inc(S("act_sa"), 1)
                act.wait_ge(S("pe_k"), it + 1)
                if behind:
                    act.wait_ge(S("dve_on"), it * 2)
                for n in range(2):
                    A(kkr[:, n, :], bank[7][:, n * T:(n + 1) * T], ACT.Copy, scale=pgc(n, "k_k"))
                    m = A(sq[:, n, :], bank[7][:, n * T:(n + 1) * T], ACT.Square, scale=pgc(n, "k_k"))
                m.then_inc(S("act_sq"), 1)
                act.wait_ge(S("dve_G"), it + 1)
                A(E1[:, :, :], Gc[:, :, :], ACT.Exp, scale=-KAPPA).then_inc(S("act_E"), 1)
                A(En.rearrange("p (q t) -> p q t", q=4), Gc[:, :, 1:129], ACT.Exp, scale=KAPPA).then_inc(S("act_E"), 1)
                A(gsm[:, 2:4], gsm[:, 0:2], ACT.Exp, scale=-KAPPA).then_inc(S("act_E"), 1)
                act.wait_ge(S("dve_ssm"), it + 1)
                A(nrm, rn, ACT.Sqrt).then_inc(S("act_nrm"), 1)
                act.wait_ge(S("pe_g"), it + 1)
                if behind:
                    act.wait_ge(S("dve_y"), it)
                A(gT, bank[5], ACT.Copy).then_inc(S("act_g"), 1)
                act.wait_ge(S("pe_tk"), it + 1)
                A(kPn.rearrange("p n i -> p (n i)"), bank[1][:, 0:256], ACT.Copy)
                A(bPn.rearrange("p n i -> p (n i)"), bank[1][:, 256:512], ACT.Copy).then_inc(S("act_kn"), 1)
                for l in range(LEVELS - 1):
                    for q in range(2):
                        act.wait_ge(S("pe_T"), it * 12 + 2 * l + q + 1)
                        A(Ts[:, 4 * q:4 * q + 4, :], bank[4 + q].rearrange("p (u t) -> p u t", u=4), ACT.Copy).then_inc(S("act_T"), 1)
                    if l == 3 - EARLY:
                        act.wait_ge(S("pe_v"), it + 1)
                        A(vT, bank[6], ACT.Copy).then_inc(S("act_v"), 1)
                    if l == 4:
                        act.wait_ge(S("pe_tv"), it + 1)
                        A(Vn.rearrange("p c n i -> p (c n i)"), bank[6], ACT.Copy).then_inc(S("act_vn"), 1)
                    if l == 5:
                        act.wait_ge(S("pe_z0"), it + 1)
                        A(Zs, bank[6][:, 0:256], ACT.Copy).then_inc(S("act_z"), 1)
                for c in range(2):
                    if c == 1:
                        act.wait_ge(S("pe_z1"), it + 1)
                        A(Zs, bank[4][:, 0:256], ACT.Copy).then_inc(S("act_z"), 1)
                    act.wait_ge(S("pe_uu"), it * 2 + c + 1)
                    A(UUs[:, c, :, :].rearrange("p n i -> p (n i)"), bank[(1, 5)[c]][:, 0:256], ACT.Copy).then_inc(S("act_uu"), 1)
                square_output(it + 1, 0)

            group(0, behind=False)
            with act.Fori(1, NGRP) as it:
                group(it)
            square_output(NGRP, 1)

            def ffn(layer):
                base = layer * NF

                def gu_hi(f, b, n):
                    act.wait_ge(s_gu[b], n * 32)
                    A(wsp[:, b, 0, 0:2048], raw[b][:, 0:2048], ACT.Copy).then_inc(S("act_gu_hi"), 1)

                def dn_hi(f, b, n, used=True):
                    act.wait_ge(s_dn[b], n * 16)
                    if used:
                        act.wait_ge(S("pe_dn"), f + (layer * (NF - 1) - 1))
                    A(wsp[:, b, 0, 2048:3072], raw[b][:, 2048:3072], ACT.Copy).then_inc(S("act_dn_hi"), 1)

                def silu(f, b):
                    act.wait_ge(S("pe_gu"), f + (base + 1))
                    A(sg[:, b, :], bank[4 + b][:, 0:T], ACT.Silu).then_inc(S("act_sg"), 1)

                n0 = layer * (NF // 2)
                gu_hi(0, 0, n0 + 1)
                gu_hi(1, 1, n0 + 1)
                dn_hi(0, 0, n0 + 1, False)
                squares((1, 3)[layer], squared[:, :], ("dve_xadd", "dve_awo")[layer], (4 * NGRP - 4, 0)[layer])
                for r in range(RT):
                    for j in range(2):
                        act.wait_ge(S("pe_turned"), (4, 16)[layer] + 2 * r + j + 1)
                        A(hparts[:, 0, 4 * j:4 * j + 4, r * P:(r + 1) * P],
                          bank[2 * r + j].rearrange("p (q t) -> p q t", q=4), ACT.Copy).then_inc(S("act_hsp"), 1)

                def tile(f, b, n, n2, more=True, used=True):
                    silu(f, b)
                    if more:
                        gu_hi(f + 2, b, n2)
                    dn_hi(f + 1, 1 - b, n, used)

                tile(0, 0, n0 + 1, n0 + 2, used=False)
                tile(1, 1, n0 + 2, n0 + 2)
                with act.Fori(1, NF // 2 - 1) as i:
                    tile(2 * i, 0, i + (n0 + 1), i + (n0 + 2))
                    tile(2 * i + 1, 1, i + (n0 + 2), i + (n0 + 2))
                n = n0 + NF // 2
                tile(NF - 2, 0, n, None, more=False)
                silu(NF - 1, 1)

            ffn(0)

            def rows_hi(parts, b0, n0):
                for i in range(4):
                    act.wait_ge(S("pe_turned"), n0 + i + 1)
                    r, j = i // 2, i % 2
                    A(parts[:, 0, 4 * j:4 * j + 4, r * P:(r + 1) * P],
                      bank[b0 + i].rearrange("p (q t) -> p q t", q=4), ACT.Copy).then_inc(S("act_aturned"), 1)

            def half_hi(p, u, used=True):
                act.wait_ge(s_raw[u % RAWS], p * (32 * 3) + 16 * NG * (u // RAWS + 1))
                if used:
                    act.wait_ge(S("pe_half"), p * (2 * UNITS) + 2 * (u - 1))
                A(wpj[:, u % 2, 0, :], rawh[u % RAWS], ACT.Copy).then_inc(S("act_w_hi"), 1)

            half_hi(0, 0, False)
            half_hi(0, 1, False)
            squares(2, turned_qk[:, 0:D], "dve_ffn")
            rows_hi(kparts, 0, 8)
            rows_hi(qparts, 4, 12)

            def heads(p, b, follow=True):
                def copy_raw(w, r):
                    act.wait_ge(S("pe_half"), p * (2 * UNITS) + (4 * w + r + 3))
                    A(akr[:, 2 * w + r, :], bank[r][:, 0:384], ACT.Copy).then_inc(S("act_raw"), 1)

                def square(w, r):
                    act.wait_ge(S("act_raw"), p * 4 + (2 * w + r + 1))
                    if b is not None or w or r:
                        act.wait_ge(S("dve_ass"), p * 4 + (2 * w + r))
                    A(asq, akr[:, 2 * w + r, :], ACT.Square).then_inc(S("act_asq"), 1)

                def probs(i):
                    r = i % 2
                    n = NG * (r + 1) * P
                    act.wait_ge(S("dve_nm"), b * 4 + (i + 1))
                    A(pr[:, r, 0:n], pr[:, r, 0:n], ACT.Exp, bias=asm[:, 4 + i:5 + i], scale=SCALE,
                      accum_out=asm[:, 8 + i:9 + i]).then_inc(S("act_p"), 1)

                def copy_p(i):
                    r = i % 2
                    act.wait_ge(S("pe_pT"), b * 4 + (i + 1))
                    n = NG * (r + 1) * P
                    m = A(pT[:, r, 0:min(n, 512)], bank[5][:, 0:min(n, 512)], ACT.Copy)
                    if n > 512:
                        m = A(pT[:, r, 512:n], bank[6][:, 0:n - 512], ACT.Copy)
                    m.then_inc(S("act_pT"), 1)

                def copy_qk(w, dst):
                    for r in range(RT):
                        act.wait_ge(S("pe_qkT"), p * 4 + (2 * w + r + 1))
                        A(dst[:, :, r * P:(r + 1) * P], bank[5 + r][:, 0:384].rearrange("p (g t) -> p g t", g=3),
                          ACT.Copy).then_inc(S("act_qkT"), 1)

                def copy_v(r):
                    act.wait_ge(S("pe_half"), p * (2 * UNITS) + (r + 11))
                    A(Vs[:, r, :], bank[r][:, 0:384], ACT.Copy).then_inc(S("act_Vs"), 1)

                def scale_out():
                    act.wait_ge(S("pe_o2"), b + 1)
                    act.wait_ge(S("dve_rden"), b + 1)
                    for i in range(4):
                        h, r = i // 2, i % 2
                        A(ao[:, r, h * HD:(h + 1) * HD], bank[7][:, i * HD:(i + 1) * HD], ACT.Copy,
                          scale=asm[:, 12 + i:13 + i]).then_inc(S("act_ao"), 1)

                X, B = p is not None, b is not None
                if X: half_hi(p, 2)
                if B: probs(0)
                if X: copy_raw(0, 0); square(0, 0); copy_raw(0, 1)
                if B: probs(1)
                if X: square(0, 1); half_hi(p, 3)
                if B: copy_p(0)
                if X: half_hi(p, 4)
                if B: probs(2); copy_p(1)
                if X: copy_raw(1, 0); square(1, 0); copy_raw(1, 1)
                if B: copy_p(2); probs(3)
                if X: square(1, 1); half_hi(p, 5)
                if X: copy_qk(0, kTt)
                if B: copy_p(3)
                if X and follow: half_hi(p + 1, 0)
                if B: scale_out()
                if X: copy_v(0); copy_v(1); copy_qk(1, qTt)
                if X and follow: half_hi(p + 1, 1)
                if B:
                    act.wait_ge(S("pe_oT"), b + 1)
                    dst = oT[:, bass.ds(b, 1), :].rearrange("p k t -> p (k t)")
                    A(dst, bank[7][:, 256:512], ACT.Copy).then_inc(S("act_oT"), 1)

            heads(0, None)
            with act.Fori(1, KT - 1) as p:
                heads(p, p - 1)
            heads(KT - 1, KT - 2, follow=False)
            heads(None, KT - 1)
            ffn(1)

        @block.vector
        def _(dve):
            def tt(o, a, b, op):
                return dve.tensor_tensor(o, a, b, op)

            def stt(o, a, s, b, op0, op1):
                return dve.scalar_tensor_tensor(o, a, s, b, op0, op1)

            chain = S("dve_step")

            class Seq:
                def __init__(self, base=0):
                    self.n = base
                    self.per = 0
                    self.it = None

                def start(self, it, per):
                    self.it, self.per, self.k = it, per, 0

                def mark(self, m):
                    m.then_inc(chain, 1)
                    if self.it is None:
                        self.n += 1
                    else:
                        self.k += 1

                def sync(self):
                    if self.it is None:
                        dve.wait_ge(chain, self.n)
                    else:
                        dve.wait_ge(chain, self.it * self.per + (self.n + self.k))

                def end(self, count):
                    assert self.k == self.per, (self.k, self.per)
                    self.n += count * self.per
                    self.it = None

            q = Seq()

            def step(m):
                q.mark(m)
                q.sync()

            step(dve.memset(onec[:, :], 1.0))
            dve.memset(mhalf[:, :], -0.5).then_inc(S("dve_mhalf"), 1)

            def scale_rows(o, gi, count, r, name):
                dve.wait_ge(s_gain[gi], count)
                stt(o[:, r, :], x[:, r, :], small[:, 4 + r:5 + r], gain[:, gi, :], ALU.mult, ALU.mult).then_inc(S(name), 1)

            def norm(n, o, name, gi, count):
                for r in range(RT):
                    dve.wait_ge(S("act_ss"), n * RT + r + 1)
                    dve.tensor_scalar(small[:, 2 + r:3 + r], small[:, r:r + 1], 1.0 / D, RMS_EPS, ALU.mult, ALU.add).then_inc(S("dve_ms"), 1)
                    dve.wait_ge(S("pool_rs"), n * RT + r + 1)
                    scale_rows(o, gi, count, r, name)

            def turned(dst, b0, n0, done):
                for r in range(RT):
                    dve.wait_ge(S("pe_turned"), n0 + 2 * r + 1)
                    dve.tensor_copy(dst[:, 0:4, r * P:(r + 1) * P], bank[b0 + 2 * r].rearrange("p (q t) -> p q t", q=4)).then_inc(S(done), 1)

            norm(0, hn, "dve_hn", 0, 16)
            dve.wait_ge(S("pe_par"), 1)
            step(dve.tensor_copy(par[:, :, :], bank[7][:, 0:KT * NR].rearrange("p (k n) -> p k n", k=KT)))
            ka = ROWS.index("k_a")
            step(dve.tensor_scalar(omk[:, :], par[:, :, ka], -1.0, 1.0, ALU.mult, ALU.add))
            turned(hT, 0, 0, "dve_turned")
            dve.wait_ge(S("dve_turned"), 2)

            def difference(k0):
                ks = slice(k0, k0 + KT // 2)
                dve.tensor_scalar(dT[:, ks, 0:1], hT[:, ks, 0:1], -1.0, None, ALU.mult)
                step(tt(dT[:, ks, 1:T], hT[:, ks, 0:T - 1], hT[:, ks, 1:T], ALU.subtract))

            def mix(i, dst, name, k0=0, n=KT):
                for k in range(k0, k0 + n):
                    m = stt(dst[:, k, :], dT[:, k, :], par[:, k, i:i + 1], hT[:, k, :], ALU.mult, ALU.add)
                m.then_inc(S(name), 1)

            difference(0)
            mix(1, xs[0], "dve_xs", 0, KT // 2)
            dve.wait_ge(S("act_turned"), 2)
            difference(KT // 2)
            mix(1, xs[0], "dve_xs", KT // 2, KT // 2)
            mix(4, xs[1], "dve_xs")
            mix(5, xs[2], "dve_xs")
            for i, dst in ((2, xk), (0, xr), (3, xv)):
                mix(i, dst, "dve_mix")
            dve.wait_ge(S("dve_mix"), 3)
            dve.wait_ge(S("pe_lora"), 3)
            q.mark(dve.memset(work[:, 0:8 * 512], 0.0))
            step(dve.memset(Gs[:, :, 0:1], 0.0))
            dve.wait_ge(s_const, 16)
            tri_f = C("tri").rearrange("p (m t) -> p m t", m=4)
            step(dve.tensor_copy(trib[:, :, :], tri_f))

            def pgc(n, name):
                i = ROWS.index(name)
                return pg[:, n, i:i + 1]

            def v4(a):
                return a.rearrange("p (q t) -> p q t", q=4)

            def flat(a):
                return a.rearrange("p n t -> p (n t)")

            def norm_output(it, c):
                o = bank[(3, 6)[c]][:, 0:T].rearrange("p (u i) -> p u i", u=4)
                cut = slice(c * T, (c + 1) * T)
                st = [gsm[:, 8 * i + 4 * c:8 * i + 4 * c + 4] for i in range(6)]
                dve.wait_ge(S("pe_o"), it * 2 + (c - 1))
                step(dve.tensor_reduce(st[1], o, AX.X, ALU.add))
                step(dve.tensor_scalar(st[2], st[1], 1.0 / HD, None, ALU.mult))
                wide_ = [st[i].rearrange("p (u o) -> p u o", o=1).broadcast_to([P, 4, HD]) for i in (2, 5)]
                occ = oc[:, cut].rearrange("p (u i) -> p u i", u=4)
                tt(occ, o, wide_[0], ALU.subtract).then_inc(S("dve_oc"), 1)
                dve.wait_ge(S("act_osq"), it * 2 + (c - 1))
                step(dve.tensor_reduce(st[3], osq[:, cut].rearrange("p (u i) -> p u i", u=4), AX.X, ALU.add))
                dve.tensor_scalar(st[4], st[3], 1.0 / HD, LNX_EPS, ALU.mult, ALU.add).then_inc(S("dve_var"), 1)
                dve.wait_ge(S("pool_ors"), it * 2 + (c - 1))
                tt(on[:, c, :, :].rearrange("p n (h i) -> p (n h) i", h=2), occ, wide_[1], ALU.mult).then_inc(S("dve_on"), 1)

            def gate_output(it, c=None):
                cut = slice(0, T) if c is None else slice(c * P, (c + 1) * P)
                b = 3 if c == 1 else 2
                dve.wait_ge(S("pe_on"), it + (c or 0))
                for n in range(2):
                    m = dve.tensor_scalar(yT[:, n, cut], bank[b].rearrange("p (n t) -> p n t", n=2)[:, n, cut], pl[:, n, 0:1], pl[:, n, 1:2], ALU.mult, ALU.add)
                step(m)
                y, bo, ga = yT[:, :, cut], *(v.rearrange("p (n t) -> p n t", n=2)[:, :, cut] for v in (bv, gT))
                step(tt(y, y, bo, ALU.add))
                tt(y, y, ga, ALU.mult).then_inc(S("dve_y"), 1)

            def add_output(it, quarters=range(4)):
                for i in quarters:
                    dve.wait_ge(S("pe_wo"), it * 4 + (i - 3))
                    xv_ = x[:, i // 2, (i % 2) * 512:(i % 2 + 1) * 512]
                    tt(xv_, bank[WO_BANKS[i]], xv_, ALU.add).then_inc(S("dve_xadd"), 1)

            def group(it, behind=True):
                two = bass.ds(it * 2, 2)
                q.mark(dve.tensor_copy(pg[:, :, 0:NR], par[:, two, :]))
                q.sync()
                dve.tensor_copy(pg[:, :, NR:NR + 1].rearrange("p n o -> p (n o)"), omk[:, two]).then_inc(S("dve_pg"), 1)
                if behind:
                    norm_output(it, 1)
                dve.wait_ge(S("dve_pg"), it + 1)
                dve.wait_ge(S("act_sz"), it + 1)
                for n in range(2):
                    for c in range(2):
                        m = dve.tensor_tensor_scan(Gs[:, 2 * n + c, 1:129], onec[:, :], sz[:, n, c * P:(c + 1) * P], 0.0, ALU.mult, ALU.add)
                step(m)
                step(tt(Gc[:, :, :], Gs[:, :, :], Gs[:, :, 64:65].broadcast_to([P, 4, 129]), ALU.subtract))
                g0 = Gc.rearrange("p (n c) t -> p n c t", n=2)
                g1 = Gs.rearrange("p (n c) t -> p n c t", n=2)
                tt(gsm[:, 0:2], g0[:, :, 0, 128], g1[:, :, 1, 64], ALU.add).then_inc(S("dve_G"), 1)
                dve.wait_ge(S("act_sa"), it + 1)
                for n in range(2):
                    m = dve.tensor_scalar(t1[:, n, :], sa[:, n, :], pgc(n, "k_a"), pg[:, n, NR:NR + 1], ALU.mult, ALU.add)
                step(m)
                dve.wait_ge(S("pe_k"), it + 1)
                dve.wait_ge(S("act_sq"), it + 1)
                step(tt(flat(kT_), bank[7], flat(t1), ALU.mult))
                dve.wait_ge(S("act_E"), it * 3 + 3)
                tt(v4(flat(kP)), v4(flat(kT_)), v4(En), ALU.mult)
                if behind:
                    gate_output(it)
                lg = ROWS.index("lnx_g")
                q.mark(dve.tensor_copy(pl[:, :, :], par[:, two, lg:lg + 2]))
                dve.wait_ge(S("pe_r"), it + 1)
                for n in range(2):
                    m = stt(rkr[:, n, :], bank[4][:, n * T:(n + 1) * T], pgc(n, "r_k"), kT_[:, n, :], ALU.mult, ALU.mult)
                m.then_inc(S("dve_rkr"), 1)
                arf = ar.rearrange("p n c m t -> p (n c) m t")
                tt(arf[:, :, 1, :], v4(bank[4]), E1[:, :, 1:129], ALU.mult)
                dve.wait_ge(S("pe_ss"), it + 1)
                dve.tensor_scalar(rn, bank[3], 1e-24, None, ALU.max).then_inc(S("dve_ssm"), 1)
                dve.wait_ge(S("act_nrm"), it + 1)
                step(dve.reciprocal(rn, nrm))
                step(tt(kn, flat(kkr), rn, ALU.mult))
                q.mark(tt(bb, kn, flat(sa), ALU.mult))
                stt(arf[:, :, 0, :], v4(kn), -1.0, E1[:, :, 0:128], ALU.mult, ALU.mult)
                q.sync()
                tt(flat(bP), bb, En, ALU.mult).then_inc(S("dve_scaled"), 1)
                if behind:
                    add_output(it)
                idb = ident.rearrange("p (o t) -> p o t", o=1).broadcast_to([P, 4, P])
                for u in range(8):
                    dve.wait_ge(S("pe_mats"), it * 8 + (u + 1))
                    dve.memset(gsm[:, 48 + u:49 + u], 0.0)
                    dve.copy_predicated(M[:, u, :, :], trib[:, :, :], bank[2 + u % 4].rearrange("p (m t) -> p m t", m=4)).then_inc(S("dve_mats"), 1)
                    if u % 4 == 3:
                        h = u // 4
                        dve.wait_ge(S("dve_mats"), it * 8 + (u + 1))
                        step(tt(Us[:, 4 * h:4 * h + 4, :], M[:, 4 * h:4 * h + 4, 0, :],
                                levels[:, 0:1, :].broadcast_to([P, 4, P]), ALU.mult))
                        tt(Us[:, 4 * h:4 * h + 4, :], Us[:, 4 * h:4 * h + 4, :], idb, ALU.add).then_inc(S("dve_U"), 1)
                for l in range(1, LEVELS):
                    for h in range(2):
                        dve.wait_ge(S("pe_X"), it * 12 + 2 * l + h - 1)
                        tt(Xs[:, 4 * h:4 * h + 4, :], bank[h].rearrange("p (u t) -> p u t", u=4),
                           levels[:, l:l + 1, :].broadcast_to([P, 4, P]), ALU.mult).then_inc(S("dve_X"), 1)
                    for h in range(2):
                        dve.wait_ge(S("pe_U"), it * 12 + 2 * l + h - 1)
                        tt(Us[:, 4 * h:4 * h + 4, :], bank[2 + h].rearrange("p (u t) -> p u t", u=4),
                           Us[:, 4 * h:4 * h + 4, :], ALU.add).then_inc(S("dve_U"), 1)
                    if l == 3:
                        dve.wait_ge(S("pe_bonus"), it + 1)
                        dve.wait_ge(S("act_v"), it + 1)
                        tt(bv, bank[7], vT, ALU.mult)
                dve.wait_ge(S("pe_S"), it + 1)
                for n in range(2):
                    m = stt(St[:, n, :], bank[2][:, n * P:(n + 1) * P], gsm[:, 2 + n:3 + n], halves, ALU.mult, ALU.mult)
                m.then_inc(S("dve_S"), 1)
                norm_output(it + 1, 0)
            HEAD, TAIL = 14, 5
            marks = q.n
            group(0, behind=False)
            assert q.n - marks == HEAD, q.n - marks
            with dve.Fori(1, NGRP) as it:
                q.start(it - 1, HEAD + TAIL)
                group(it)
            q.end(NGRP - 1)
            def low_part(dst, src, hi, done):
                tt(dst, src, hi.bitcast(F32), ALU.subtract).then_inc(S(done), 1)

            def gu_lo(f, b, base):
                dve.wait_ge(S("act_gu_hi"), f + (base + 1))
                low_part(wsp[:, b, 1, 0:2048], raw[b][:, 0:2048], wsp[:, b, 0, 0:2048], "dve_gu_lo")

            def dn_lo(f, b, base):
                dve.wait_ge(S("act_dn_hi"), f + (base + 1))
                low_part(wsp[:, b, 1, 2048:3072], raw[b][:, 2048:3072], wsp[:, b, 0, 2048:3072], "dve_dn_lo")

            def half_lo(p, u):
                dve.wait_ge(S("act_w_hi"), p * UNITS + (u + 1))
                low_part(wpj[:, u % 2, 1, :], rawh[u % RAWS], wpj[:, u % 2, 0, :], "dve_w_lo")

            gate_output(NGRP, 0)
            norm_output(NGRP, 1)
            gate_output(NGRP, 1)
            add_output(NGRP, [0, 1])
            gu_lo(0, 0, 0)
            add_output(NGRP, [2, 3])

            def ffn(layer):
                base = layer * NF
                norm((1, 3)[layer], fhn, "dve_hn", (1, 0)[layer], (16, 48)[layer])

                def product(f, b, later=True):
                    if later:
                        dve.wait_ge(S("dve_act"), f + base)
                    dve.wait_ge(S("act_sg"), f + (base + 1))
                    step(tt(am[:, :], sg[:, b, :], bank[4 + b][:, T:2 * T], ALU.mult))
                    step(dve.tensor_copy(asp[:, b, 0, :], am[:, :]))
                    low_part(asp[:, b, 1, :], am[:, :], asp[:, b, 0, :], "dve_act")

                for r in range(RT):
                    for j in range(2):
                        dve.wait_ge(S("act_hsp"), 4 * layer + 2 * r + j + 1)
                        part = [hparts[:, s_, 4 * j:4 * j + 4, r * P:(r + 1) * P] for s_ in range(2)]
                        low_part(part[1], bank[2 * r + j].rearrange("p (q t) -> p q t", q=4), part[0], "dve_hsp")
                gu_lo(1, 1, base)
                dn_lo(0, 0, base)

                def tile(f, b, more=True, later=True):
                    product(f, b, later)
                    if more:
                        gu_lo(f + 2, b, base)
                    dn_lo(f + 1, 1 - b, base)

                q.start(None, 0)
                tile(0, 0, later=layer > 0)
                tile(1, 1)
                with dve.Fori(1, NF // 2 - 1) as i:
                    q.start(i - 1, 4)
                    tile(2 * i, 0)
                    tile(2 * i + 1, 1)
                q.end(NF // 2 - 2)
                tile(NF - 2, 0, more=False)
                product(NF - 1, 1)
                for i in range(4):
                    dve.wait_ge(S("pe_sums"), 4 * layer + i + 1)
                    xv_ = x[:, i // 2, (i % 2) * 512:(i % 2 + 1) * 512]
                    tt(xv_, bank[i], xv_, ALU.add).then_inc(S("dve_ffn"), 1)

            ffn(0)
            norm(2, ahn, "dve_ahn", 0, 32)
            for r in range(RT):
                scale_rows(ahn2, 1, 32, r, "dve_ahn")

            def rows_lo(parts, b0, n0):
                for i in range(4):
                    dve.wait_ge(S("act_aturned"), n0 + i + 1)
                    r, j = i // 2, i % 2
                    part = [parts[:, s_, 4 * j:4 * j + 4, r * P:(r + 1) * P] for s_ in range(2)]
                    low_part(part[1], bank[b0 + i].rearrange("p (q t) -> p q t", q=4), part[0], "dve_aturned")

            half_lo(0, 0)
            rows_lo(kparts, 0, 0)
            rows_lo(qparts, 4, 4)
            half_lo(0, 1)
            dve.wait_ge(s_qkg, 32)
            for w in range(2):
                for r in range(RT):
                    cosr = C("cos")[:, r * HD:(r + 1) * HD].rearrange("p (o d) -> p o d", o=1)
                    sinr = C("sin")[:, r * HD:(r + 1) * HD].rearrange("p (o d) -> p o d", o=1)
                    tt(rot[:, w, 0, r, :, :], qkg[:, w, :, :], cosr.broadcast_to([P, NG, HD]), ALU.mult)
                    for a, b in ((0, 32), (32, 0)):
                        m = tt(rot[:, w, 1, r, :, a:a + 32], qkg[:, w, :, b:b + 32],
                               sinr[:, :, a:a + 32].broadcast_to([P, NG, 32]), ALU.mult)
            m.then_inc(S("dve_rot"), 1)
            dve.wait_ge(S("dve_rot"), 1)

            def heads(p, b, follow=True):
                def mean_squares(w, r):
                    j = 2 * w + r
                    dve.wait_ge(S("act_asq"), p * 4 + (j + 1))
                    dve.tensor_reduce(asm[:, 16:22], asq.rearrange("p (g d) -> p g d", g=6), AX.X, ALU.add).then_inc(S("dve_ass"), 1)
                    dve.wait_ge(S("dve_ass"), p * 4 + (j + 1))
                    dve.tensor_scalar(asm[:, 24:30], asm[:, 16:22], 1.0 / HD, RMS_EPS, ALU.mult, ALU.add).then_inc(S("dve_av"), 1)

                def norm_rotate(w, r):
                    j = 2 * w + r
                    dve.wait_ge(S("pool_ars"), p * 4 + (j + 1))
                    rs = asm[:, 32:38].rearrange("p (g o) -> p g o", o=1).broadcast_to([P, 6, HD])
                    tt(akn.rearrange("p g h d -> p (g h) d"), akr[:, j, :].rearrange("p (g d) -> p g d", g=6),
                       rs, ALU.mult).then_inc(S("dve_kn"), 1)
                    dve.wait_ge(S("dve_kn"), p * 4 + (j + 1))
                    cosb = rot[:, w, 0, r, :, :].rearrange("p g (o d) -> p g o d", o=1).broadcast_to([P, NG, 2, HD])
                    q.mark(tt(am1[:, :, :, :], akn[:, :, :, :], cosb, ALU.mult))
                    for c, d in ((0, 32), (32, 0)):
                        sinb = rot[:, w, 1, r, :, c:c + 32].rearrange("p g (o d) -> p g o d", o=1).broadcast_to([P, NG, 2, 32])
                        m = tt(am2[:, :, :, c:c + 32], akn[:, :, :, d:d + 32], sinb, ALU.mult)
                    step(m)
                    tt(akr[:, j, :], am1.rearrange("p g h d -> p (g h d)"), am2.rearrange("p g h d -> p (g h d)"), ALU.add).then_inc(S("dve_kr"), 1)

                def mask_max(i):
                    r = i % 2
                    n = NG * (r + 1) * P
                    dve.wait_ge(S("pe_s"), b * 4 + (i + 1))
                    if i >= 2:
                        dve.wait_ge(S("pe_pT"), b * 4 + (i - 1))
                    dve.memset(asm[:, 48 + i:49 + i], 0.0)
                    src = bank[2][:, 0:n] if r == 0 else wide[:, 0:n]
                    dve.tensor_tensor_reduce(pr[:, r, 0:n], src, C(f"mask{r}"), 1.0, 3.0 * NEG, ALU.add, ALU.max,
                                             asm[:, i:i + 1]).then_inc(S("dve_sm"), 1)
                    dve.wait_ge(S("dve_sm"), b * 4 + (i + 1))
                    dve.tensor_scalar(asm[:, 4 + i:5 + i], asm[:, i:i + 1], -SCALE, None, ALU.mult).then_inc(S("dve_nm"), 1)

                X, B = p is not None, b is not None
                if B: mask_max(0)
                if X: half_lo(p, 2)
                if B: mask_max(1)
                if X: mean_squares(0, 0); norm_rotate(0, 0); mean_squares(0, 1); half_lo(p, 3); norm_rotate(0, 1)
                if B: mask_max(2); mask_max(3)
                if X: half_lo(p, 4); mean_squares(1, 0); norm_rotate(1, 0)
                if X: mean_squares(1, 1); half_lo(p, 5); norm_rotate(1, 1)
                if B:
                    dve.wait_ge(S("act_p"), b * 4 + 4)
                    dve.reciprocal(asm[:, 12:16], asm[:, 8:12]).then_inc(S("dve_rden"), 1)
                if X and follow: half_lo(p + 1, 0); half_lo(p + 1, 1)

            MARKS = 8
            marks = q.n
            heads(0, None)
            assert q.n - marks == MARKS, q.n - marks
            with dve.Fori(1, KT - 1) as p:
                q.start(p - 1, MARKS)
                heads(p, p - 1)
            q.end(KT - 2)
            heads(KT - 1, KT - 2, follow=False)
            heads(None, KT - 1)
            gu_lo(0, 0, NF)
            for i in range(4):
                dve.wait_ge(S("pe_awo"), i + 1)
                xv_ = x[:, i // 2, (i % 2) * 512:(i % 2 + 1) * 512]
                tt(xv_, bank[i], xv_, ALU.add).then_inc(S("dve_awo"), 1)
            ffn(1)

        @block.gpsimd
        def _(pool):
            pool.wait_ge(S("dve_mhalf"), 1)

            def root(dst, src, n):
                return pool.tensor_tensor(dst, src, mhalf[:, 0:n], ALU.pow)

            def norm_root(n):
                for r in range(RT):
                    pool.wait_ge(S("dve_ms"), n * RT + r + 1)
                    root(small[:, 4 + r:5 + r], small[:, 2 + r:3 + r], 1).then_inc(S("pool_rs"), 1)

            norm_root(0)
            with pool.Fori(0, NGRP) as it:
                for c in range(2):
                    pool.wait_ge(S("dve_var"), it * 2 + (c + 1))
                    root(gsm[:, 40 + 4 * c:44 + 4 * c], gsm[:, 32 + 4 * c:36 + 4 * c], 4).then_inc(S("pool_ors"), 1)
            norm_root(1)
            norm_root(2)
            with pool.Fori(0, KT) as p:
                for j in range(4):
                    pool.wait_ge(S("dve_av"), p * 4 + j + 1)
                    root(asm[:, 32:38], asm[:, 24:30], 6).then_inc(S("pool_ars"), 1)
            norm_root(3)


ROW_INPUTS = ["a_mu", "a_w0", "a_a0", "a_k_k", "a_k_a", "a_r_k", "a_lnx_g", "a_lnx_b"]
INS = ["x", "a_norm_g", "a_w_r", "a_w_k", "a_w_v", "a_w1", "a_w2", "a_a1", "a_a2", "a_g1", "a_g2", "a_w_o", "kv_norm_g", "w_kv", "k_norm_g",
       "b_norm_g", "b_w_q", "b_q_norm_g", "b_w_o", "f_norm_g", "f_w_gu", "f_w_down"]


def kernel(**inputs):
    import concourse.bacc as bacc
    from concourse.bass_utils import run_bass_kernel_spmd

    nc = bacc.Bacc("TRN2", target_bir_lowering=False, num_devices=1)
    arrays, args = {}, {}
    table = np.concatenate([CONSTS[n] for n in CAT], 1)
    rows = np.concatenate([np.asarray(inputs[n]).reshape(-1, D) for n in ROW_INPUTS], 0)
    for name in INS + ["const", "rows"]:
        a = {"const": table, "rows": rows}.get(name)
        if a is None:
            a = np.ascontiguousarray(inputs[name])
        arrays[f"in_{name}"] = a
        args[name] = nc.dram_tensor(f"in_{name}", a.shape, mybir.dt.from_np(a.dtype), kind="ExternalInput").ap()
    out = nc.dram_tensor("out", (1, T, D), F32, kind="ExternalOutput").ap()
    program(nc, args, out)
    r = run_bass_kernel_spmd(nc, [arrays], core_ids=[0])
    return r.results[0]["out"]
```
